# Optimizing a Trainium2 kernel written in Bass

```python
import math
import jax
import jax.numpy as jnp
from jax import lax
import numpy as np

D_MODEL = 1024
BATCH = 1
SEQ = 1024
DEPTH = 2

N_A_LAYERS = DEPTH // 2
N_B_LAYERS = DEPTH - N_A_LAYERS
SSM_WIDTH = D_MODEL
GROUP = 16
N_GROUPS = SSM_WIDTH // GROUP
STATE = 64
DT_MIN = 1e-3
DT_MAX = 1e-1
N_HEADS = 16
HEAD_DIM = D_MODEL // N_HEADS
ATTN_WIDTH = N_HEADS * HEAD_DIM
Q_BLOCK = 128
EPS = 1e-6


def _rms(x, g):
    xf = x.astype(jnp.float32)
    y = xf * lax.rsqrt(jnp.mean(xf * xf, axis=-1, keepdims=True) + EPS)
    return (y * g.astype(jnp.float32)).astype(x.dtype)

def _modulation(c, w, b, n):
    m = jax.nn.silu(c) @ w + b
    return jnp.split(m[:, None, :], n, axis=-1)

def _cplx_combine(e1, e2):
    a1r, a1i, b1r, b1i = e1
    a2r, a2i, b2r, b2i = e2
    ar = a1r * a2r - a1i * a2i
    ai = a1r * a2i + a1i * a2r
    br = a2r * b1r - a2i * b1i + b2r
    bi = a2r * b1i + a2i * b1r + b2i
    return (ar, ai, br, bi)

def _s5_mixer(h, w_in, log_dt, A_re, A_im, B_re, B_im, C_re, C_im, D, w_glu, b_glu, w_out):
    bsz, L, _ = h.shape
    u, z = jnp.split(h @ w_in, 2, axis=-1)
    f32 = jnp.float32
    dt = jnp.exp(log_dt.astype(f32))[:, None]
    ar, ai = A_re.astype(f32), A_im.astype(f32)
    mag = jnp.exp(ar * dt)
    abar_r, abar_i = mag * jnp.cos(ai * dt), mag * jnp.sin(ai * dt)
    den = ar * ar + ai * ai
    nr = abar_r - 1.0
    coef_r = (nr * ar + abar_i * ai) / den
    coef_i = (abar_i * ar - nr * ai) / den
    br, bi = B_re.astype(f32), B_im.astype(f32)
    bb_r = coef_r[..., None] * br - coef_i[..., None] * bi
    bb_i = coef_r[..., None] * bi + coef_i[..., None] * br
    ug = u.astype(f32).reshape(bsz, L, N_GROUPS, GROUP)
    bu_r = jnp.einsum('blgc,gpc->blgp', ug, bb_r)
    bu_i = jnp.einsum('blgc,gpc->blgp', ug, bb_i)
    a_r = jnp.broadcast_to(abar_r[None, None], (1, L, N_GROUPS, STATE))
    a_i = jnp.broadcast_to(abar_i[None, None], (1, L, N_GROUPS, STATE))
    _, _, s_r, s_i = lax.associative_scan(_cplx_combine, (a_r, a_i, bu_r, bu_i), axis=1)
    y = (jnp.einsum('blgp,gcp->blgc', s_r, C_re.astype(f32))
         - jnp.einsum('blgp,gcp->blgc', s_i, C_im.astype(f32)))
    y = y.reshape(bsz, L, SSM_WIDTH) + D.astype(f32) * u.astype(f32)
    y = jax.nn.gelu(y)
    y = y * jax.nn.sigmoid(y @ w_glu.astype(f32) + b_glu.astype(f32))
    y = y * jax.nn.silu(z.astype(f32))
    return y.astype(h.dtype) @ w_out

def _head_rms(t, g):
    tf = t.astype(jnp.float32)
    return tf * lax.rsqrt(jnp.mean(tf * tf, axis=-1, keepdims=True) + EPS) * g.astype(jnp.float32)

def _shared_kv(x, c, g, mod_w, mod_b, kv_w, f_bias, k_norm_g):
    bsz, L, _ = x.shape
    shift, scale = _modulation(c, mod_w, mod_b, 2)
    h = _rms(x, g) * (1.0 + scale) + shift
    kvf = h @ kv_w
    k = kvf[..., :ATTN_WIDTH].reshape(bsz, L, N_HEADS, HEAD_DIM)
    v = kvf[..., ATTN_WIDTH:2 * ATTN_WIDTH].reshape(bsz, L, N_HEADS, HEAD_DIM)
    f_logit = kvf[..., 2 * ATTN_WIDTH:].astype(jnp.float32) + f_bias.astype(jnp.float32)
    k = _head_rms(k, k_norm_g)
    F = jnp.cumsum(jax.nn.log_sigmoid(f_logit), axis=1)
    return k, v, F

def _fox_mixer(h, k, v, F, w_in, q_norm_g, w_out):
    bsz, L, _ = h.shape
    nblk = L // Q_BLOCK
    q, z = jnp.split(h @ w_in, 2, axis=-1)
    q = _head_rms(q.reshape(bsz, L, N_HEADS, HEAD_DIM), q_norm_g) * (HEAD_DIM ** -0.5)
    qb = q.reshape(bsz, nblk, Q_BLOCK, N_HEADS, HEAD_DIM).transpose(1, 0, 3, 2, 4)
    fq = F.reshape(bsz, nblk, Q_BLOCK, N_HEADS).transpose(1, 0, 3, 2)
    kt = k.transpose(0, 2, 1, 3)
    vt = v.astype(jnp.float32).transpose(0, 2, 1, 3)
    fk = F.transpose(0, 2, 1)
    kpos = jnp.arange(L)

    def one_block(args):
        qi, fqi, i = args
        s = jnp.einsum('bhqd,bhkd->bhqk', qi, kt)
        s = s + fqi[..., None] - fk[:, :, None, :]
        qpos = i * Q_BLOCK + jnp.arange(Q_BLOCK)
        s = jnp.where(kpos[None, :] <= qpos[:, None], s, -jnp.inf)
        p = jax.nn.softmax(s, axis=-1)
        return jnp.einsum('bhqk,bhkd->bhqd', p, vt)

    o = lax.map(one_block, (qb, fq, jnp.arange(nblk)))
    o = o.transpose(1, 0, 3, 2, 4).reshape(bsz, L, ATTN_WIDTH)
    o = o * jax.nn.silu(z.astype(jnp.float32))
    return o.astype(h.dtype) @ w_out

def first_inputs(seed: int = 0) -> dict:
    key = jax.random.key(seed)
    ks = iter(jax.random.split(key, 40))
    f32 = jnp.float32

    def nrm(shape, scale):
        return scale * jax.random.normal(next(ks), shape, f32)

    D, E, G, P, NA, NB = D_MODEL, SSM_WIDTH, N_GROUPS, STATE, N_A_LAYERS, N_B_LAYERS
    AW, H = ATTN_WIDTH, N_HEADS
    inp = {}
    inp['x'] = nrm((BATCH, SEQ, D), 1.0)
    inp['c'] = nrm((BATCH, D), 1.0)
    inp['a_norm_g'] = 1.0 + nrm((NA, D), 0.02)
    inp['a_mod_w'] = nrm((NA, D, 3 * D), 0.5 * D ** -0.5)
    inp['a_mod_b'] = nrm((NA, 3 * D), 0.02)
    inp['a_w_in'] = nrm((NA, D, 2 * E), D ** -0.5)
    inp['a_log_dt'] = jax.random.uniform(next(ks), (NA, G), f32, math.log(DT_MIN), math.log(DT_MAX))
    inp['a_A_re'] = -0.5 + nrm((NA, G, P), 0.01)
    inp['a_A_im'] = math.pi * jnp.broadcast_to(jnp.arange(P, dtype=f32), (NA, G, P)) + nrm((NA, G, P), 0.01)
    inp['a_B_re'] = nrm((NA, G, P, GROUP), (2 * GROUP) ** -0.5)
    inp['a_B_im'] = nrm((NA, G, P, GROUP), (2 * GROUP) ** -0.5)
    inp['a_C_re'] = nrm((NA, G, GROUP, P), 0.5)
    inp['a_C_im'] = nrm((NA, G, GROUP, P), 0.5)
    inp['a_D'] = nrm((NA, E), 1.0)
    inp['a_w_glu'] = nrm((NA, E, E), E ** -0.5)
    inp['a_b_glu'] = nrm((NA, E), 0.02)
    inp['a_w_out'] = nrm((NA, E, D), E ** -0.5)
    inp['kv_norm_g'] = 1.0 + nrm((D,), 0.02)
    inp['kv_mod_w'] = nrm((D, 2 * D), 0.5 * D ** -0.5)
    inp['kv_mod_b'] = nrm((2 * D,), 0.02)
    inp['kv_w'] = nrm((D, 2 * AW + H), D ** -0.5)
    inp['kv_f_bias'] = jax.random.uniform(next(ks), (H,), f32, 1.0, 4.0)
    inp['k_norm_g'] = 1.0 + nrm((HEAD_DIM,), 0.02)
    inp['b_norm_g'] = 1.0 + nrm((NB, D), 0.02)
    inp['b_mod_w'] = nrm((NB, D, 3 * D), 0.5 * D ** -0.5)
    inp['b_mod_b'] = nrm((NB, 3 * D), 0.02)
    inp['b_w_in'] = nrm((NB, D, 2 * AW), D ** -0.5)
    inp['q_norm_g'] = 1.0 + nrm((NB, HEAD_DIM), 0.02)
    inp['b_w_out'] = nrm((NB, AW, D), AW ** -0.5)
    return inp

def first_block(x, c, a_norm_g, a_mod_w, a_mod_b, a_w_in, a_log_dt, a_A_re, a_A_im,
              a_B_re, a_B_im, a_C_re, a_C_im, a_D, a_w_glu, a_b_glu, a_w_out,
              kv_norm_g, kv_mod_w, kv_mod_b, kv_w, kv_f_bias, k_norm_g,
              b_norm_g, b_mod_w, b_mod_b, b_w_in, q_norm_g, b_w_out):
    k = v = F = None
    for layer in range(DEPTH):
        if layer < N_A_LAYERS:
            i = layer
            shift, scale, gate = _modulation(c, a_mod_w[i], a_mod_b[i], 3)
            h = _rms(x, a_norm_g[i]) * (1.0 + scale) + shift
            y = _s5_mixer(h, a_w_in[i], a_log_dt[i], a_A_re[i], a_A_im[i], a_B_re[i], a_B_im[i],
                          a_C_re[i], a_C_im[i], a_D[i], a_w_glu[i], a_b_glu[i], a_w_out[i])
            x = x + gate * y
        else:
            if layer == N_A_LAYERS:
                k, v, F = _shared_kv(x, c, kv_norm_g, kv_mod_w, kv_mod_b, kv_w, kv_f_bias, k_norm_g)
            j = layer - N_A_LAYERS
            shift, scale, gate = _modulation(c, b_mod_w[j], b_mod_b[j], 3)
            h = _rms(x, b_norm_g[j]) * (1.0 + scale) + shift
            y = _fox_mixer(h, k, v, F, b_w_in[j], q_norm_g[j], b_w_out[j])
            x = x + gate * y
    return x


GRID_W = 64
CTX_LEN = 256
NORM_EPS = 1e-6
ROPE_BASE = 10000.0
NEG_INF = -1e30

A_HEADS = 8
A_KV_HEADS = 2
A_HEAD_DIM = 64
WINDOW = 128
A_BLOCK = 128
B_WIDTH = 512
B_GROUPS = 4
B_CHUNK = 128
C_HEADS = 8
C_Q_LORA = 384
C_KV_LORA = 256
C_NOPE = 64
C_ROPE = 32
C_V = 64
C_BLOCK = 128
D_WIDTH = 512
D_CONV = 3
N_EXPERTS = 16
EXPERT_FF = 1024
EC_FACTOR = 2

A_Q_W = A_HEADS * A_HEAD_DIM
A_KV_W = A_KV_HEADS * A_HEAD_DIM
EVEN_CTX_COLS = 2 * A_KV_W
EVEN_IN = EVEN_CTX_COLS + A_Q_W + 2 * B_WIDTH
EVEN_OUT = A_Q_W + B_WIDTH
ODD_CTX_COLS = C_KV_LORA + C_ROPE
ODD_IN = ODD_CTX_COLS + C_Q_LORA + 3 * D_WIDTH
ODD_OUT = C_HEADS * C_V + D_WIDTH
N_EVEN = (DEPTH + 1) // 2
N_ODD = DEPTH // 2


def rms_norm(x, g):
    xf = x.astype(jnp.float32)
    y = xf * lax.rsqrt(jnp.mean(xf * xf, axis=-1, keepdims=True) + NORM_EPS)
    return (y * g.astype(jnp.float32)).astype(x.dtype)

def layer_norm(x, g):
    xf = x.astype(jnp.float32)
    mu = jnp.mean(xf, axis=-1, keepdims=True)
    var = jnp.mean(jnp.square(xf - mu), axis=-1, keepdims=True)
    return ((xf - mu) * lax.rsqrt(var + NORM_EPS) * g.astype(jnp.float32)).astype(x.dtype)

def axial_rope_tables(rows, rot_dim):
    row = jnp.repeat(jnp.arange(rows, dtype=jnp.float32), GRID_W)
    col = jnp.tile(jnp.arange(GRID_W, dtype=jnp.float32), rows)
    n_freq = rot_dim // 4
    inv_freq = ROPE_BASE ** (-jnp.arange(n_freq, dtype=jnp.float32) / n_freq)
    ang = jnp.concatenate([row[:, None] * inv_freq[None, :], col[:, None] * inv_freq[None, :]], axis=-1)
    return jnp.cos(ang), jnp.sin(ang)

def apply_rope(x, cos, sin):
    x1, x2 = jnp.split(x, 2, axis=-1)
    cs = cos[None, :, None, :].astype(x.dtype)
    sn = sin[None, :, None, :].astype(x.dtype)
    return jnp.concatenate([x1 * cs - x2 * sn, x2 * cs + x1 * sn], axis=-1)

def gqa_attend(q, k, v, mask, sink, scale):
    s = jnp.einsum('bqhgd,bkhd->bhgqk', q, k).astype(jnp.float32) * scale
    if mask is not None:
        s = jnp.where(mask, s, NEG_INF)
    if sink is not None:
        sk = jnp.broadcast_to(sink.astype(jnp.float32)[None, :, :, None, None], s.shape[:-1] + (1,))
        s = jnp.concatenate([s, sk], axis=-1)
    p = jax.nn.softmax(s, axis=-1)
    if sink is not None:
        p = p[..., :-1]
    return jnp.einsum('bhgqk,bkhd->bqhgd', p.astype(v.dtype), v)

def window_attention(q, k, v, k_ctx, v_ctx, sink_g, scale):
    bsz, n = q.shape[0], q.shape[1]
    g = A_HEADS // A_KV_HEADS
    nb = n // A_BLOCK
    span = A_BLOCK + 2 * WINDOW
    pad = ((0, 0), (WINDOW, WINDOW), (0, 0), (0, 0))
    kp = jnp.pad(k, pad)
    vp = jnp.pad(v, pad)
    qi = jnp.arange(A_BLOCK)
    kj = jnp.arange(span)
    band = jnp.abs(kj[None, :] - WINDOW - qi[:, None]) <= WINDOW
    ctx_ok = jnp.ones((A_BLOCK, k_ctx.shape[1]), dtype=jnp.bool_)

    def block(nidx):
        start = nidx * A_BLOCK
        qb = lax.dynamic_slice_in_dim(q, start, A_BLOCK, axis=1).reshape(bsz, A_BLOCK, A_KV_HEADS, g, A_HEAD_DIM)
        kb = lax.dynamic_slice_in_dim(kp, start, span, axis=1)
        vb = lax.dynamic_slice_in_dim(vp, start, span, axis=1)
        kpos = start - WINDOW + kj
        mask = band & ((kpos >= 0) & (kpos < n))[None, :]
        mask = jnp.concatenate([mask, ctx_ok], axis=1)
        o = gqa_attend(qb, jnp.concatenate([kb, k_ctx], axis=1), jnp.concatenate([vb, v_ctx], axis=1), mask, sink_g, scale)
        return o.reshape(bsz, A_BLOCK, A_Q_W)

    out = lax.map(block, jnp.arange(nb))
    return jnp.moveaxis(out, 0, 1).reshape(bsz, n, A_Q_W)

def dense_block_attention(q, k_all, v_all, scale):
    bsz, n, h, _ = q.shape
    dv = v_all.shape[-1]
    nb = n // C_BLOCK

    def block(nidx):
        qb = lax.dynamic_slice_in_dim(q, nidx * C_BLOCK, C_BLOCK, axis=1)
        return gqa_attend(qb[:, :, :, None], k_all, v_all, None, None, scale)[:, :, :, 0]

    out = lax.map(block, jnp.arange(nb))
    return jnp.moveaxis(out, 0, 1).reshape(bsz, n, h * dv)

def spatial_gating(z, norm_g, w_s, b_s):
    bsz, n, _ = z.shape
    u, v = jnp.split(jax.nn.gelu(z), 2, axis=-1)
    v = layer_norm(v, norm_g)
    vc = v.reshape(bsz, n // B_CHUNK, B_CHUNK, B_GROUPS, B_WIDTH // B_GROUPS)
    mixed = jnp.einsum('gpq,bcqgd->bcpgd', w_s, vc) + b_s.T[None, None, :, :, None]
    return u * mixed.reshape(bsz, n, B_WIDTH)

def gated_short_conv(z, conv_w):
    gb, gc, hh = jnp.split(z, 3, axis=-1)
    u = gc * hh
    n = u.shape[1]
    half = D_CONV // 2
    up = jnp.pad(u, ((0, 0), (half, half), (0, 0)))
    conv = sum(up[:, j:j + n] * conv_w[j] for j in range(D_CONV))
    return gb * conv

def mla_q(cq, q_norm_g, w_uq, cos, sin):
    bsz, n, _ = cq.shape
    q = (rms_norm(cq, q_norm_g) @ w_uq).reshape(bsz, n, C_HEADS, C_NOPE + C_ROPE)
    q_nope, q_rope = q[..., :C_NOPE], q[..., C_NOPE:]
    if cos is not None:
        q_rope = apply_rope(q_rope, cos, sin)
    return jnp.concatenate([q_nope, q_rope], axis=-1)

def mla_kv(ckv, kr, kv_norm_g, w_ukv, cos, sin):
    bsz, n, _ = ckv.shape
    kv = (rms_norm(ckv, kv_norm_g) @ w_ukv).reshape(bsz, n, C_HEADS, C_NOPE + C_V)
    k_nope, v = kv[..., :C_NOPE], kv[..., C_NOPE:]
    kr = kr[:, :, None, :]
    if cos is not None:
        kr = apply_rope(kr, cos, sin)
    k = jnp.concatenate([k_nope, jnp.broadcast_to(kr, (bsz, n, C_HEADS, C_ROPE))], axis=-1)
    return k, v

def even_mixer(h_lat, h_ctx, w_in, sink, sgu_norm_g, sgu_w, sgu_b, w_out, cos, sin, need_ctx):
    bsz, n_lat, _ = h_lat.shape
    n_ctx = h_ctx.shape[1]
    g = A_HEADS // A_KV_HEADS
    scale = A_HEAD_DIM ** -0.5
    sink_g = sink.reshape(A_KV_HEADS, g)
    z_lat = h_lat @ w_in
    z_ctx = h_ctx @ (w_in if need_ctx else w_in[:, :EVEN_CTX_COLS])
    k_ctx = z_ctx[..., :A_KV_W].reshape(bsz, n_ctx, A_KV_HEADS, A_HEAD_DIM)
    v_ctx = z_ctx[..., A_KV_W:EVEN_CTX_COLS].reshape(bsz, n_ctx, A_KV_HEADS, A_HEAD_DIM)
    k_lat = apply_rope(z_lat[..., :A_KV_W].reshape(bsz, n_lat, A_KV_HEADS, A_HEAD_DIM), cos, sin)
    v_lat = z_lat[..., A_KV_W:EVEN_CTX_COLS].reshape(bsz, n_lat, A_KV_HEADS, A_HEAD_DIM)
    q_lat = apply_rope(z_lat[..., EVEN_CTX_COLS:EVEN_CTX_COLS + A_Q_W].reshape(bsz, n_lat, A_HEADS, A_HEAD_DIM), cos, sin)
    o_lat = window_attention(q_lat, k_lat, v_lat, k_ctx, v_ctx, sink_g, scale)
    s_lat = spatial_gating(z_lat[..., EVEN_CTX_COLS + A_Q_W:], sgu_norm_g, sgu_w, sgu_b)
    y_lat = jnp.concatenate([o_lat, s_lat], axis=-1) @ w_out
    if not need_ctx:
        return y_lat, None
    q_ctx = z_ctx[..., EVEN_CTX_COLS:EVEN_CTX_COLS + A_Q_W].reshape(bsz, n_ctx, A_KV_HEADS, g, A_HEAD_DIM)
    o_ctx = gqa_attend(q_ctx, k_ctx, v_ctx, None, sink_g, scale).reshape(bsz, n_ctx, A_Q_W)
    s_ctx = spatial_gating(z_ctx[..., EVEN_CTX_COLS + A_Q_W:], sgu_norm_g, sgu_w, sgu_b)
    y_ctx = jnp.concatenate([o_ctx, s_ctx], axis=-1) @ w_out
    return y_lat, y_ctx

def odd_mixer(h_lat, h_ctx, w_in, q_norm_g, w_uq, kv_norm_g, w_ukv, conv_w, w_out, cos, sin, need_ctx):
    bsz, n_ctx = h_ctx.shape[0], h_ctx.shape[1]
    scale = (C_NOPE + C_ROPE) ** -0.5
    z_lat = h_lat @ w_in
    z_ctx = h_ctx @ (w_in if need_ctx else w_in[:, :ODD_CTX_COLS])
    k_ctx, v_ctx = mla_kv(z_ctx[..., :C_KV_LORA], z_ctx[..., C_KV_LORA:ODD_CTX_COLS], kv_norm_g, w_ukv, None, None)
    k_lat, v_lat = mla_kv(z_lat[..., :C_KV_LORA], z_lat[..., C_KV_LORA:ODD_CTX_COLS], kv_norm_g, w_ukv, cos, sin)
    q_lat = mla_q(z_lat[..., ODD_CTX_COLS:ODD_CTX_COLS + C_Q_LORA], q_norm_g, w_uq, cos, sin)
    k_all = jnp.concatenate([k_lat, k_ctx], axis=1)
    v_all = jnp.concatenate([v_lat, v_ctx], axis=1)
    o_lat = dense_block_attention(q_lat, k_all, v_all, scale)
    c_lat = gated_short_conv(z_lat[..., ODD_CTX_COLS + C_Q_LORA:], conv_w)
    y_lat = jnp.concatenate([o_lat, c_lat], axis=-1) @ w_out
    if not need_ctx:
        return y_lat, None
    q_ctx = mla_q(z_ctx[..., ODD_CTX_COLS:ODD_CTX_COLS + C_Q_LORA], q_norm_g, w_uq, None, None)
    o_ctx = gqa_attend(q_ctx[:, :, :, None], k_ctx, v_ctx, None, None, scale)[:, :, :, 0].reshape(bsz, n_ctx, C_HEADS * C_V)
    c_ctx_out = gated_short_conv(z_ctx[..., ODD_CTX_COLS + C_Q_LORA:], conv_w)
    y_ctx = jnp.concatenate([o_ctx, c_ctx_out], axis=-1) @ w_out
    return y_lat, y_ctx

def expert_choice_ffn(h, w_router, w1, w3, w2):
    n_tok, d = h.shape[1], h.shape[2]
    cap = EC_FACTOR * n_tok // N_EXPERTS
    aff = jax.nn.softmax(jnp.einsum('bnd,de->bne', h, w_router).astype(jnp.float32), axis=-1)
    gate, idx = lax.top_k(jnp.swapaxes(aff, 1, 2), cap)
    xs = jax.vmap(lambda hb, ib: hb[ib])(h, idx)
    a = jnp.einsum('becd,edf->becf', xs, w1)
    b = jnp.einsum('becd,edf->becf', xs, w3)
    y = jnp.einsum('becf,efd->becd', jax.nn.silu(a) * b, w2) * gate[..., None].astype(h.dtype)

    def combine(yb, ib):
        return jnp.zeros((n_tok, d), h.dtype).at[ib.reshape(-1)].add(yb.reshape(-1, d))

    return jax.vmap(combine)(y, idx)

def second_inputs(seed: int = 0) -> dict:
    key = jax.random.key(seed)
    ks = iter(jax.random.split(key, 32))
    D = D_MODEL

    def nrm(shape, scale):
        return jax.random.normal(next(ks), shape, jnp.float32) * scale

    return {
        'x': nrm((BATCH, SEQ, D), 1.0),
        'c': nrm((BATCH, D), 1.0),
        'ctx': nrm((BATCH, CTX_LEN, D), 1.0),
        'c_ctx': nrm((D,), 1.0),
        'mod_w': nrm((DEPTH, D, 6 * D), 0.5 * D ** -0.5),
        'mod_b': nrm((DEPTH, 6 * D), 0.01),
        'norm1_g': 1.0 + nrm((DEPTH, D), 0.05),
        'norm2_g': 1.0 + nrm((DEPTH, D), 0.05),
        'ev_w_in': nrm((N_EVEN, D, EVEN_IN), D ** -0.5),
        'ev_sink': nrm((N_EVEN, A_HEADS), 0.5),
        'ev_sgu_norm_g': 1.0 + nrm((N_EVEN, B_WIDTH), 0.05),
        'ev_sgu_w': nrm((N_EVEN, B_GROUPS, B_CHUNK, B_CHUNK), B_CHUNK ** -0.5),
        'ev_sgu_b': nrm((N_EVEN, B_GROUPS, B_CHUNK), 0.1),
        'ev_w_out': nrm((N_EVEN, EVEN_OUT, D), EVEN_OUT ** -0.5),
        'od_w_in': nrm((N_ODD, D, ODD_IN), D ** -0.5),
        'od_q_norm_g': 1.0 + nrm((N_ODD, C_Q_LORA), 0.05),
        'od_w_uq': nrm((N_ODD, C_Q_LORA, C_HEADS * (C_NOPE + C_ROPE)), C_Q_LORA ** -0.5),
        'od_kv_norm_g': 1.0 + nrm((N_ODD, C_KV_LORA), 0.05),
        'od_w_ukv': nrm((N_ODD, C_KV_LORA, C_HEADS * (C_NOPE + C_V)), C_KV_LORA ** -0.5),
        'od_conv_w': nrm((N_ODD, D_CONV, D_WIDTH), D_CONV ** -0.5),
        'od_w_out': nrm((N_ODD, ODD_OUT, D), ODD_OUT ** -0.5),
        'router_w': nrm((DEPTH, D, N_EXPERTS), D ** -0.5),
        'exp_w1': nrm((DEPTH, N_EXPERTS, D, EXPERT_FF), D ** -0.5),
        'exp_w3': nrm((DEPTH, N_EXPERTS, D, EXPERT_FF), D ** -0.5),
        'exp_w2': nrm((DEPTH, N_EXPERTS, EXPERT_FF, D), EXPERT_FF ** -0.5),
        'final_g': 1.0 + nrm((D,), 0.05),
    }

def second_block(x, c, ctx, c_ctx, mod_w, mod_b, norm1_g, norm2_g, ev_w_in, ev_sink, ev_sgu_norm_g, ev_sgu_w, ev_sgu_b, ev_w_out, od_w_in, od_q_norm_g, od_w_uq, od_kv_norm_g, od_w_ukv, od_conv_w, od_w_out, router_w, exp_w1, exp_w3, exp_w2, final_g):
    rows = x.shape[1] // GRID_W
    cos_a, sin_a = axial_rope_tables(rows, A_HEAD_DIM)
    cos_c, sin_c = axial_rope_tables(rows, C_ROPE)
    silu_c = jax.nn.silu(c)
    silu_cc = jax.nn.silu(c_ctx)[None, :]
    x_lat, x_ctx = x, ctx
    for layer in range(DEPTH):
        need_ctx = layer < DEPTH - 1
        m_lat = jnp.split((silu_c @ mod_w[layer] + mod_b[layer])[:, None, :], 6, axis=-1)
        m_ctx = jnp.split((silu_cc @ mod_w[layer] + mod_b[layer])[:, None, :], 6, axis=-1)
        h_lat = rms_norm(x_lat, norm1_g[layer]) * (1 + m_lat[1]) + m_lat[0]
        h_ctx = rms_norm(x_ctx, norm1_g[layer]) * (1 + m_ctx[1]) + m_ctx[0]
        i = layer // 2
        if layer % 2 == 0:
            y_lat, y_ctx = even_mixer(h_lat, h_ctx, ev_w_in[i], ev_sink[i], ev_sgu_norm_g[i], ev_sgu_w[i], ev_sgu_b[i], ev_w_out[i], cos_a, sin_a, need_ctx)
        else:
            y_lat, y_ctx = odd_mixer(h_lat, h_ctx, od_w_in[i], od_q_norm_g[i], od_w_uq[i], od_kv_norm_g[i], od_w_ukv[i], od_conv_w[i], od_w_out[i], cos_c, sin_c, need_ctx)
        x_lat = x_lat + m_lat[2] * y_lat
        h_lat = rms_norm(x_lat, norm2_g[layer]) * (1 + m_lat[4]) + m_lat[3]
        x_lat = x_lat + m_lat[5] * expert_choice_ffn(h_lat, router_w[layer], exp_w1[layer], exp_w3[layer], exp_w2[layer])
        if need_ctx:
            x_ctx = x_ctx + m_ctx[2] * y_ctx
            h_ctx = rms_norm(x_ctx, norm2_g[layer]) * (1 + m_ctx[4]) + m_ctx[3]
            x_ctx = x_ctx + m_ctx[5] * expert_choice_ffn(h_ctx, router_w[layer], exp_w1[layer], exp_w3[layer], exp_w2[layer])
    return rms_norm(x_lat, final_g)


def setup_inputs(seed=0):
    out = dict(first_inputs(seed))
    for name, value in second_inputs(seed + 1).items():
        if name != "x":
            out[name + "_2"] = value
    return out


def reference(
    x, c, a_norm_g, a_mod_w, a_mod_b, a_w_in, a_log_dt, a_A_re, a_A_im, a_B_re, a_B_im, a_C_re,
    a_C_im, a_D, a_w_glu, a_b_glu, a_w_out, kv_norm_g, kv_mod_w, kv_mod_b, kv_w, kv_f_bias,
    k_norm_g, b_norm_g, b_mod_w, b_mod_b, b_w_in, q_norm_g, b_w_out, c_2, ctx_2, c_ctx_2,
    mod_w_2, mod_b_2, norm1_g_2, norm2_g_2, ev_w_in_2, ev_sink_2, ev_sgu_norm_g_2, ev_sgu_w_2,
    ev_sgu_b_2, ev_w_out_2, od_w_in_2, od_q_norm_g_2, od_w_uq_2, od_kv_norm_g_2, od_w_ukv_2,
    od_conv_w_2, od_w_out_2, router_w_2, exp_w1_2, exp_w3_2, exp_w2_2, final_g_2,
):
    x = first_block(
        x, c, a_norm_g, a_mod_w, a_mod_b, a_w_in, a_log_dt, a_A_re, a_A_im, a_B_re, a_B_im,
        a_C_re, a_C_im, a_D, a_w_glu, a_b_glu, a_w_out, kv_norm_g, kv_mod_w, kv_mod_b, kv_w,
        kv_f_bias, k_norm_g, b_norm_g, b_mod_w, b_mod_b, b_w_in, q_norm_g, b_w_out,
    )
    return second_block(
        x, c_2, ctx_2, c_ctx_2, mod_w_2, mod_b_2, norm1_g_2, norm2_g_2, ev_w_in_2, ev_sink_2,
        ev_sgu_norm_g_2, ev_sgu_w_2, ev_sgu_b_2, ev_w_out_2, od_w_in_2, od_q_norm_g_2,
        od_w_uq_2, od_kv_norm_g_2, od_w_ukv_2, od_conv_w_2, od_w_out_2, router_w_2, exp_w1_2,
        exp_w3_2, exp_w2_2, final_g_2,
    )


_drawn_inputs = setup_inputs


def setup_inputs(seed=0):
    import zlib

    import numpy as np

    out = dict(_drawn_inputs(seed))
    spreads = {}
    factors = {'a_norm_g': 8.0,
     'a_mod_b': 6.313,
     'a_A_re': 8.0,
     'a_b_glu': 8.0,
     'kv_norm_g': 8.0,
     'kv_mod_b': 8.0,
     'k_norm_g': 8.0,
     'b_norm_g': 8.0,
     'b_mod_b': 5.692,
     'q_norm_g': 8.0,
     'ctx_2': 3.312,
     'mod_b_2': 3.663,
     'norm2_g_2': 3.68,
     'ev_sink_2': 64.0,
     'ev_sgu_norm_g_2': 22.418,
     'ev_sgu_b_2': 11.843,
     'od_q_norm_g_2': 8.0,
     'od_w_uq_2': 3.658,
     'od_kv_norm_g_2': 8.0,
     'od_conv_w_2': 3.23}
    for name, (base, spread) in spreads.items():
        noise = np.random.default_rng([zlib.crc32(name.encode()), seed]).standard_normal(out[name].shape)
        drawn = base * np.exp(spread * noise) if base else spread * noise
        out[name] = jnp.asarray(drawn.astype(out[name].dtype))
    for name, factor in factors.items():
        out[name] = (out[name] * factor).astype(out[name].dtype)
    return out
```

```python
import math
import numpy as np
import concourse.bass as bass
from concourse import mybir
from contextlib import ExitStack

F32 = mybir.dt.float32
U32 = mybir.dt.uint32
I32 = mybir.dt.int32
ACT = mybir.ActivationFunctionType
ALU = mybir.AluOpType
AXX = mybir.AxisListType.X

P = 128
D = 1024
SEQ = 1024
KT = D // P
NT = SEQ // P
CTX = 256
NTC = NT + CTX // P
NTOK = SEQ + CTX
EPS = 1e-6
NEG = -1e30
GROUPS, STATE, GRP = 64, 64, 16
T_CH = 8
NCH = SEQ // T_CH
NPAIR = GROUPS // 2
HD = 64
HB = 16
HW_ = 8
HC = 8
QKC = 96
NE = 16
CAP = 2 * SEQ // NE
CAPC = 2 * CTX // NE
RING = 3
TILE = KT * 512
N_MOD = 40
W_MOD = 0
W_AIN = W_MOD + N_MOD
W_GLU = W_AIN + 4
W_AOUT = W_GLU + 2
W_KV = W_AOUT + 2
W_BIN = W_KV + 4
W_BOUT = W_BIN + 4
W_EIN = W_BOUT + 2
W_EOUT = W_EIN + 4
W_MOE0 = W_EOUT + 2
W_OIN = W_MOE0 + 6 * NE
W_UQ = W_OIN + 5
W_UKV = W_UQ + 1
W_OOUT = W_UKV + 1
W_MOE1 = W_OOUT + 2
N_TILES = W_MOE1 + 6 * NE
MC_A, MC_KV, MC_B, MC_L = 0, 24, 40, 64
V_C, V_LAT, V_CTX = 0, 1, 2
C_ID, C_ONE, C_TRI, C_CAUSAL, C_PREV = range(5)
GS_A, GS_KV, GS_B, GS_1L0, GS_1C0, GS_2L0, GS_2C0, GS_1L1, GS_1C1, GS_2L1 = range(10)


class Link:

    def __init__(self, eng, sem):
        self.eng, self.sem, self.n = eng, sem, 0

    def __call__(self, ins):
        self.n = self.n + 1
        ins.then_inc(self.sem, 1)
        self.eng.wait_ge(self.sem, self.n)


class Core:

    def __init__(self, nc, ctx, io):
        self.nc, self.io = nc, io

        def sb(name, shape, dt=F32):
            return ctx.enter_context(nc.sbuf_tensor(name, shape, dt))

        self.ring = sb("w_ring", [P, RING, TILE])
        self.arena = sb("arena", [P, 38400])
        self.consts = sb("consts", [P, 5, P])
        self.modcol = sb("modcol", [P, 160, 3])
        self.gs = sb("gs", [P, 10, KT])
        self.gains = sb("gains", [P, 7, KT])
        self.cols = sb("cols", [P, 40])
        self.small = sb("small", [P, 900])
        self.psum = ctx.enter_context(nc.psum_tensor("psum", [P, 8, 512], F32))
        self.bank = [self.psum[:, i, :] for i in range(8)]
        self.loaded = [ctx.enter_context(nc.semaphore(f"w_loaded{i}")) for i in range(RING)]
        self.ctx = ctx
        self.scratch = {}
        self.of_block = []

    def score_view(self, n, nb):
        return self.psum[:, n * nb:(n + 1) * nb, :].rearrange("p b c -> p (b c)")

    def dram(self, name, shape):
        if name not in self.scratch:
            self.scratch[name] = self.nc.dram_tensor(name, shape, F32).ap()
        return self.scratch[name]

    def at(self, off, *shape):
        n = int(np.prod(shape))
        assert off + n <= 38400, (off, shape)
        v = self.arena[:, off:off + n]
        if len(shape) == 1:
            return v
        names = [f"a{i}" for i in range(len(shape))]
        return v.rearrange(f"p ({' '.join(names)}) -> p {' '.join(names)}",
                           **{a: s for a, s in zip(names[1:], shape[1:])})

    def const(self, i):
        return self.consts[:, i, :]

    def sems(self, prefix, names):
        new = [self.nc.alloc_semaphore(f"{prefix}_{n}") for n in names.split()]
        self.of_block += new
        return new

    def end_block(self):
        self.nc.clear_and_free_semaphores(self.of_block)
        self.nc.all_engine_barrier(sem_only=True)
        self.of_block = []

    def load_w(self, sp, n):
        if n < N_TILES:
            sp.dma_start(self.ring[:, n % RING, :], self.io["wstream"][n]).then_inc(self.loaded[n % RING], 16)

    def wait_w(self, pe, n):
        pe.wait_ge(self.loaded[n % RING], 16 * (n // RING + 1))

    def w(self, n, kt=KT):
        v = self.ring[:, n % RING, :]
        return v.rearrange("p (k n) -> p k n", k=kt)

    def shift(self, col, variant):
        return lambda k: self.modcol[:, col + k, variant:variant + 1]

    def gain(self, g):
        return lambda k: self.gs[:, g, k:k + 1]


A_V, A_S, A_U, A_Y, A_M = 0, 9216, 17472, 26624, 34816
SCOL = NCH + 1
S_A8R, S_A8I, S_NA8I, S_T1, S_T2 = 0, 32, 64, 96, 160


def block_mods_and_tables(cr, upto=99):
    nc, io = cr.nc, cr.io
    s_c, s_cs, s_row, s_tr, s_used, s_dve, s_in, s_e, s_ed, s_v, s_g, s_kmm, s_kst, s_kd0, s_kd1, s_gt, s_gte, s_z, s_zd, s_mc = cr.sems(
        "mod", "c_loaded silu_done row_copied transposed tile_used dve in_loaded act dve_for_act v_done g_done k_mm k_staged k_stored0 k_stored1 g_transposed g_copied zeros zeros_stored modcol")
    craw = cr.small[:, 300:324].rearrange("p (k v) -> p k v", v=3)
    cs = cr.small[:, 324:348].rearrange("p (k v) -> p k v", v=3)
    mrow = cr.at(A_M, 3, 512)
    modb = cr.small[:, 348:508]
    V = [cr.at(A_V + r * 4608, NPAIR, 9, GRP) for r in range(2)]
    G = cr.at(A_S, NPAIR, 2, T_CH, GRP)
    WT = cr.at(A_Y, NPAIR, 2, P)
    tmp9 = cr.at(A_U, NPAIR, 9, GRP)
    o = A_U + 4608
    tabs = cr.at(o, 6, NPAIR, GRP)
    c_r, c_i, b_r, b_i, bb_r, bb_i = [tabs[:, i] for i in range(6)]
    Dd = cr.at(o + 3072, GROUPS, GRP)
    vec = cr.at(A_M + 1536, 16, NPAIR)
    kst = cr.at(A_M + 1536 + 512, 2, 4, P)
    pw = cr.small[:, 508:508 + 288].rearrange("p (j t) -> p j t", t=9)
    pwi_ = cr.at(o + 4096, NPAIR, 9)
    dcol = cr.small[:, 796:796 + GROUPS]
    are, aim, ldt, dt, th, mag, kk, r_, sn, cn, den, nr, cfr, cfi, q1, q2 = [vec[:, i] for i in range(16)]
    psM = cr.bank[3]
    s_kd = (s_kd0, s_kd1)
    N_IN = 12

    with nc.Block() as block:
        @block.sync
        def _(sp):
            for n in range(RING):
                cr.load_w(sp, n)
            with sp.Fori(1, N_MOD // RING) as i:
                for s in range(RING):
                    sp.wait_ge(s_used, RING * i + s - 2)
                    sp.dma_start(cr.ring[:, s, :], io["wstream"][bass.ds(RING * i + s, 1)].rearrange(
                        "a p n -> (a p) n")).then_inc(cr.loaded[s], 16)
            for n in range(N_MOD // RING * RING, N_MOD + RING):
                sp.wait_ge(s_used, n - 2)
                cr.load_w(sp, n)
            Kd = cr.dram("k_lags", [GRP, GROUPS, 2 * P])
            for b in range(16):
                sp.wait_ge(s_kst, b + 1)
                g0 = b // 2 * 8 + b % 2
                sp.dma_start(Kd[:, g0:g0 + 7:2, P:2 * P], kst[0:GRP, b % 2]).then_inc(s_kd[b % 2], 16)
            sp.wait_ge(s_kd[0], 16 * 8)
            sp.wait_ge(s_kd[1], 16 * 8)

        @block.gpsimd
        def _(pool):
            Kd = cr.dram("k_lags", [GRP, GROUPS, 2 * P])
            z = cr.at(A_M, 3, 512)[0:GRP, 2, :]
            pool.dma_start(Kd[:, :, 0:P], io["zeros"][:, :, :]).then_inc(s_zd, 16)
            pool.wait_ge(s_zd, 16)

        @block.tensor
        def _(pe):
            pe.wait_ge(s_cs, 1)

            def matvec(n, s, first):
                pe.wait_ge(cr.loaded[s], 16 * first + 16)
                if not (isinstance(n, int) and n < 3):
                    pe.wait_ge(s_row, n - 2)
                for k in range(KT):
                    last = nc.tensor.matmul(cr.bank[s][0:3, :], cs[:, k, :], cr.w(s)[:, k, :],
                                            start=(k == 0), stop=(k == KT - 1))
                last.then_inc(s_used, 1)

            def to_columns(n, s):
                pe.wait_ge(s_row, n + 1)
                for j in range(4):
                    last = nc.tensor.matmul(psM[:, bass.ds(12 * n + 3 * j, 3)], mrow[0:3, s, j * P:(j + 1) * P],
                                            cr.const(C_ID)[0:3, 0:3], start=True, stop=True)
                last.then_inc(s_tr, 1)

            for n in range(RING):
                matvec(n, n, 0)
                if n:
                    to_columns(n - 1, n - 1)
            with pe.Fori(1, N_MOD // RING) as i:
                for s in range(RING):
                    matvec(RING * i + s, s, i)
                    to_columns(RING * i + s - 1, (s - 1) % RING)
            n = N_MOD - 1
            matvec(n, n % RING, n // RING)
            to_columns(n - 1, (n - 1) % RING)
            to_columns(n, n % RING)
            pe.wait_ge(s_row, N_MOD)
            pe.wait_ge(s_v, 1)
            pe.wait_ge(s_g, 1)
            for g in range(GROUPS):
                j, h = g // 2, (g % 2) * 64
                b, q = g // 8, j % 4
                if g % 8 == 0 and b >= 2:
                    pe.wait_ge(s_kst, 2 * (b - 1))
                dst = cr.bank[4 + b % 2 * 2 + g % 2][0:GRP, q * P:(q + 1) * P]
                for r, bb in enumerate((bb_r, bb_i)):
                    last = nc.tensor.matmul(dst, bb[h:h + 64, j, :],
                                            V[r][h:h + 64, j, 0:8, :].rearrange("p t c -> p (t c)"),
                                            start=(r == 0), stop=(r == 1))
                if q == 3:
                    last.then_inc(s_kmm, 1)
            for j in range(NPAIR):
                if j >= 2:
                    pe.wait_ge(s_gte, j - 1)
                for r in range(2):
                    last = nc.tensor.transpose(cr.bank[j % 2][:, r * P:(r + 1) * P],
                                               G[:, j, r].rearrange("p t c -> p (t c)"), cr.const(C_ID))
                last.then_inc(s_gt, 1)

        @block.scalar
        def _(act):
            act.dma_start(craw, io["ccols"]).then_inc(s_c, 16)
            for dst, src in ((cr.consts[:, :, :], "consts"), (cr.gains[:, :, :], "gains"), (cr.cols[:, :], "cols"), (modb, "modb"),
                             (are, "a_re"), (aim, "a_im"), (ldt, "a_ldt"), (c_r, "c_re"), (c_i, "c_im"),
                             (b_r, "b_re"), (b_i, "b_im")):
                act.dma_start(dst, io[src]).then_inc(s_in, 16)
            act.dma_start(dcol[0:GRP, :], io["d_cols"]).then_inc(s_in, 16)
            act.wait_ge(s_c, 16)
            nc.scalar.activation(cs, craw, ACT.Silu).then_inc(s_e, 1)
            act.wait_ge(s_in, 16 * N_IN)
            act.wait_ge(s_e, 1)
            nc.scalar.activation(craw, cs, ACT.Copy).then_inc(s_cs, 1)
            nc.scalar.activation(dt, ldt, ACT.Exp).then_inc(s_e, 1)
            act.wait_ge(s_ed, 1)
            nc.scalar.activation(mag, q1, ACT.Exp).then_inc(s_e, 1)
            act.wait_ge(s_ed, 2)
            nc.scalar.activation(sn, r_, ACT.Sin).then_inc(s_e, 1)
            nc.scalar.activation(cn, q2, ACT.Sin).then_inc(s_e, 1)

            def row(n, s):
                act.wait_ge(s_used, n + 1)
                if not (isinstance(n, int) and n < 3):
                    act.wait_ge(s_tr, n - 2)
                nc.scalar.activation(mrow[0:3, s, :], cr.bank[s][0:3, :], ACT.Copy).then_inc(s_row, 1)

            for n in range(RING):
                row(n, n)
            with act.Fori(1, N_MOD // RING) as i:
                for s in range(RING):
                    row(RING * i + s, s)
            row(N_MOD - 1, (N_MOD - 1) % RING)
            for j in range(NPAIR):
                act.wait_ge(s_gt, j + 1)
                nc.scalar.activation(WT[:, j], cr.bank[j % 2][:, 0:2 * P].rearrange("p (r n) -> p r n", r=2),
                                     ACT.Copy).then_inc(s_gte, 1)

        @block.vector
        def _(dve):
            ln = Link(dve, s_dve)
            tt, ts = nc.vector.tensor_tensor, nc.vector.tensor_scalar
            stt = nc.vector.scalar_tensor_tensor
            dve.wait_ge(s_in, 16 * N_IN)
            dve.wait_ge(s_e, 2)
            tt(q1, are, dt, ALU.mult).then_inc(s_ed, 1)
            ln(tt(th, aim, dt, ALU.mult))
            ln(ts(kk, th, 1.0 / (2 * math.pi), None, ALU.mult))
            ln(ts(kk, kk, 12582912.0, -12582912.0, ALU.add, ALU.add))
            c1 = 6.28125
            c2 = 0.00193500518798828125
            c3 = 2 * math.pi - c1 - c2
            ln(stt(r_, kk, -c1, th, ALU.mult, ALU.add))
            ln(stt(r_, kk, -c2, r_, ALU.mult, ALU.add))
            ln(stt(r_, kk, -c3, r_, ALU.mult, ALU.add))
            pi = 3.1415925
            ln(ts(r_, r_, pi, -pi, ALU.min, ALU.max))
            ln(ts(q2, r_, -1.0, None, ALU.mult))
            ln(tt(q2, q2, r_, ALU.max))
            ts(q2, q2, -1.0, math.pi / 2, ALU.mult, ALU.add).then_inc(s_ed, 1)
            ln(tt(den, are, are, ALU.mult))
            ln(tt(nr, aim, aim, ALU.mult))
            ln(tt(den, den, nr, ALU.add))
            ln(nc.vector.reciprocal(den, den))
            dve.wait_ge(s_e, 5)
            ar, ai = pw[:, :, 1], pwi_[:, :, 1]
            ln(nc.vector.memset(pw[:, :, 0], 1.0))
            ln(nc.vector.memset(pwi_[:, :, 0], 0.0))
            ln(tt(ar, mag, cn, ALU.mult))
            ln(tt(ai, mag, sn, ALU.mult))
            ln(ts(nr, ar, -1.0, None, ALU.add))
            ln(tt(cfr, nr, are, ALU.mult))
            ln(tt(q1, ai, aim, ALU.mult))
            ln(tt(cfr, cfr, q1, ALU.add))
            ln(tt(cfr, cfr, den, ALU.mult))
            ln(tt(cfi, ai, are, ALU.mult))
            ln(tt(q1, nr, aim, ALU.mult))
            ln(tt(cfi, cfi, q1, ALU.subtract))
            ln(tt(cfi, cfi, den, ALU.mult))
            bc = lambda v: v.unsqueeze(2).broadcast_to([P, NPAIR, GRP])
            t16 = tmp9[:, :, 0, :]
            ln(tt(bb_r, b_r, bc(cfr), ALU.mult))
            ln(tt(t16, b_i, bc(cfi), ALU.mult))
            ln(tt(bb_r, bb_r, t16, ALU.subtract))
            ln(tt(bb_i, b_i, bc(cfr), ALU.mult))
            ln(tt(t16, b_r, bc(cfi), ALU.mult))
            ln(tt(bb_i, bb_i, t16, ALU.add))
            for t in range(2, 9):
                pr, pi_ = pw[:, :, t - 1], pwi_[:, :, t - 1]
                ln(tt(q1, pr, ar, ALU.mult))
                ln(tt(q2, pi_, ai, ALU.mult))
                ln(tt(pw[:, :, t], q1, q2, ALU.subtract))
                ln(tt(q1, pr, ai, ALU.mult))
                ln(tt(q2, pi_, ar, ALU.mult))
                ln(tt(pwi_[:, :, t], q1, q2, ALU.add))
            ln(nc.vector.tensor_copy(cr.small[:, S_A8R:S_A8R + 32], pw[:, :, 8]))
            ln(nc.vector.tensor_copy(cr.small[:, S_A8I:S_A8I + 32], pwi_[:, :, 8]))
            ln(ts(cr.small[:, S_NA8I:S_NA8I + 32], pwi_[:, :, 8], -1.0, None, ALU.mult))
            S9 = [P, NPAIR, 9, GRP]
            cb = lambda v: v.unsqueeze(2).broadcast_to(S9)
            pb = lambda v: v.unsqueeze(3).broadcast_to(S9)
            flat = lambda v: v.rearrange("p j t c -> p (j t c)")
            ln(tt(V[0], cb(c_r), pb(pw), ALU.mult))
            ln(tt(tmp9, cb(c_i), pb(pwi_), ALU.mult))
            ln(tt(flat(V[0]), flat(V[0]), flat(tmp9), ALU.subtract))
            ln(tt(V[1], cb(c_r), pb(pwi_), ALU.mult))
            ln(tt(tmp9, cb(c_i), pb(pw), ALU.mult))
            stt(flat(V[1]), flat(V[1]), -1.0, flat(tmp9), ALU.mult, ALU.subtract).then_inc(s_v, 1)
            dve.wait_ge(s_v, 1)
            t16 = tmp9[:, :, 0, :]
            for t in range(T_CH):
                pr, pi_ = bc(pw[:, :, 7 - t]), bc(pwi_[:, :, 7 - t])
                ln(tt(G[:, :, 0, t, :], bb_r, pr, ALU.mult))
                ln(tt(t16, bb_i, pi_, ALU.mult))
                ln(tt(G[:, :, 0, t, :], G[:, :, 0, t, :], t16, ALU.subtract))
                ln(tt(G[:, :, 1, t, :], bb_i, pr, ALU.mult))
                ln(tt(t16, bb_r, pi_, ALU.mult))
                ln(tt(G[:, :, 1, t, :], G[:, :, 1, t, :], t16, ALU.add))
            i16 = cr.const(C_ID)[0:GRP, 0:GRP].unsqueeze(1).broadcast_to([GRP, GROUPS, GRP])
            d16 = dcol[0:GRP, :].unsqueeze(2).broadcast_to([GRP, GROUPS, GRP])
            tt(Dd[0:GRP], i16, d16, ALU.mult).then_inc(s_g, 1)
            dve.wait_ge(s_tr, N_MOD)
            ln(tt(cr.modcol[:, :, :], psM[:, 0:480].rearrange("p (m v) -> p m v", v=3),
                  modb.unsqueeze(2).broadcast_to([P, 160, 3]), ALU.add))
            for g, (gain, col, var) in enumerate((
                    (0, MC_A + 8, V_C), (1, MC_KV + 8, V_C), (2, MC_B + 8, V_C),
                    (3, MC_L + 8, V_LAT), (3, MC_L + 8, V_CTX), (5, MC_L + 32, V_LAT), (5, MC_L + 32, V_CTX),
                    (4, MC_L + 56, V_LAT), (4, MC_L + 56, V_CTX), (6, MC_L + 80, V_LAT))):
                ln(stt(cr.gs[:, g, :], cr.modcol[:, col:col + 8, var], 1.0, cr.gains[:, gain, :], ALU.add, ALU.mult))
            dve.wait_ge(s_g, 1)
            for b in range(16):
                dve.wait_ge(s_kmm, b + 1)
                if b >= 2:
                    dve.wait_ge(s_kd[b % 2], 16 * (b // 2))
                g0 = b // 2 * 8 + b % 2
                ps = cr.bank[4 + b % 4][0:GRP, :].rearrange("p (g n) -> p g n", g=4)
                st = kst[0:GRP, b % 2]
                nc.vector.tensor_copy(st[:, :, GRP:P], ps[:, :, GRP:P])
                last = tt(st[:, :, 0:GRP], ps[:, :, 0:GRP], Dd[0:GRP, g0:g0 + 7:2, :], ALU.add)
                last.then_inc(s_kst, 1)


class Norm:

    def __init__(self, cr, prefix, nt, src, xn, outs, stat, before=None, fetched=None, store=None, width=D):
        (self.ss, self.var, self.std, self.rstd, self.xnr, self.tr, self.ev, self.st0, self.st1) = cr.sems(
            prefix + "_norm", "squares variance std rstd normed turned placed kept0 kept1")
        self.cr, self.nt, self.src, self.xn, self.outs = cr, nt, src, xn, outs
        self.stat = stat
        self.fetched, self.store, self.width = fetched, store, width
        self.st = (self.st0, self.st1)

    def _stat(self, j):
        return self.stat[:, j * self.nt:(j + 1) * self.nt]

    def act(self, act):
        nc = self.cr.nc
        for i in range(self.nt):
            if self.fetched:
                self.fetched(act, i)
            if i >= 2:
                act.wait_ge(self.ss, i - 1)
            nc.scalar.activation(self.xn[i % 2], self.src(i), ACT.Square,
                                 accum_out=self._stat(0)[:, i:i + 1]).then_inc(self.ss, 1)
        act.wait_ge(self.var, 1)
        nc.scalar.activation(self._stat(2), self._stat(1), ACT.Sqrt).then_inc(self.std, 1)
        act.wait_ge(self.rstd, 1)
        act.wait_ge(self.ss, self.nt)
        for i in range(self.nt):
            if i >= 2:
                act.wait_ge(self.tr, 2 * (i - 1))
                if self.store:
                    act.wait_ge(self.st[i % 2], 16 * (i // 2))
            nc.scalar.activation(self.xn[i % 2], self.src(i), ACT.Copy,
                                 scale=self._stat(3)[:, i:i + 1]).then_inc(self.xnr, 1)

    def dve(self, dve):
        nc = self.cr.nc
        dve.wait_ge(self.ss, self.nt)
        nc.vector.tensor_scalar(self._stat(1), self._stat(0), 1.0 / self.width, EPS, ALU.mult, ALU.add).then_inc(self.var, 1)
        dve.wait_ge(self.std, 1)
        nc.vector.reciprocal(self._stat(3), self._stat(2)).then_inc(self.rstd, 1)
        for i in range(self.nt):
            for h in range(2):
                dve.wait_ge(self.tr, 2 * i + h + 1)
                for q in range(4):
                    k = 4 * h + q
                    for dst, gain, shift in self.outs:
                        last = nc.vector.tensor_scalar(dst(k, i), self.cr.bank[h][:, q * P:(q + 1) * P],
                                                       gain(i)(k), shift(i)(k), ALU.mult, ALU.add)
                last.then_inc(self.ev, 1)

    def pe(self, pe):
        for i in range(self.nt):
            pe.wait_ge(self.xnr, i + 1)
            for h in range(2):
                if i:
                    pe.wait_ge(self.ev, 2 * i + h - 1)
                for q in range(4):
                    k = 4 * h + q
                    last = self.cr.nc.tensor.transpose(self.cr.bank[h][:, q * P:(q + 1) * P],
                                                       self.xn[i % 2][:, k * P:(k + 1) * P], self.cr.const(C_ID))
                last.then_inc(self.tr, 1)

    def keep(self, eng):
        for i in range(self.nt):
            eng.wait_ge(self.xnr, i + 1)
            eng.dma_start(self.store(i), self.xn[i % 2]).then_inc(self.st[i % 2], 16)

    def kept(self, eng):
        for s in range(2):
            eng.wait_ge(self.st[s], 16 * ((self.nt + 1 - s) // 2))


LBANK = (2, 3, 4, 5)


class Units:

    def __init__(self, cr, prefix):
        self.full, self.empty = cr.sems(prefix, "product_ready product_taken")
        self.cr, self.n = cr, 0

    def bank(self, u):
        return self.cr.bank[LBANK[u % 4]][:, :]

    def before(self, pe, u):
        if u >= 4:
            pe.wait_ge(self.empty, u - 3)


def stream(cr, sp, first, count, units, per_tile):
    u = 0
    for t in range(count):
        u += per_tile[t]
        sp.wait_ge(units.full, u)
        cr.load_w(sp, first + t + RING)


def product(cr, pe, un, bank_ap, pairs):
    un.before(pe, un.n)
    for k, (l, r) in enumerate(pairs):
        last = cr.nc.tensor.matmul(bank_ap, l, r, start=(k == 0), stop=(k == len(pairs) - 1))
    last.then_inc(un.full, 1)
    un.n += 1


def block_a_in(cr):
    nc, io = cr.nc, cr.io
    uT, zT = cr.dram("u_T", [D, SEQ]), cr.dram("z_T", [D, SEQ])
    x_in, st0, st1 = cr.sems("ain", "x_loaded stored0 stored1")
    st = (st0, st1)
    hT = cr.at(A_U, KT, SEQ)
    xa = cr.at(A_S, NT, D)
    stage = cr.at(A_M + 2048, 2, 512)
    un = Units(cr, "ain")
    nrm = Norm(cr, "ain", NT, lambda i: xa[:, i], [cr.at(A_M, D), cr.at(A_M + D, D)],
               [(lambda k, i: hT[:, k, i * P:(i + 1) * P], lambda i: cr.gain(GS_A), lambda i: cr.shift(MC_A, V_C))],
               cr.small[:, 300:332])
    NU = 32

    with nc.Block() as block:
        @block.sync
        def _(sp):
            sp.dma_start(xa, io["x"].rearrange("b (c t) d -> (b c) t d", t=T_CH)).then_inc(x_in, 16)
            stream(cr, sp, W_AIN, 4, un, [8] * 4)

        @block.scalar
        def _(act):
            act.wait_ge(x_in, 16)
            nrm.act(act)
            for u in range(NU):
                act.wait_ge(un.full, u + 1)
                if u >= 2:
                    act.wait_ge(st[u % 2], 16 * (u // 2))
                nc.scalar.activation(stage[:, u % 2], un.bank(u), ACT.Copy if u < NU // 2 else ACT.Silu).then_inc(un.empty, 1)

        @block.gpsimd
        def _(pool):
            for u in range(NU):
                m, h = u // 2, u % 2
                dst = (uT if m < KT else zT)[(m % KT) * P:(m % KT + 1) * P, h * 512:(h + 1) * 512]
                pool.wait_ge(un.empty, u + 1)
                pool.dma_start(dst, stage[:, u % 2]).then_inc(st[u % 2], 16)
            for s in range(2):
                pool.wait_ge(st[s], 16 * NU // 2)

        @block.vector
        def _(dve):
            nrm.dve(dve)

        @block.tensor
        def _(pe):
            nrm.pe(pe)
            pe.wait_ge(nrm.ev, 2 * NT)
            for t in range(4):
                cr.wait_w(pe, W_AIN + t)
                w = cr.w(W_AIN + t)
                for m in range(4):
                    for h in range(2):
                        product(cr, pe, un, un.bank(un.n), [(w[:, k, m * P:(m + 1) * P], hT[:, k, h * 512:(h + 1) * 512])
                                                            for k in range(KT)])


def block_ssm(cr):
    nc = cr.nc
    uT, Kd = cr.dram("u_T", [D, SEQ]), cr.dram("k_lags", [GRP, GROUPS, 2 * P])
    u_in, m0, m1, b_full, b_empty, s_link, s_scan, y_full, y_empty = cr.sems(
        "ssm", "u_loaded m_loaded0 m_loaded1 inputs_ready inputs_taken dve scanned y_ready y_taken")
    m_in = (m0, m1)
    V = [cr.at(A_V + r * 4608, NPAIR, 9, GRP) for r in range(2)]
    S = cr.at(A_S, 2, NPAIR, SCOL)
    U = cr.at(A_U, GROUPS, NCH)
    WT = cr.at(A_Y, NPAIR, 2, P)
    Y = cr.at(A_Y, T_CH, D)
    M = cr.at(A_M, 2, 8, P)
    sm = cr.small
    a8r, a8i, na8i = sm[:, S_A8R:S_A8R + 32], sm[:, S_A8I:S_A8I + 32], sm[:, S_NA8I:S_NA8I + 32]
    t1 = sm[:, S_T1:S_T1 + 64].rearrange("p (r j) -> p r j", r=2)
    t2 = sm[:, S_T2:S_T2 + 64].rearrange("p (r j) -> p r j", r=2)

    with nc.Block() as block:
        def load_m(eng, c):
            for t in range(T_CH):
                eng.dma_start(M[GRP * t:GRP * (t + 1), c % 2], Kd[:, 8 * c:8 * c + 8, P - GRP * t:2 * P - GRP * t]).then_inc(m_in[c % 2], 16)

        @block.sync
        def _(sp):
            for t in range(T_CH):
                sp.dma_start(U[GRP * t:GRP * (t + 1)], uT.rearrange("(g c) t -> c g t", c=GRP)[:, :, t * NCH:(t + 1) * NCH]).then_inc(u_in, 16)
            for c in range(8):
                if c >= 2:
                    sp.wait_ge(y_full, 2 * (c - 1))
                load_m(sp, c)

        @block.tensor
        def _(pe):
            pe.wait_ge(u_in, 16 * T_CH)
            for j in range(NPAIR):
                if j >= 4:
                    pe.wait_ge(b_empty, j - 3)
                for r in range(2):
                    for h in range(2):
                        last = nc.tensor.matmul(cr.bank[j % 4][64 * h:64 * h + 64, r * P:(r + 1) * P],
                                                WT[:, j, r, 64 * h:64 * h + 64], U[:, 2 * j + h, :], start=True, stop=True)
                last.then_inc(b_full, 1)
            pe.wait_ge(s_scan, 1)
            for g in range(GROUPS):
                j, h, b = g // 2, 64 * (g % 2), g // 8
                if g % 8 == 0:
                    pe.wait_ge(m_in[b % 2], P * (b // 2 + 1))
                    if b >= 2:
                        pe.wait_ge(y_empty, 2 * (b - 1))
                dst = cr.bank[4 + b % 2 * 2 + g % 2][:, (j % 4) * P:(j % 4 + 1) * P]
                nc.tensor.matmul(dst, U[:, g, :], M[:, (g // 8) % 2, g % 8, :], start=True, stop=False)
                for r in range(2):
                    last = nc.tensor.matmul(dst, S[h:h + 64, r, j, 0:NCH],
                                            V[r][h:h + 64, j, 1:9, :].rearrange("p t c -> p (t c)"),
                                            start=False, stop=(r == 1))
                if j % 4 == 3:
                    last.then_inc(y_full, 1)

        @block.scalar
        def _(act):
            for j in range(NPAIR):
                act.wait_ge(b_full, j + 1)
                nc.scalar.activation(S[:, :, j, 1:SCOL], cr.bank[j % 4][:, 0:2 * P].rearrange("p (r n) -> p r n", r=2),
                                     ACT.Copy).then_inc(b_empty, 1)
            for b in range(16):
                act.wait_ge(y_full, b + 1)
                g0 = b // 2 * 8 + b % 2
                nc.scalar.activation(Y.rearrange("p t (g c) -> p g t c", c=GRP)[:, g0:g0 + 7:2],
                                     cr.bank[4 + b % 4][:, :].rearrange("p (g t c) -> p g t c", g=4, t=T_CH),
                                     ACT.Gelu_apprx_tanh).then_inc(y_empty, 1)

        @block.vector
        def _(dve):
            ln = Link(dve, s_link)
            tt = nc.vector.tensor_tensor
            nc.vector.memset(S[:, :, :, 0:1], 0.0).then_inc(s_link, 1)
            dve.wait_ge(s_link, 1)
            dve.wait_ge(b_empty, NPAIR)
            a2 = a8r.unsqueeze(1).broadcast_to([P, 2, NPAIR])
            UNR = 4
            with dve.Fori(0, NCH // UNR) as i:
                for q in range(UNR):
                    k = UNR * i + q
                    at = lambda d: S[:, :, :, bass.ds(k + d, 1)].rearrange("p r j o -> p r (j o)")
                    s, b = at(0), at(1)
                    done = UNR * 3 * i + 3 * q + 1
                    tt(t1, s, a2, ALU.mult)
                    tt(t2[:, 0], s[:, 1], na8i, ALU.mult)
                    tt(t2[:, 1], s[:, 0], a8i, ALU.mult).then_inc(s_link, 1)
                    dve.wait_ge(s_link, done + 1)
                    tt(t1, t1, t2, ALU.add).then_inc(s_link, 1)
                    dve.wait_ge(s_link, done + 2)
                    tt(b, b, t1, ALU.add).then_inc(s_link, 1)
                    dve.wait_ge(s_link, done + 3)
            nc.vector.memset(t1, 0.0).then_inc(s_scan, 1)


def gate_diag(cr, dve_unused, diag, col, variant, sem):
    for k in range(KT):
        last = cr.nc.vector.tensor_scalar(diag[:, k * P:(k + 1) * P], cr.const(C_ID), cr.shift(col, variant)(k), None, ALU.mult)
    last.then_inc(sem, 1)


def gate_rows(cr, diag, banks, sem):
    for k in range(KT):
        last = cr.nc.tensor.matmul(cr.bank[banks[k // 4]][:, (k % 4) * P:(k % 4 + 1) * P], cr.const(C_ONE),
                                   diag[:, k * P:(k + 1) * P], start=True, stop=True)
    last.then_inc(sem, 1)


def X(cr):
    return cr.at(0, NTC, D)


def block_a_out(cr):
    nc, io = cr.nc, cr.io
    zT = cr.dram("z_T", [D, SEQ])
    x_in, z0, z1, t_full, t_empty, sg, s_l, s_g, s_y, d_ok, g_mm, g_ok = cr.sems(
        "aout", "x_loaded z_loaded0 z_loaded1 turned placed sigmoid dve gated y_done diag gate_mm gate_copied")
    z_in = (z0, z1)
    Xr = X(cr)
    yT = cr.at(10240, KT, SEQ)
    y3 = cr.at(18432, KT, SEQ)
    Y = cr.at(A_Y, T_CH, D)
    zs = cr.at(34816, 2, SEQ)
    gate = cr.at(36864, D)
    diag = cr.at(8192, D)
    tmp = cr.at(A_Y, 2, 512)
    un = Units(cr, "aout")
    bglu = cr.cols[:, 0:8]

    with nc.Block() as block:
        @block.sync
        def _(sp):
            sp.dma_start(Xr[:, 0:NT], io["x"].rearrange("b (i p) d -> (b p) i d", p=P)).then_inc(x_in, 16)
            stream(cr, sp, W_GLU, 4, un, [8] * 4)

        @block.gpsimd
        def _(pool):
            for m in range(KT):
                if m >= 2:
                    pool.wait_ge(s_g, 2 * (m - 1))
                pool.dma_start(zs[:, m % 2], zT[m * P:(m + 1) * P, :]).then_inc(z_in[m % 2], 16)

        @block.tensor
        def _(pe):
            pe.wait_ge(d_ok, 1)
            gate_rows(cr, diag, (6, 7), g_mm)
            for v in range(16):
                dch, h = v // 2, v % 2
                if v >= 2:
                    pe.wait_ge(t_empty, v - 1)
                for q in range(4):
                    last = nc.tensor.transpose(cr.bank[v % 2][:, q * P:(q + 1) * P], Y[:, 4 * h + q, dch * P:(dch + 1) * P], cr.const(C_ID))
                last.then_inc(t_full, 1)
            pe.wait_ge(t_empty, 16)
            for t in range(2):
                cr.wait_w(pe, W_GLU + t)
                w = cr.w(W_GLU + t)
                for m in range(4):
                    for h in range(2):
                        product(cr, pe, un, un.bank(un.n), [(w[:, k, m * P:(m + 1) * P], yT[:, k, h * 512:(h + 1) * 512]) for k in range(KT)])
            pe.wait_ge(s_g, 16)
            for t in range(2):
                cr.wait_w(pe, W_AOUT + t)
                w = cr.w(W_AOUT + t)
                for i in range(NT):
                    product(cr, pe, un, un.bank(un.n), [(y3[:, k, i * P:(i + 1) * P], w[:, k, :]) for k in range(KT)])

        @block.scalar
        def _(act):
            act.wait_ge(g_mm, 1)
            for b in range(2):
                nc.scalar.activation(gate[:, b * 512:(b + 1) * 512], cr.bank[6 + b][:, :], ACT.Copy).then_inc(g_ok, 1)
            for u in range(16):
                m, h = u // 2, u % 2
                act.wait_ge(un.full, u + 1)
                nc.scalar.activation(y3[:, m, h * 512:(h + 1) * 512], un.bank(u), ACT.Sigmoid, bias=bglu[:, m:m + 1]).then_inc(sg, 1)

        @block.vector
        def _(dve):
            ln = Link(dve, s_l)
            gate_diag(cr, dve, diag, MC_A + 16, V_C, d_ok)
            for v in range(16):
                dch, h = v // 2, v % 2
                dve.wait_ge(t_full, v + 1)
                nc.vector.tensor_copy(yT[:, dch].rearrange("p (c t) -> p t c", t=T_CH)[:, 4 * h:4 * h + 4],
                                      cr.bank[v % 2][:, :].rearrange("p (t c) -> p t c", t=4)).then_inc(t_empty, 1)
            dve.wait_ge(t_empty, 16)
            for u in range(16):
                m, h = u // 2, u % 2
                dve.wait_ge(sg, u + 1)
                y_ = y3[:, m, h * 512:(h + 1) * 512]
                nc.vector.tensor_tensor(y_, y_, yT[:, m, h * 512:(h + 1) * 512], ALU.mult).then_inc(un.empty, 1)
                dve.wait_ge(un.empty, u + 1)
                dve.wait_ge(z_in[m % 2], 16 * (m // 2 + 1))
                y4 = y_.rearrange("p (c t) -> p c t", t=T_CH)
                nc.vector.tensor_tensor(y4, y4, zs[:, m % 2].rearrange("p (t c) -> p c t", t=T_CH)[:, 64 * h:64 * h + 64], ALU.mult).then_inc(s_g, 1)
            dve.wait_ge(x_in, 16)
            dve.wait_ge(g_ok, 2)
            for u in range(16, 32):
                t, i = (u - 16) // NT, (u - 16) % NT
                dve.wait_ge(un.full, u + 1)
                residual_add(cr, dve, ln, un, u, tmp[:, u % 2], gate[:, t * 512:(t + 1) * 512], Xr[:, i, t * 512:(t + 1) * 512])


def residual_add(cr, dve, ln, un, u, tmp, gate, x):
    cr.nc.vector.tensor_tensor(tmp, un.bank(u), gate, ALU.mult).then_inc(un.empty, 1)
    dve.wait_ge(un.empty, u + 1)
    ln(cr.nc.vector.tensor_tensor(x, x, tmp, ALU.add))


def block_heads(cr, name, w0, gain, shift, head_col, scale, dst_T, dst_rows, rows_func, forget):
    nc, io = cr.nc, cr.io
    hT_d, rows_d = cr.dram(dst_T, [D, SEQ]), cr.dram(dst_rows, [SEQ, D])
    sq, red, var, std, rst, scaled, turned, placed, link = cr.sems(
        name, "squared reduced variance std rstd scaled turned placed dve")
    st, kst_ = cr.sems(name, "stored0 stored1"), cr.sems(name, "t_stored0 t_stored1")
    raw = cr.at(18432, NT, D)
    hT = cr.at(10240, KT, SEQ)
    stage = cr.at(28672, 2, 512)
    sqb = cr.at(29696, 2, 512)
    kst = cr.at(30720, 2, 512)
    hs = cr.at(31744, 4, NT * HB)
    un = Units(cr, name)
    Xr = X(cr)
    nrm = Norm(cr, name, NT, lambda i: Xr[:, i], [cr.at(26624, D), cr.at(27648, D)],
               [(lambda k, i: hT[:, k, i * P:(i + 1) * P], lambda i: cr.gain(gain), lambda i: cr.shift(shift, V_C))],
               cr.small[:, 300:332])
    if forget:
        f_in, f_mm, f_x, f_e, f_l, f_ls, f_cum, f_row, f_st = cr.sems(
            name, "f_loaded f_logits f_biased f_exp f_log f_logsig f_sums f_rows f_stored")
        fw = cr.at(32256, KT, HB)
        fb = cr.at(32384, HB)
        fx, fa, fe, fl = [cr.at(32400 + 128 * n, NT, HB) for n in range(4)]
        FT = cr.at(33000, 2, SEQ)
        F_d = cr.dram("f_rows", [2, HB, SEQ])

    with nc.Block() as block:
        @block.sync
        def _(sp):
            if forget:
                sp.dma_start(fw, io["f_w"]).then_inc(f_in, 16)
                sp.dma_start(fb, io["f_b"].broadcast_to([P, HB])).then_inc(f_in, 16)
            stream(cr, sp, w0, 4, un, [8] * 4)
            if forget:
                sp.wait_ge(f_row, 1)
                for n in range(2):
                    sp.dma_start(F_d[n], FT[0:HB, n]).then_inc(f_st, 16)
            for v in range(16):
                c, h = v // 2, v % 2
                sp.wait_ge(placed, v + 1)
                sp.dma_start(hT_d[c * P:(c + 1) * P, h * 512:(h + 1) * 512], kst[:, v % 2]).then_inc(kst_[v % 2], 16)
            for s in range(2):
                sp.wait_ge(kst_[s], 16 * 8)
            if forget:
                sp.wait_ge(f_st, 32)

        @block.gpsimd
        def _(pool):
            for u in range(16, 32):
                t, i = (u - 16) // NT, u % NT
                pool.wait_ge(un.empty, u + 1)
                pool.dma_start(rows_d[i * P:(i + 1) * P, t * 512:(t + 1) * 512], stage[:, u % 2]).then_inc(st[u % 2], 16)
            for s in range(2):
                pool.wait_ge(st[s], 16 * 8)

        @block.tensor
        def _(pe):
            nrm.pe(pe)
            pe.wait_ge(nrm.ev, 2 * NT)
            if forget:
                pe.wait_ge(f_in, 32)
                for i in range(NT):
                    for k in range(KT):
                        last = nc.tensor.matmul(cr.bank[7][:, i * HB:(i + 1) * HB], hT[:, k, i * P:(i + 1) * P], fw[:, k],
                                                start=(k == 0), stop=(k == KT - 1))
                last.then_inc(f_mm, 1)
            for t in range(4):
                cr.wait_w(pe, w0 + t)
                w = cr.w(w0 + t)
                for i in range(NT):
                    product(cr, pe, un, un.bank(un.n), [(hT[:, k, i * P:(i + 1) * P], w[:, k, :]) for k in range(KT)])
                if forget and t == 1:
                    pe.wait_ge(f_ls, 1)
                    for i in range(NT):
                        for j in range(i + 1):
                            last = nc.tensor.matmul(cr.bank[i // 4][0:HB, (i % 4) * P:(i % 4 + 1) * P], fe[:, j],
                                                    cr.const(C_TRI if j == i else C_ONE), start=(j == 0), stop=(j == i))
                    last.then_inc(f_cum, 1)
            for v in range(16):
                c, h = v // 2, v % 2
                pe.wait_ge(scaled, NT)
                if v >= 2:
                    pe.wait_ge(placed, v - 1)
                for q in range(4):
                    i = 4 * h + q
                    last = nc.tensor.transpose(cr.bank[6 + v % 2][:, q * P:(q + 1) * P], raw[:, i, c * P:(c + 1) * P], cr.const(C_ID))
                last.then_inc(turned, 1)

        @block.scalar
        def _(act):
            nrm.act(act)
            if forget:
                act.wait_ge(f_x, 1)
                nc.scalar.activation(fe, fa, ACT.Exp, scale=-1.0).then_inc(f_e, 1)
                act.wait_ge(f_e, 1)
                nc.scalar.activation(fl, fe, ACT.Ln, bias=1.0).then_inc(f_l, 1)
            for u in range(16):
                t, i = u // NT, u % NT
                act.wait_ge(un.full, u + 1)
                r = raw[:, i, t * 512:(t + 1) * 512]
                if u >= 2:
                    act.wait_ge(red, u - 1)
                nc.scalar.activation(sqb[:, u % 2], un.bank(u), ACT.Square).then_inc(sq, 1)
                nc.scalar.activation(r, un.bank(u), ACT.Copy).then_inc(un.empty, 1)
            act.wait_ge(var, 1)
            nc.scalar.activation(hs[:, 2], hs[:, 1], ACT.Sqrt).then_inc(std, 1)
            for u in range(16, 32):
                act.wait_ge(un.full, u + 1)
                if u >= 18:
                    act.wait_ge(st[u % 2], 16 * ((u - 16) // 2))
                nc.scalar.activation(stage[:, u % 2], un.bank(u), rows_func).then_inc(un.empty, 1)

        @block.vector
        def _(dve):
            ln = Link(dve, link)
            nrm.dve(dve)
            tt, ts = nc.vector.tensor_tensor, nc.vector.tensor_scalar
            if forget:
                dve.wait_ge(f_mm, 1)
                ln(tt(fx, cr.bank[7][:, 0:NT * HB].rearrange("p (i h) -> p i h", h=HB), fb.unsqueeze(1).broadcast_to([P, NT, HB]), ALU.add))
                ln(ts(fa, fx, -1.0, None, ALU.mult))
                tt(fa, fa, fx, ALU.max).then_inc(f_x, 1)
                dve.wait_ge(f_l, 1)
                flat = lambda v: v.rearrange("p i h -> p (i h)")
                nc.vector.scalar_tensor_tensor(flat(fe), flat(fx), 0.0, flat(fl), ALU.min, ALU.subtract).then_inc(f_ls, 1)
            for u in range(16):
                t, i = u // NT, u % NT
                dve.wait_ge(sq, u + 1)
                nc.vector.tensor_reduce(hs[:, 0, i * HB + 8 * t:i * HB + 8 * t + 8], sqb[:, u % 2].rearrange("p (h d) -> p h d", d=HD),
                                        AXX, ALU.add).then_inc(red, 1)
            dve.wait_ge(red, 16)
            ts(hs[:, 1], hs[:, 0], 1.0 / HD, EPS, ALU.mult, ALU.add).then_inc(var, 1)
            dve.wait_ge(std, 1)
            nc.vector.reciprocal(hs[:, 3], hs[:, 2]).then_inc(rst, 1)
            dve.wait_ge(rst, 1)
            dve.wait_ge(un.empty, 16)
            for i in range(NT):
                r = raw[:, i].rearrange("p (h d) -> p h d", d=HD)
                tt(r, r, hs[:, 3, i * HB:(i + 1) * HB].unsqueeze(2).broadcast_to([P, HB, HD]), ALU.mult).then_inc(scaled, 1)
            if forget:
                dve.wait_ge(f_cum, 1)
                for b in range(2):
                    ln(nc.vector.tensor_copy(FT[0:HB, 0, b * 512:(b + 1) * 512], cr.bank[b][0:HB, :]))
                ts(FT[0:HB, 1], FT[0:HB, 0], -1.0, None, ALU.mult).then_inc(f_row, 1)
            for v in range(16):
                dve.wait_ge(turned, v + 1)
                if v >= 2:
                    dve.wait_ge(kst_[v % 2], 16 * (v // 2))
                ts(kst[:, v % 2], cr.bank[6 + v % 2][:, :], cr.cols[:, head_col:head_col + 1], scale, ALU.mult, ALU.mult).then_inc(placed, 1)


def block_kv(cr):
    block_heads(cr, "kv", W_KV, GS_KV, MC_KV, 8, 1.0, "k_T", "v_rows", ACT.Copy, True)


def block_bq(cr):
    block_heads(cr, "bq", W_BIN, GS_B, MC_B, 9, HD ** -0.5, "q_T", "zb_rows", ACT.Silu, False)


class Step:

    def __init__(self, slot, q, pieces, masks, width, pv, sink, o):
        self.slot, self.q, self.pieces, self.masks = slot, q, pieces, masks
        self.width, self.pv, self.sink, self.o = width, pv, sink, o
        self.groups = (len(pv) + 3) // 4


def attention(cr, name, n_iter, steps, loads, static_loads, store, scores_banks, p_buf, t_buf, share_o):
    nc = cr.nc
    qk, mx, pr, tr, te, pv, oe, li, s_in = cr.sems(name, "scores maxima probs turned placed products o_taken dve fixed_loaded")
    ld, st = cr.sems(name, "loaded0 loaded1"), cr.sems(name, "stored0 stored1")
    NS = len(steps)
    goff = [0]
    for s_ in steps:
        goff.append(goff[-1] + s_.groups)
    NG = goff[-1]
    last_of = [max(n for n, s_ in enumerate(steps) if s_.slot == k) for k in range(2)]
    first_of = [min(n for n, s_ in enumerate(steps) if s_.slot == k) for k in range(2)]
    NL = [len(loads(k, 0)) for k in range(2)]
    nb = scores_banks
    nmax, rsum, rinv = [cr.small[:, 300 + 2 * n:302 + 2 * n] for n in range(3)]
    pt0 = 2 * nb
    o_at = (lambda u: cr.bank[u % 2 * nb + nb - 1][:, 256:256 + HD]) if share_o else (lambda u: cr.bank[6 + u % 2][:, 0:HD])

    def sc(u, a, b):
        n = a // 512
        assert (b - 1) // 512 == n
        return cr.bank[u % 2 * nb + n][:, a - 512 * n:b - 512 * n]

    def sc_wide(u, w):
        return cr.score_view(u % 2, nb)[:, 0:w]

    with nc.Block() as block:
        @block.sync
        def _(sp):
            for k in range(2):
                sp.sem_inc(st[k], 1)
            for to, of in static_loads:
                sp.dma_start(to, of).then_inc(s_in, 16)
            for k in range(2):
                for to, of in loads(k, 0):
                    sp.dma_start(to, of).then_inc(ld[k], 16)
            def finish(k, it):
                sp.wait_ge(oe, it * NS + (last_of[k] + 2))
                to, of = store(k, it)
                sp.dma_start(to, of).then_inc(st[k], 16)

            with sp.Fori(0, n_iter - 1) as it:
                for k in range(2):
                    finish(k, it)
                    for to, of in loads(k, it + 1):
                        sp.dma_start(to, of).then_inc(ld[k], 16)
            for k in range(2):
                finish(k, n_iter - 1)
            for k in range(2):
                sp.wait_ge(st[k], 16 * n_iter + 1)

        @block.tensor
        def _(pe):
            pe.wait_ge(s_in, 16 * len(static_loads))
            with pe.Fori(0, n_iter) as it:
                def scores(u):
                    s_ = steps[u]
                    if u in first_of:
                        pe.wait_ge(ld[s_.slot], (it + 1) * (16 * NL[s_.slot]))
                    pe.wait_ge(pr, it * NS + max(u, 1))
                    if share_o:
                        pe.wait_ge(oe, it * NS + max(u, 1))
                    for a, b, rhs in s_.pieces:
                        last = nc.tensor.matmul(sc(u, a, b), s_.q, rhs, start=True, stop=True)
                    last.then_inc(qk, 1)

                def values(u):
                    s_ = steps[u]
                    pe.wait_ge(pr, it * NS + (u + 2))
                    for g in range(s_.groups):
                        G = goff[u] + g
                        pe.wait_ge(te, it * NG + max(G, 1))
                        for n in range(4 * g, min(4 * g + 4, len(s_.pv))):
                            last = nc.tensor.transpose(cr.bank[pt0 + G % 2][:, (n % 4) * P:(n % 4 + 1) * P],
                                                       p_buf[:, u % 2, s_.pv[n][0]:s_.pv[n][0] + P], cr.const(C_ID))
                        last.then_inc(tr, 1)
                    pe.wait_ge(te, it * NG + (goff[u + 1] + 1))
                    pe.wait_ge(oe, it * NS + max(u, 1))
                    for n, (_, v) in enumerate(s_.pv):
                        last = nc.tensor.matmul(o_at(u), t_buf[:, u % 2, n, :], v, start=(n == 0), stop=(n == len(s_.pv) - 1))
                    last.then_inc(pv, 1)

                for u in range(NS):
                    scores(u)
                    if u:
                        values(u - 1)
                values(NS - 1)

        @block.scalar
        def _(act):
            act.sem_inc(pr, 1)
            with act.Fori(0, n_iter) as it:
                for u, s_ in enumerate(steps):
                    act.wait_ge(mx, it * NS + (u + 1))
                    act.wait_ge(oe, it * NS + max(u, 1))
                    w = s_.width + (s_.sink is not None)
                    nc.scalar.activation(p_buf[:, u % 2, 0:w], sc_wide(u, w), ACT.Exp, bias=nmax[:, u % 2:u % 2 + 1],
                                         accum_out=rsum[:, u % 2:u % 2 + 1]).then_inc(pr, 1)

        @block.vector
        def _(dve):
            dve.sem_inc(te, 1)
            dve.sem_inc(oe, 1)
            dve.wait_ge(s_in, 16 * len(static_loads))
            NLK = sum((len(s_.masks) + (s_.sink is not None) > 0) + 1 for s_ in steps)
            with dve.Fori(0, n_iter) as it:
                links = [0]

                def maximum(u):
                    s_ = steps[u]
                    dve.wait_ge(qk, it * NS + (u + 1))
                    dve.wait_ge(pr, it * NS + max(u, 1))
                    last = None
                    for col, c in s_.masks:
                        last = nc.vector.tensor_tensor(sc(u, col, col + P), sc(u, col, col + P), cr.const(c), ALU.add)
                    w = s_.width
                    if s_.sink is not None:
                        last = nc.vector.tensor_scalar(sc(u, w, w + 1), s_.sink(it), 1.0, None, ALU.mult)
                        w += 1
                    if last is not None:
                        links[0] += 1
                        last.then_inc(li, 1)
                        dve.wait_ge(li, it * NLK + links[0])
                    nc.vector.tensor_reduce(nmax[:, u % 2:u % 2 + 1], sc_wide(u, w), AXX, ALU.max, negate=True).then_inc(mx, 1)

                def taken(u):
                    s_ = steps[u]
                    for g in range(s_.groups):
                        G = goff[u] + g
                        m = min(4, len(s_.pv) - 4 * g)
                        dve.wait_ge(tr, it * NG + (G + 1))
                        nc.vector.tensor_copy(t_buf[:, u % 2, 4 * g:4 * g + m, :].rearrange("p n q -> p (n q)"),
                                              cr.bank[pt0 + G % 2][:, 0:m * P]).then_inc(te, 1)
                    links[0] += 1
                    nc.vector.reciprocal(rinv[:, u % 2:u % 2 + 1], rsum[:, u % 2:u % 2 + 1]).then_inc(li, 1)
                    dve.wait_ge(li, it * NLK + links[0])
                    dve.wait_ge(pv, it * NS + (u + 1))
                    if u in first_of:
                        dve.wait_ge(st[s_.slot], 16 * it + 1)
                    nc.vector.tensor_scalar(s_.o, o_at(u), rinv[:, u % 2:u % 2 + 1], None, ALU.mult).then_inc(oe, 1)

                for u in range(NS):
                    maximum(u)
                    if u:
                        taken(u - 1)
                taken(NS - 1)
                assert links[0] == NLK


def rows_of(ap, it_col, width, tiles):
    return ap.rearrange("(i p) c -> p i c", p=P)[:, 0:tiles, bass.ds(it_col, width)]


def block_fox(cr):
    qT, kT, v_d, F_d = (cr.dram(n, s_) for n, s_ in (("q_T", [D, SEQ]), ("k_T", [D, SEQ]), ("v_rows", [SEQ, D]), ("f_rows", [2, HB, SEQ])))
    O = cr.dram("o_rows", [NTOK, D])
    KD = HD + 2
    qa, ka = cr.at(10240, 2, SEQ), cr.at(12288, 2, SEQ)
    vb = cr.at(14336, 2, NT, HD)
    p_buf, t_buf = cr.at(15360, 2, 1024), cr.at(17408, 2, NT, P)
    ob = cr.at(19456, 2, NT, HD)
    ones = cr.io["ones"][0:1, 0:SEQ]

    def loads(k, it):
        h = 2 * it + k
        return [(qa[0:HD, k], qT[bass.ds(h * HD, HD), :]), (ka[0:HD, k], kT[bass.ds(h * HD, HD), :]),
                (qa[HD:HD + 1, k], F_d[0, bass.ds(h, 1), :]), (ka[HD + 1:HD + 2, k], F_d[1, bass.ds(h, 1), :]),
                (vb[:, k], rows_of(v_d, h * HD, HD, NT))]

    steps = []
    for k in range(2):
        for i in range(NT):
            w = (i + 1) * P
            pieces = [(a, min(a + 512, w), ka[0:KD, k, a:min(a + 512, w)]) for a in range(0, w, 512)]
            steps.append(Step(k, qa[0:KD, k, i * P:(i + 1) * P], pieces, [(i * P, C_CAUSAL)], w,
                              [(n * P, vb[:, k, n]) for n in range(i + 1)], None, ob[:, k, i]))
    static = [(qa[HD + 1:HD + 2, k], ones) for k in range(2)] + [(ka[HD:HD + 1, k], ones) for k in range(2)]
    attention(cr, "fox", HB // 2, steps, loads, static,
              lambda k, it: (rows_of(O, (2 * it + k) * HD, HD, NT), ob[:, k]), 2, p_buf, t_buf, False)


def block_out(cr, name, w0, nt, oc, z_name, t_name, gates):
    nc = cr.nc
    O = cr.dram("o_rows", [NTOK, D])
    z_d = cr.dram(z_name, [SEQ, D]) if z_name else None
    t_d = cr.dram(t_name, [512, NTOK]) if t_name else None
    mult, tr, te, t_in, d_ok, g_mm, g_ok, link = cr.sems(name, "gated turned placed t_loaded diag gate_mm gate_copied dve")
    ld = cr.sems(name, "loaded0 loaded1")
    OT = cr.at(10240, KT, NTOK)
    orow, zrow = cr.at(20480, 2, D), cr.at(22528, 2, D)
    gate = cr.at(24576, 2, D)
    diag = cr.at(26624, 2, D)
    tmp = cr.at(28672, 2, 512)
    un = Units(cr, name)
    Xr = X(cr)
    nh = (oc + 3) // 4
    nl = 2 if z_d is not None else 1

    with nc.Block() as block:
        @block.sync
        def _(sp):
            if t_d is not None:
                sp.dma_start(OT[:, oc:KT, 0:nt * P], t_d.rearrange("(k p) n -> p k n", p=P)[:, :, 0:nt * P]).then_inc(t_in, 16)
            for i in range(nt):
                if i >= 2:
                    sp.wait_ge(tr, nh * (i - 1))
                sp.dma_start(orow[:, i % 2, 0:oc * P], O[i * P:(i + 1) * P, 0:oc * P]).then_inc(ld[i % 2], 16)
                if z_d is not None:
                    sp.dma_start(zrow[:, i % 2], z_d[i * P:(i + 1) * P, :]).then_inc(ld[i % 2], 16)
            stream(cr, sp, w0, 2, un, [nt] * 2)

        @block.tensor
        def _(pe):
            for n, g in enumerate(gates):
                pe.wait_ge(d_ok, n + 1)
                if n:
                    pe.wait_ge(g_ok, 2 * n)
                gate_rows(cr, diag[:, n], (6, 7), g_mm)
            for i in range(nt):
                pe.wait_ge(mult if z_d is not None else ld[i % 2], i + 1 if z_d is not None else 16 * (i // 2 + 1))
                for h in range(nh):
                    if i:
                        pe.wait_ge(te, nh * (i - 1) + h + 1)
                    for q in range(4):
                        k = 4 * h + q
                        last = nc.tensor.transpose(cr.bank[h][:, q * P:(q + 1) * P], orow[:, i % 2, k * P:(k + 1) * P], cr.const(C_ID))
                    last.then_inc(tr, 1)
            pe.wait_ge(te, nh * nt)
            if t_d is not None:
                pe.wait_ge(t_in, 16)
            for t in range(2):
                cr.wait_w(pe, w0 + t)
                w = cr.w(w0 + t)
                for i in range(nt):
                    product(cr, pe, un, un.bank(un.n), [(OT[:, k, i * P:(i + 1) * P], w[:, k, :]) for k in range(KT)])

        @block.scalar
        def _(act):
            for n in range(len(gates)):
                act.wait_ge(g_mm, n + 1)
                for b in range(2):
                    nc.scalar.activation(gate[:, n, b * 512:(b + 1) * 512], cr.bank[6 + b][:, :], ACT.Copy).then_inc(g_ok, 1)
            for i in range(nt):
                for h in range(nh):
                    act.wait_ge(tr, nh * i + h + 1)
                    nc.scalar.activation(OT[:, 4 * h:4 * h + 4, i * P:(i + 1) * P], cr.bank[h][:, :].rearrange("p (k n) -> p k n", k=4),
                                         ACT.Copy).then_inc(te, 1)

        @block.vector
        def _(dve):
            ln = Link(dve, link)
            for n, (col, var) in enumerate(gates):
                gate_diag(cr, dve, diag[:, n], col, var, d_ok)
            if z_d is not None:
                for i in range(nt):
                    dve.wait_ge(ld[i % 2], 16 * nl * (i // 2 + 1))
                    nc.vector.tensor_tensor(orow[:, i % 2], orow[:, i % 2], zrow[:, i % 2], ALU.mult).then_inc(mult, 1)
            dve.wait_ge(g_ok, 2 * len(gates))
            for u in range(2 * nt):
                t, i = u // nt, u % nt
                dve.wait_ge(un.full, u + 1)
                g = gate[:, 1 if i >= NT else 0, t * 512:(t + 1) * 512]
                residual_add(cr, dve, ln, un, u, tmp[:, u % 2], g, Xr[:, i, t * 512:(t + 1) * 512])


def block_bout(cr):
    block_out(cr, "bout", W_BOUT, NT, KT, "zb_rows", None, [(MC_B + 16, V_C)])


def variant(lat, ctx):
    return lambda i: lat if i < NT else ctx


def rope(nc, ln, x1, x2, cos, sin, o1, o2, ta, tb):
    tt = nc.vector.tensor_tensor
    tt(o1, x1, cos, ALU.mult)
    tt(ta, x2, sin, ALU.mult)
    tt(o2, x2, cos, ALU.mult)
    ln(tt(tb, x1, sin, ALU.mult))
    tt(o1, o1, ta, ALU.subtract)
    return tt(o2, o2, tb, ALU.add)


def block_ein(cr):
    nc, io = cr.nc, cr.io
    kT, qT, v_d, s_T = (cr.dram(n, s_) for n, s_ in (("ek_T", [P, NTOK]), ("eq_T", [512, NTOK]), ("ev_rows", [NTOK, P]), ("s_T", [512, NTOK])))
    x_in, c_in, link, turned, placed, v_st, s_bn, s_std, s_rst, s_vn, s_mm, s_s = cr.sems(
        "ein", "ctx_loaded tables_loaded dve turned placed v_stored moments std rstd v_normed mixed gated")
    kst_, sst_ = cr.sems("ein", "t_stored0 t_stored1"), cr.sems("ein", "s_stored0 s_stored1")
    Xr = X(cr)
    hT = cr.at(10240, KT, NTOK)
    raw = cr.at(22528, NTC, 768)
    uT = cr.at(30208, 4, NTOK)
    vrow = cr.at(35328, 2, 512)
    kst = vrow
    wsT = cr.at(36352, 4, P)
    bs = cr.at(36864, 4, P)
    gln = cr.at(37376, 512)
    tab = cr.at(37888, NT, 2, 32)
    vn = cr.at(20480, 2, 512)
    sst = cr.at(21504, 2, 4, P)
    ta, tb = cr.small[:, 340:596], cr.small[:, 596:852]
    mom = cr.small[:, 852:892]
    un = Units(cr, "ein")
    nrm = Norm(cr, "ein", NTC, lambda i: Xr[:, i], [cr.at(20480, D), cr.at(20480 + D, D)],
               [(lambda k, i: hT[:, k, i * P:(i + 1) * P], variant(cr.gain(GS_1L0), cr.gain(GS_1C0)),
                 variant(cr.shift(MC_L, V_LAT), cr.shift(MC_L, V_CTX)))], cr.small[:, 300:340])
    TOK = [(0, 512), (512, 1024), (1024, NTOK)]
    GROUPS_T = [(0, 4), (4, 8), (8, 10)]
    NR = 2 * NTC
    NU = 4 * 3

    with nc.Block() as block:
        @block.sync
        def _(sp):
            sp.dma_start(Xr[:, NT:NTC], io["ctx"].rearrange("b (i p) d -> (b p) i d", p=P)).then_inc(x_in, 16)
            for to, of in ((wsT, io["sgu_w"]), (bs.rearrange("p g q -> p (g q)"), io["sgu_b"].broadcast_to([P, 512])),
                           (gln, io["sgu_g"].broadcast_to([P, 512])), (tab, io["rope_a"])):
                sp.dma_start(to, of).then_inc(c_in, 16)
            stream(cr, sp, W_EIN, 4, un, [NTC, NTC, NU, NTC])

        @block.gpsimd
        def _(pool):
            pool.wait_ge(un.empty, NTC)
            pool.dma_start(v_d.rearrange("(i p) c -> p i c", p=P), raw[:, :, 640:768]).then_inc(v_st, 16)
            for v in range(15):
                c, (a, b) = v // 3, GROUPS_T[v % 3]
                dst = kT if c == 0 else qT[(c - 1) * P:c * P, :]
                pool.wait_ge(placed, v + 1)
                pool.dma_start(dst[:, a * P:b * P], kst[:, v % 2, 0:(b - a) * P]).then_inc(kst_[v % 2], 16)
            for i in range(NTC):
                pool.wait_ge(s_s, i + 1)
                pool.dma_start(s_T.rearrange("(g d) n -> d g n", d=P)[:, :, i * P:(i + 1) * P], sst[:, i % 2]).then_inc(sst_[i % 2], 16)
            pool.wait_ge(v_st, 16)
            for k in range(2):
                pool.wait_ge(kst_[k], 16 * (8 - k))
                pool.wait_ge(sst_[k], 16 * 5)

        @block.tensor
        def _(pe):
            nrm.pe(pe)
            pe.wait_ge(nrm.ev, 2 * NTC)
            for t in range(2):
                cr.wait_w(pe, W_EIN + t)
                w = cr.w(W_EIN + t)
                n = 512 if t else 256
                for i in range(NTC):
                    product(cr, pe, un, un.bank(un.n)[:, 0:n], [(hT[:, k, i * P:(i + 1) * P], w[:, k, 0:n]) for k in range(KT)])
            cr.wait_w(pe, W_EIN + 2)
            w = cr.w(W_EIN + 2)
            for m in range(4):
                for a, b in TOK:
                    product(cr, pe, un, un.bank(un.n)[:, 0:b - a], [(w[:, k, m * P:(m + 1) * P], hT[:, k, a:b]) for k in range(KT)])
            pe.wait_ge(un.empty, NR)
            for v in range(15):
                c, (a, b) = v // 3, GROUPS_T[v % 3]
                if v >= 2:
                    pe.wait_ge(placed, v - 1)
                for i in range(a, b):
                    last = nc.tensor.transpose(cr.bank[6 + v % 2][:, (i - a) * P:(i - a + 1) * P], raw[:, i, c * P:(c + 1) * P], cr.const(C_ID))
                last.then_inc(turned, 1)
            cr.wait_w(pe, W_EIN + 3)
            w = cr.w(W_EIN + 3)
            pe.wait_ge(placed, 15)

            def mix(i):
                pe.wait_ge(s_vn, i + 1)
                if i >= 2:
                    pe.wait_ge(s_s, i - 1)
                for g in range(4):
                    last = nc.tensor.matmul(cr.bank[6 + i % 2][:, g * P:(g + 1) * P], vn[:, i % 2, g * P:(g + 1) * P], wsT[:, g],
                                            start=True, stop=True)
                last.then_inc(s_mm, 1)

            for i in range(NTC):
                product(cr, pe, un, un.bank(un.n), [(hT[:, k, i * P:(i + 1) * P], w[:, k, :]) for k in range(KT)])
                if i:
                    mix(i - 1)
            mix(NTC - 1)

        @block.scalar
        def _(act):
            act.wait_ge(x_in, 16)
            nrm.act(act)
            u0 = NR
            act.wait_ge(un.empty, NR)
            for n in range(NU):
                m, (a, b) = n // 3, TOK[n % 3]
                act.wait_ge(un.full, u0 + n + 1)
                nc.scalar.activation(uT[:, m, a:b], un.bank(u0 + n)[:, 0:b - a], ACT.Gelu_apprx_tanh).then_inc(un.empty, 1)
            act.wait_ge(kst_[0], 16 * 8)
            act.wait_ge(kst_[1], 16 * 7)
            u0 += NU
            for i in range(NTC):
                act.wait_ge(un.full, u0 + i + 1)
                if i >= 2:
                    act.wait_ge(s_vn, i - 1)
                nc.scalar.activation(vrow[:, i % 2], un.bank(u0 + i), ACT.Gelu_apprx_tanh).then_inc(un.empty, 1)
                act.wait_ge(s_bn, i + 1)
                nc.scalar.activation(mom[:, 12 + i % 2:13 + i % 2], mom[:, 10 + i % 2:11 + i % 2], ACT.Sqrt).then_inc(s_std, 1)

        @block.vector
        def _(dve):
            ln = Link(dve, link)
            tt, ts = nc.vector.tensor_tensor, nc.vector.tensor_scalar
            nrm.dve(dve)
            dve.wait_ge(c_in, 64)

            def turn(i, ps, lo, heads):
                x = ps.rearrange("p (h e d) -> p h e d", h=heads, e=2)
                o = raw[:, i, lo:lo + heads * HD].rearrange("p (h e d) -> p h e d", h=heads, e=2)
                c, s_ = (tab[:, i, n].unsqueeze(1).broadcast_to([P, heads, 32]) for n in range(2))
                n = heads * 32
                t1, t2 = (v[:, 0:n].rearrange("p (h d) -> p h d", h=heads) for v in (ta, tb))
                return rope(nc, ln, x[:, :, 0], x[:, :, 1], c, s_, o[:, :, 0], o[:, :, 1], t1, t2)

            for u in range(NR):
                t, i = u // NTC, u % NTC
                dve.wait_ge(un.full, u + 1)
                ps = un.bank(u)
                if t == 0:
                    if i < NT:
                        ln(turn(i, ps[:, 0:P], 0, 2))
                    else:
                        ln(nc.vector.tensor_copy(raw[:, i, 0:P], ps[:, 0:P]))
                    nc.vector.tensor_copy(raw[:, i, 640:768], ps[:, P:2 * P]).then_inc(un.empty, 1)
                else:
                    if i < NT:
                        ln(turn(i, ps, P, 8))
                    else:
                        ln(nc.vector.tensor_copy(raw[:, i, P:640], ps))
                    ts(raw[:, i, P:640], raw[:, i, P:640], HD ** -0.5, None, ALU.mult).then_inc(un.empty, 1)
            for v in range(15):
                a, b = GROUPS_T[v % 3]
                dve.wait_ge(turned, v + 1)
                if v >= 2:
                    dve.wait_ge(kst_[v % 2], 16 * (v // 2))
                nc.vector.tensor_copy(kst[:, v % 2, 0:(b - a) * P], cr.bank[6 + v % 2][:, 0:(b - a) * P]).then_inc(placed, 1)
            u0 = NR + NU
            for i in range(NTC):
                dve.wait_ge(un.empty, u0 + i + 1)
                vr = vrow[:, i % 2]
                ln(nc.vector.bn_stats(mom[:, 0:6], vr))
                ln(nc.vector.bn_aggr(mom[:, 6:8], mom[:, 0:6]))
                ts(mom[:, 10 + i % 2:11 + i % 2], mom[:, 7:8], EPS, None, ALU.add).then_inc(s_bn, 1)
                dve.wait_ge(s_std, i + 1)
                ln(nc.vector.reciprocal(mom[:, 14:15], mom[:, 12 + i % 2:13 + i % 2]))
                if i >= 2:
                    dve.wait_ge(s_mm, i - 1)
                ln(ts(vn[:, i % 2], vr, mom[:, 6:7], mom[:, 14:15], ALU.subtract, ALU.mult))
                tt(vn[:, i % 2], vn[:, i % 2], gln, ALU.mult).then_inc(s_vn, 1)
                dve.wait_ge(s_mm, i + 1)
                if i >= 2:
                    dve.wait_ge(sst_[i % 2], 16 * (i // 2))
                ln(tt(sst[:, i % 2], cr.bank[6 + i % 2].rearrange("p (g q) -> p g q", g=4), bs, ALU.add))
                tt(sst[:, i % 2], sst[:, i % 2], uT[:, :, i * P:(i + 1) * P], ALU.mult).then_inc(s_s, 1)


def block_window(cr):
    kT, qT, v_d = cr.dram("ek_T", [P, NTOK]), cr.dram("eq_T", [512, NTOK]), cr.dram("ev_rows", [NTOK, P])
    O = cr.dram("o_rows", [NTOK, D])
    qa, ka = cr.at(10240, 2, NTOK), cr.at(12800, 2, NTOK)
    vb = cr.at(15360, 2, NTC, HD)
    p_buf, t_buf = cr.at(16640, 2, 1024), cr.at(18688, 2, NT, P)
    ob = cr.at(20736, 2, NTC, HD)
    sink = cr.at(22016, HW_)
    g = HW_ // 2

    def loads(k, it):
        return [(qa[0:HD, k], qT[bass.ds((g * k + it) * HD, HD), :])]

    static = [(sink, cr.io["sink"].broadcast_to([P, HW_]))]
    for k in range(2):
        static += [(ka[0:HD, k], kT[k * HD:(k + 1) * HD, :]), (vb[:, k], rows_of(v_d, k * HD, HD, NTC))]
    steps = []
    for k in range(2):
        keys = ka[0:HD, k]
        snk = lambda it, k=k: sink[:, bass.ds(it + g * k, 1)]
        for i in range(NTC):
            pieces, masks, w = [(0, CTX, keys[:, SEQ:NTOK])], [], CTX
            pv = [(0, vb[:, k, NT]), (P, vb[:, k, NT + 1])]
            if i < NT:
                for b in range(max(i - 1, 0), min(i + 1, NT - 1) + 1):
                    if b != i:
                        masks.append((w, C_PREV if b < i else C_CAUSAL))
                    pieces.append((w, w + P, keys[:, b * P:(b + 1) * P]))
                    pv.append((w, vb[:, k, b]))
                    w += P
            steps.append(Step(k, qa[0:HD, k, i * P:(i + 1) * P], pieces, masks, w, pv, snk, ob[:, k, i]))
    attention(cr, "win", g, steps, loads, static,
              lambda k, it: (rows_of(O, (g * k + it) * HD, HD, NTC), ob[:, k]), 2, p_buf, t_buf, False)


def block_eout(cr):
    block_out(cr, "eout", W_EOUT, NTC, 4, None, "s_T", [(MC_L + 16, V_LAT), (MC_L + 16, V_CTX)])


S_IX, S_IXC, S_GT, S_GTC = 500, 516, 532, 548


def block_router(cr, l):
    nc, io = cr.nc, cr.io
    nt = NTC if l == 0 else NT
    ntok = nt * P
    name = f"router{l}"
    x_d, xn_d = cr.dram("x_rows", [NTOK, D]), cr.dram("xn_rows", [NTOK, D])
    x_st, r_in, lg, s_m, s_e, tr, link, tk, ix = cr.sems(name, "x_stored w_loaded logits shifted exp turned dve chosen columns")
    Xr = X(cr)
    hT = cr.at(10240, KT, NTOK)
    o = 22528
    rw = cr.at(o, KT, NE)
    af = cr.at(o + 128, nt, NE)
    mx, sm = cr.at(o + 300, nt), cr.at(o + 320, nt)
    w0, w1 = cr.at(o + 512, NTOK), cr.at(o + 512 + NTOK, NTOK)
    nv = CAP + CAPC
    vals = cr.at(o + 3200, nv)
    idx = cr.at(o + 3400, nv).bitcast(U32)
    idf = cr.at(o + 3600, nv)
    gs, gc = (GS_2L0, GS_2C0) if l == 0 else (GS_2L1, GS_2L1)
    sh = MC_L + 48 * l + 24
    nrm = Norm(cr, name, nt, lambda i: Xr[:, i], [cr.at(20480, D), cr.at(20480 + D, D)],
               [(lambda k, i: hT[:, k, i * P:(i + 1) * P], variant(cr.gain(gs), cr.gain(gc)),
                 variant(cr.shift(sh, V_LAT), cr.shift(sh, V_CTX)))], cr.small[:, 300:340],
               store=lambda i: xn_d[i * P:(i + 1) * P, :])

    with nc.Block() as block:
        @block.sync
        def _(sp):
            sp.dma_start(rw, io["router"][:, l]).then_inc(r_in, 16)
            sp.dma_start(x_d.rearrange("(i p) d -> p i d", p=P)[:, 0:nt], Xr[:, 0:nt]).then_inc(x_st, 16)
            sp.wait_ge(x_st, 16)

        @block.gpsimd
        def _(pool):
            nrm.keep(pool)
            nrm.kept(pool)

        @block.tensor
        def _(pe):
            nrm.pe(pe)
            pe.wait_ge(nrm.ev, 2 * nt)
            pe.wait_ge(r_in, 16)
            for i in range(nt):
                for k in range(KT):
                    last = nc.tensor.matmul(cr.bank[2][:, i * NE:(i + 1) * NE], hT[:, k, i * P:(i + 1) * P], rw[:, k],
                                            start=(k == 0), stop=(k == KT - 1))
            last.then_inc(lg, 1)
            pe.wait_ge(s_m, 2)
            for i in range(nt):
                last = nc.tensor.transpose(cr.bank[3 + i // 4][0:NE, (i % 4) * P:(i % 4 + 1) * P], af[:, i], cr.const(C_ID))
            last.then_inc(tr, 1)
            pe.wait_ge(tk, 1)
            i16 = cr.const(C_ID)[0:NE, 0:NE]
            last = nc.tensor.transpose(cr.bank[6][:, 0:NE], idf[0:NE, 0:CAP], i16)
            last = nc.tensor.transpose(cr.bank[6][:, NE:2 * NE], vals[0:NE, 0:CAP], i16)
            if l == 0:
                last = nc.tensor.transpose(cr.bank[6][0:CAPC, 2 * NE:3 * NE], idf[0:NE, CAP:nv], i16)
                last = nc.tensor.transpose(cr.bank[6][0:CAPC, 3 * NE:4 * NE], vals[0:NE, CAP:nv], i16)
            last.then_inc(ix, 1)

        @block.scalar
        def _(act):
            nrm.act(act)
            act.wait_ge(s_m, 1)
            nc.scalar.activation(af, af, ACT.Exp).then_inc(s_e, 1)

        @block.vector
        def _(dve):
            ln = Link(dve, link)
            tt, ts = nc.vector.tensor_tensor, nc.vector.tensor_scalar
            nrm.dve(dve)
            dve.wait_ge(lg, 1)
            ps = cr.bank[2][:, 0:nt * NE].rearrange("p (i e) -> p i e", e=NE)
            bc = lambda v: v.unsqueeze(2).broadcast_to([P, nt, NE])
            ln(nc.vector.tensor_reduce(mx, ps, AXX, ALU.max))
            tt(af, ps, bc(mx), ALU.subtract).then_inc(s_m, 1)
            dve.wait_ge(s_e, 1)
            ln(nc.vector.tensor_reduce(sm, af, AXX, ALU.add))
            ln(nc.vector.reciprocal(sm, sm))
            tt(af, af, bc(sm), ALU.mult).then_inc(s_m, 1)
            dve.wait_ge(tr, 1)
            for b in range((nt + 3) // 4):
                n = min(4, nt - 4 * b) * P
                ln(nc.vector.tensor_copy(w0[0:NE, b * 512:b * 512 + n], cr.bank[3 + b][0:NE, 0:n]))
            for lo, n, at, cap in ((0, SEQ, 0, CAP), (SEQ, CTX, CAP, CAPC))[:2 - l]:
                a, b = w0[0:NE, lo:lo + n], w1[0:NE, lo:lo + n]
                for r in range(cap // 8):
                    v8, i8 = vals[0:NE, at + 8 * r:at + 8 * r + 8], idx[0:NE, at + 8 * r:at + 8 * r + 8]
                    ln(nc.vector.max(v8, a))
                    ln(nc.vector.max_index(i8, v8, a))
                    ln(nc.vector.match_replace(b, v8, a, -1.0))
                    a, b = b, a
            nn = nv if l == 0 else CAP
            ln(nc.vector.tensor_copy(idf[0:NE, 0:nn], idx[0:NE, 0:nn]))
            if l == 0:
                ln(ts(idf[0:NE, CAP:nv], idf[0:NE, CAP:nv], float(SEQ), None, ALU.add))
            nc.vector.tensor_copy(mx[0:NE, 0:1], idf[0:NE, 0:1]).then_inc(tk, 1)
            dve.wait_ge(ix, 1)
            sm_ = cr.small
            ln(nc.vector.tensor_copy(sm_[:, S_IX:S_IX + NE].bitcast(U32), cr.bank[6][:, 0:NE]))
            ln(nc.vector.tensor_copy(sm_[:, S_GT:S_GT + NE], cr.bank[6][:, NE:2 * NE]))
            if l == 0:
                ln(nc.vector.tensor_copy(sm_[0:CAPC, S_IXC:S_IXC + NE].bitcast(U32), cr.bank[6][0:CAPC, 2 * NE:3 * NE]))
                ln(nc.vector.tensor_copy(sm_[0:CAPC, S_GTC:S_GTC + NE], cr.bank[6][0:CAPC, 3 * NE:4 * NE]))


def block_moe(cr, l):
    nc = cr.nc
    w0 = W_MOE0 if l == 0 else W_MOE1
    name = f"moe{l}"
    n = CAP + CAPC if l == 0 else CAP
    parts = [(0, CAP, V_LAT)] + ([(CAP, n, V_CTX)] if l == 0 else [])
    TY = 2 * len(parts)
    TX = 4
    TB = TY + TX
    GX = 16 * len(parts)
    a_r, a_e, b_r, b_e, t_r, t_e, c_r, c_e, gx, sc = cr.sems(
        name, "a_ready a_taken b_ready b_taken turned placed y_ready y_taken gathered scattered")
    x_d, xn_d = cr.dram("x_rows", [NTOK, D]), cr.dram("xn_rows", [NTOK, D])
    xg, xgc = cr.at(0, D), cr.at(1024, D)
    xT = cr.at(2048, KT, n)
    sa = cr.at(3400, 2, 2, n)
    hid = cr.at(4096, KT, n)
    yT = cr.at(5400, KT, n)
    yr, yrc = cr.at(6700, D), cr.at(7724, D)
    src, dst = (xg, xgc), (yr, yrc)
    rows = (P, CAPC)
    sm = cr.small
    ixs = (sm[:, S_IX:S_IX + NE].bitcast(U32), sm[0:CAPC, S_IXC:S_IXC + NE].bitcast(U32))
    gts = (sm[:, S_GT:S_GT + NE], sm[0:CAPC, S_GTC:S_GTC + NE])
    gcol, scol, mcol = (GS_2L0 if l == 0 else GS_2L1), MC_L + 48 * l + 24, MC_L + 48 * l + 40

    def t_base(e):
        return TX if isinstance(e, int) and e == 0 else TX + TX - TB + TB * e

    TBANK, CBANK = (4, 5), (6, 7)

    def half(bank):
        return cr.bank[bank][:, 0:2 * n].rearrange("p (c n) -> p c n", c=2)

    with nc.Block() as block:
        @block.sync
        def _(sp):
            def refill(e):
                for j, (sem, k) in enumerate(((a_r, 2), (b_r, 2), (a_r, 4), (b_r, 4), (c_r, 2), (c_r, 4))):
                    sp.wait_ge(sem, 4 * e + k)
                    t = w0 + 6 * e + j + RING
                    if isinstance(e, int):
                        cr.load_w(sp, t)
                    else:
                        slot = (w0 + j) % RING
                        sp.dma_start(cr.ring[:, slot, :], cr.io["wstream"][bass.ds(t, 1)].rearrange("a p n -> (a p) n")).then_inc(cr.loaded[slot], 16)
            with sp.Fori(0, NE - 1) as e:
                refill(e)
            refill(NE - 1)

        @block.gpsimd
        def _(pool):
            def gather(e):
                if e:
                    pool.wait_ge(t_r, TX if e == 1 else t_base(e - 1))
                for p in range(len(parts)):
                    pool.indirect_dma_start(out=src[p][0:rows[p], :], out_offset=None, in_=xn_d[:, :],
                                            in_offset=bass.IndirectOffsetOnAxis(ap=ixs[p][0:rows[p], e:e + 1], axis=0)).then_inc(gx, 16)

            def scatter(e):
                pool.wait_ge(t_e, t_base(e + 1) + TY if e + 1 < NE else t_base(NE - 1) + 2 * TY)
                if e:
                    pool.wait_ge(sc, GX * e)
                for p in range(len(parts)):
                    pool.indirect_dma_start(out=x_d[:, :], out_offset=bass.IndirectOffsetOnAxis(ap=ixs[p][0:rows[p], e:e + 1], axis=0),
                                            in_=dst[p][0:rows[p], :], in_offset=None, compute_op=ALU.add).then_inc(sc, 16)

            gather(0)
            gather(1)
            for e in range(NE):
                if e + 2 < NE:
                    gather(e + 2)
                scatter(e)
            pool.wait_ge(sc, GX * NE)

        def turned_units(e, with_y, with_x):
            b = t_base(e)
            ys = [("y", v, b + v) for v in range(TY)] if with_y else []
            xs = [("x", v, b + (TY if with_y else 0) + v) for v in range(TX)] if with_x else []
            return ys, xs

        @block.tensor
        def _(pe):
            def up(e, j, bank0, ready, taken, first):
                slot = (w0 + j) % RING
                pe.wait_ge(cr.loaded[slot], 16 * ((w0 + j) // RING + 1) + 32 * e)
                w = cr.w(slot)
                for v in range(2):
                    k0 = 4 * e + first + v
                    if not (isinstance(e, int) and e == 0 and first + v < 2):
                        pe.wait_ge(taken, k0 - 1)
                    for c in range(2):
                        m = 2 * v + c
                        for k in range(KT):
                            last = nc.tensor.matmul(half(bank0 + v)[:, c], w[:, k, m * P:(m + 1) * P], xT[:, k, :],
                                                    start=(k == 0), stop=(k == KT - 1))
                    last.then_inc(ready, 1)

            def turn(units, e):
                for kind, v, at in units:
                    pe.wait_ge(t_e, at - 1)
                    bank = cr.bank[TBANK[v % 2]]
                    if kind == "y":
                        p, h = v // 2, v % 2
                        if v == 0:
                            pe.wait_ge(c_e, 4 * e)
                        a, b, _ = parts[p]
                        for q in range(4):
                            last = nc.tensor.transpose(bank[0:b - a, q * P:(q + 1) * P], yT[:, 4 * h + q, a:b], cr.const(C_ID))
                    else:
                        if v == 0:
                            pe.wait_ge(gx, GX * (e + 2))
                        for c in range(2):
                            k = 2 * v + c
                            for p, (a, b, _) in enumerate(parts):
                                r = b - a
                                last = nc.tensor.transpose(half(TBANK[v % 2])[:, c, a:b], src[p][0:r, k * P:(k + 1) * P], cr.const(C_ID)[0:r, 0:r])
                    last.then_inc(t_r, 1)

            def down(e):
                pe.wait_ge(b_e, 4 * e + 4)
                for j in (4, 5):
                    slot = (w0 + j) % RING
                    pe.wait_ge(cr.loaded[slot], 16 * ((w0 + j) // RING + 1) + 32 * e)
                    w = cr.w(slot)
                    for v in range(2):
                        at = 4 * e + 2 * (j - 4) + v
                        if not (isinstance(e, int) and e == 0 and j == 4):
                            pe.wait_ge(c_e, at - 1)
                        for c in range(2):
                            m = 2 * v + c
                            for k in range(KT):
                                last = nc.tensor.matmul(half(CBANK[v])[:, c], w[:, k, m * P:(m + 1) * P], hid[:, k, :],
                                                        start=(k == 0), stop=(k == KT - 1))
                        last.then_inc(c_r, 1)

            def body(e, with_y, with_x):
                ys, xs = turned_units(e, with_y, with_x)
                pe.wait_ge(t_e, t_base(e))
                up(e, 0, 0, a_r, a_e, 0)
                turn(ys, e)
                up(e, 1, 2, b_r, b_e, 0)
                up(e, 2, 0, a_r, a_e, 2)
                up(e, 3, 2, b_r, b_e, 2)
                turn(xs, e)
                down(e)

            for v in range(TX):
                if v >= 2:
                    pe.wait_ge(t_e, v - 1)
                if v == 0:
                    pe.wait_ge(gx, GX)
                for c in range(2):
                    for p, (a, b, _) in enumerate(parts):
                        k, r = 2 * v + c, b - a
                        last = nc.tensor.transpose(half(TBANK[v % 2])[:, c, a:b], src[p][0:r, k * P:(k + 1) * P], cr.const(C_ID)[0:r, 0:r])
                last.then_inc(t_r, 1)
            body(0, False, True)
            with pe.Fori(1, NE - 1) as e:
                body(e, True, True)
            body(NE - 1, True, False)
            turn([("y", v, t_base(NE - 1) + TY + v) for v in range(TY)], NE)

        @block.scalar
        def _(act):
            def gates(e, first):
                for v in range(first, first + 2):
                    act.wait_ge(a_r, 4 * e + (v + 1))
                    if not (isinstance(e, int) and e == 0 and v < 2):
                        act.wait_ge(b_e, 4 * e + (v - 1))
                    nc.scalar.activation(sa[:, v % 2], half(v % 2), ACT.Silu).then_inc(a_e, 1)

            def outs(e):
                for v in range(4):
                    act.wait_ge(c_r, 4 * e + (v + 1))
                    if v == 0:
                        act.wait_ge(t_r, t_base(e) + (0 if isinstance(e, int) and e == 0 else TY))
                    for c in range(2):
                        k = 2 * v + c
                        for a, b, var in parts:
                            last = nc.scalar.activation(yT[:, k, a:b], half(CBANK[v % 2])[:, c, a:b], ACT.Copy, scale=cr.shift(mcol, var)(k))
                    last.then_inc(c_e, 1)

            def body(e):
                gates(e, 0)
                gates(e, 2)
                outs(e)

            body(0)
            with act.Fori(1, NE - 1) as e:
                body(e)
            body(NE - 1)

        @block.vector
        def _(dve):
            ts = nc.vector.tensor_scalar

            def place(units, e):
                for kind, v, at in units:
                    dve.wait_ge(t_r, at + 1)
                    bank = cr.bank[TBANK[v % 2]]
                    if kind == "y":
                        p, h = v // 2, v % 2
                        if v == 0 and not (isinstance(e, int) and e == 1):
                            dve.wait_ge(sc, GX * (e - 1))
                        r = rows[p]
                        g = gts[p][0:r, e - 1:e] if isinstance(e, int) else gts[p][0:r, bass.ds(e - 1, 1)]
                        last = ts(dst[p][0:r, h * 512:(h + 1) * 512], bank[0:r, :], g, None, ALU.mult)
                    else:
                        for c in range(2):
                            k = 2 * v + c
                            for a, b, var in parts:
                                gc = gcol + (var == V_CTX)
                                last = ts(xT[:, k, a:b], half(TBANK[v % 2])[:, c, a:b], cr.gain(gc)(k), cr.shift(scol, var)(k), ALU.mult, ALU.add)
                    last.then_inc(t_e, 1)

            def hidden(e, first):
                for v in range(first, first + 2):
                    dve.wait_ge(a_e, 4 * e + (v + 1))
                    dve.wait_ge(b_r, 4 * e + (v + 1))
                    nc.vector.tensor_tensor(hid[:, 2 * v:2 * v + 2], sa[:, v % 2], half(2 + v % 2), ALU.mult).then_inc(b_e, 1)

            def body(e, with_y, with_x):
                ys, xs = turned_units(e, with_y, with_x)
                place(ys, e)
                hidden(e, 0)
                hidden(e, 2)
                place(xs, e)

            place([("x", v, v) for v in range(TX)], 0)
            body(0, False, True)
            body(1, True, True)
            with dve.Fori(2, NE - 1) as e:
                body(e, True, True)
            body(NE - 1, True, False)
            place([("y", v, t_base(NE - 1) + TY + v) for v in range(TY)], NE)


O_RAW, O_RAWQ = 10240, 10240 + NTC * 288


def block_oin(cr):
    nc, io = cr.nc, cr.io
    x_d, c_T = cr.dram("x_rows", [NTOK, D]), cr.dram("c_T", [512, NTOK])
    x_in, t_in, link, s_ss, s_var, s_std, s_rst, s_hh, s_cv, s_pad = cr.sems(
        "oin", "x_loaded tables_loaded dve squares variance std rstd products conv padded")
    c_st = cr.sems("oin", "c_stored0 c_stored1")
    Xr = X(cr)
    raw, rawq = cr.at(O_RAW, NTC, 288), cr.at(O_RAWQ, NT, 384)
    hT = cr.at(16192, KT, NTOK)
    gb, gc = cr.at(28480, 2, SEQ), cr.at(30528, 2, SEQ)
    ub = cr.at(32576, SEQ + 2)
    co = cr.at(33604, 2, SEQ)
    junk = cr.at(35652, 2, 384)
    tab = cr.at(36420, NT, 2, 16)
    hh = cr.at(36676, SEQ)
    st = cr.small[:, 360:440].rearrange("p (n i) -> p n i", n=4)
    tmp = [cr.small[:, 560 + 80 * n:640 + 80 * n] for n in range(4)]
    un = Units(cr, "oin")
    nrm = Norm(cr, "oin", NTC, lambda i: Xr[:, i], [cr.at(26432, D), cr.at(26432 + D, D)],
               [(lambda k, i: hT[:, k, i * P:(i + 1) * P], variant(cr.gain(GS_1L1), cr.gain(GS_1C1)),
                 variant(cr.shift(MC_L + 48, V_LAT), cr.shift(MC_L + 48, V_CTX)))], cr.small[:, 300:340])
    NRW = NTC + NT
    convw = lambda s_, m: cr.cols[:, 15 + 4 * s_ + m:16 + 4 * s_ + m]

    with nc.Block() as block:
        @block.sync
        def _(sp):
            sp.dma_start(Xr, x_d.rearrange("(i p) d -> p i d", p=P)).then_inc(x_in, 16)
            sp.dma_start(tab, io["rope_c"]).then_inc(t_in, 16)
            stream(cr, sp, W_OIN, 5, un, [NTC, NT, 8, 8, 8])

        @block.gpsimd
        def _(pool):
            for m in range(4):
                pool.wait_ge(s_cv, m + 1)
                pool.dma_start(c_T[m * P:(m + 1) * P, 0:SEQ], co[:, m % 2]).then_inc(c_st[m % 2], 16)
            for k in range(2):
                pool.wait_ge(c_st[k], 32)

        @block.tensor
        def _(pe):
            nrm.pe(pe)
            pe.wait_ge(nrm.ev, 2 * NTC)
            for t, n, cnt in ((0, 288, NTC), (1, 384, NT)):
                cr.wait_w(pe, W_OIN + t)
                w = cr.w(W_OIN + t)
                for i in range(cnt):
                    product(cr, pe, un, un.bank(un.n)[:, 0:n], [(hT[:, k, i * P:(i + 1) * P], w[:, k, 0:n]) for k in range(KT)])
            for t in range(2, 5):
                cr.wait_w(pe, W_OIN + t)
                w = cr.w(W_OIN + t)
                for m in range(4):
                    for h in range(2):
                        product(cr, pe, un, un.bank(un.n), [(w[:, k, m * P:(m + 1) * P], hT[:, k, h * 512:(h + 1) * 512]) for k in range(KT)])

        @block.scalar
        def _(act):
            act.wait_ge(x_in, 16)
            nrm.act(act)
            for u in range(NRW):
                q, i = u >= NTC, u % NTC
                n, full = (384, 384) if q else (256, 288)
                act.wait_ge(un.full, u + 1)
                if u >= 2:
                    act.wait_ge(s_ss, u - 1)
                nc.scalar.activation(junk[:, u % 2, 0:n], un.bank(u)[:, 0:n], ACT.Square, accum_out=st[:, 0, u:u + 1]).then_inc(s_ss, 1)
                nc.scalar.activation((rawq if q else raw)[:, i, 0:full], un.bank(u)[:, 0:full], ACT.Copy).then_inc(un.empty, 1)
            act.wait_ge(s_var, 1)
            nc.scalar.activation(st[:, 2, 0:NRW], st[:, 1, 0:NRW], ACT.Sqrt).then_inc(s_std, 1)
            for v in range(24):
                s_, h = v // 2, v % 2
                m, kind = s_ // 3, s_ % 3
                act.wait_ge(un.full, NRW + v + 1)
                if kind == 2 and m:
                    act.wait_ge(s_hh, m)
                if kind == 0 and m >= 2:
                    act.wait_ge(s_cv, m - 1)
                to = (gb[:, m % 2], gc[:, m % 2], hh)[kind]
                nc.scalar.activation(to[:, h * 512:(h + 1) * 512], un.bank(NRW + v), ACT.Copy).then_inc(un.empty, 1)

        @block.vector
        def _(dve):
            ln = Link(dve, link)
            tt, ts, stt = nc.vector.tensor_tensor, nc.vector.tensor_scalar, nc.vector.scalar_tensor_tensor
            nrm.dve(dve)
            dve.wait_ge(s_ss, NRW)
            ts(st[:, 1, 0:NTC], st[:, 0, 0:NTC], 1.0 / 256, EPS, ALU.mult, ALU.add)
            ts(st[:, 1, NTC:NRW], st[:, 0, NTC:NRW], 1.0 / 384, EPS, ALU.mult, ALU.add).then_inc(s_var, 1)
            dve.wait_ge(s_std, 1)
            ln(nc.vector.reciprocal(st[:, 3, 0:NRW], st[:, 2, 0:NRW]))
            dve.wait_ge(un.empty, NRW)
            for i in range(NTC):
                ts(raw[:, i, 0:256], raw[:, i, 0:256], st[:, 3, i:i + 1], None, ALU.mult)
            for i in range(NT):
                ts(rawq[:, i], rawq[:, i], st[:, 3, NTC + i:NTC + i + 1], None, ALU.mult)
            dve.wait_ge(t_in, 16)
            for i0 in range(0, NT, 4):
                k4 = raw[:, i0:i0 + 4, 256:288]
                c, s_ = tab[:, i0:i0 + 4, 0], tab[:, i0:i0 + 4, 1]
                t = [v[:, 0:64].rearrange("p (i d) -> p i d", d=16) for v in tmp]
                tt(t[0], k4[:, :, 0:16], c, ALU.mult)
                tt(t[1], k4[:, :, 16:32], s_, ALU.mult)
                tt(t[2], k4[:, :, 16:32], c, ALU.mult)
                ln(tt(t[3], k4[:, :, 0:16], s_, ALU.mult))
                tt(k4[:, :, 0:16], t[0], t[1], ALU.subtract)
                ln(tt(k4[:, :, 16:32], t[2], t[3], ALU.add))
            nc.vector.memset(ub[:, 0:1], 0.0)
            ln(nc.vector.memset(ub[:, SEQ + 1:SEQ + 2], 0.0))
            for m in range(4):
                dve.wait_ge(un.empty, NRW + 6 * (m + 1))
                tt(ub[:, 1:SEQ + 1], gc[:, m % 2], hh, ALU.mult).then_inc(s_hh, 1)
                dve.wait_ge(s_hh, m + 1)
                if m >= 2:
                    dve.wait_ge(c_st[m % 2], 16 * (m // 2))
                c = co[:, m % 2]
                ln(ts(c, ub[:, 0:SEQ], convw(0, m), None, ALU.mult))
                ln(stt(c, ub[:, 1:SEQ + 1], convw(1, m), c, ALU.mult, ALU.add))
                ln(stt(c, ub[:, 2:SEQ + 2], convw(2, m), c, ALU.mult, ALU.add))
                tt(c, c, gb[:, m % 2], ALU.mult).then_inc(s_cv, 1)
            dve.wait_ge(s_cv, 4)


def block_oup(cr):
    nc, io = cr.nc, cr.io
    qT, kN, kr_d, v_d = (cr.dram(n, s_) for n, s_ in (
        ("oq_T", [HC * QKC, SEQ]), ("ok_T", [512, NTOK]), ("okr_T", [32, NTOK]), ("ov_rows", [NTOK, 512])))
    t_in, link, turned, placed, q_ok, tq, pq, kr_st = cr.sems("oup", "tables_loaded dve turned placed q_rows q_turned q_placed kr_stored")
    st_, qst_ = cr.sems("oup", "stored0 stored1"), cr.sems("oup", "q_stored0 q_stored1")
    raw, rawq = cr.at(O_RAW, NTC, 288), cr.at(O_RAWQ, NT, 384)
    ckvT, cqT = cr.at(16192, 2, NTOK), cr.at(18752, 3, SEQ)
    krT = cr.at(21824, NTOK)
    qrow = cr.at(23104, NT, 768)
    stage, qst = cr.at(29248, 2, 512), cr.at(30272, 2, 512)
    tab = cr.at(31296, NT, 2, 16)
    tmp = [cr.at(31552 + 128 * n, HC, 16) for n in range(4)]
    un = Units(cr, "oup")
    G3 = [(0, 4), (4, 8), (8, 10)]
    turns = [(lambda i, c=c: raw[:, i, c * P:(c + 1) * P], ckvT[:, c], a, b, 10 + c) for c in range(2) for a, b in G3]
    turns += [(lambda i: raw[:, i, 256:288], krT, a, b, None) for a, b in G3]
    turns += [(lambda i, c=c: rawq[:, i, c * P:(c + 1) * P], cqT[:, c], a, b, 12 + c) for c in range(3) for a, b in G3[:2]]
    TOK = [(0, 512), (512, 1024), (1024, NTOK)]
    NQ, NK = 2 * NT, 12

    with nc.Block() as block:
        @block.sync
        def _(sp):
            sp.dma_start(tab, io["rope_c"]).then_inc(t_in, 16)
            stream(cr, sp, W_UQ, 2, un, [NQ, NK + NTC])
            sp.wait_ge(placed, len(turns))
            sp.dma_start(kr_d[:, :], krT[0:32]).then_inc(kr_st, 16)
            for v in range(16):
                h, g = v // 2, v % 2
                sp.wait_ge(pq, v + 1)
                sp.dma_start(qT[h * QKC:(h + 1) * QKC, g * 512:(g + 1) * 512], qst[0:QKC, v % 2]).then_inc(qst_[v % 2], 16)
            sp.wait_ge(kr_st, 16)
            for k in range(2):
                sp.wait_ge(qst_[k], 16 * 8)

        @block.gpsimd
        def _(pool):
            for n in range(NK + NTC):
                pool.wait_ge(un.empty, NQ + n + 1)
                if n < NK:
                    m, (a, b) = n // 3, TOK[n % 3]
                    pool.dma_start(kN[m * P:(m + 1) * P, a:b], stage[:, n % 2, 0:b - a]).then_inc(st_[n % 2], 16)
                else:
                    i = n - NK
                    pool.dma_start(v_d[i * P:(i + 1) * P, :], stage[:, n % 2]).then_inc(st_[n % 2], 16)
            for k in range(2):
                pool.wait_ge(st_[k], 16 * (NK + NTC) // 2)

        @block.tensor
        def _(pe):
            for v, (src, dst, a, b, g) in enumerate(turns):
                if v >= 2:
                    pe.wait_ge(placed, v - 1)
                m = 32 if g is None else P
                for i in range(a, b):
                    last = nc.tensor.transpose(cr.bank[v % 2][0:m, (i - a) * P:(i - a + 1) * P], src(i), cr.const(C_ID))
                last.then_inc(turned, 1)
            pe.wait_ge(placed, len(turns))
            cr.wait_w(pe, W_UQ)
            w = cr.ring[:, W_UQ % RING, 0:3 * 768].rearrange("p (k n) -> p k n", k=3)
            for i in range(NT):
                for c in range(2):
                    product(cr, pe, un, un.bank(un.n)[:, 0:384], [(cqT[:, k, i * P:(i + 1) * P], w[:, k, c * 384:(c + 1) * 384]) for k in range(3)])
            cr.wait_w(pe, W_UKV)
            w = cr.ring[:, W_UKV % RING, 0:2 * 1024].rearrange("p (k n) -> p k n", k=2)
            for m in range(4):
                for a, b in TOK:
                    product(cr, pe, un, un.bank(un.n)[:, 0:b - a], [(w[:, k, m * P:(m + 1) * P], ckvT[:, k, a:b]) for k in range(2)])
            for i in range(NTC):
                product(cr, pe, un, un.bank(un.n), [(ckvT[:, k, i * P:(i + 1) * P], w[:, k, 512:1024]) for k in range(2)])
            pe.wait_ge(q_ok, NT)
            for v in range(16):
                h, g = v // 2, v % 2
                if v >= 2:
                    pe.wait_ge(pq, v - 1)
                for q in range(4):
                    last = nc.tensor.transpose(cr.bank[6 + v % 2][0:QKC, q * P:(q + 1) * P], qrow[:, 4 * g + q, h * QKC:(h + 1) * QKC], cr.const(C_ID))
                last.then_inc(tq, 1)

        @block.scalar
        def _(act):
            for u in range(NQ):
                act.wait_ge(un.full, u + 1)
                nc.scalar.activation(qrow[:, u // 2, (u % 2) * 384:(u % 2 + 1) * 384], un.bank(u)[:, 0:384], ACT.Copy,
                                     scale=QKC ** -0.5).then_inc(un.empty, 1)
            for n in range(NK + NTC):
                act.wait_ge(un.full, NQ + n + 1)
                if n >= 2:
                    act.wait_ge(st_[n % 2], 16 * (n // 2))
                a, b = TOK[n % 3] if n < NK else (0, 512)
                nc.scalar.activation(stage[:, n % 2, 0:b - a], un.bank(NQ + n)[:, 0:b - a], ACT.Copy).then_inc(un.empty, 1)

        @block.vector
        def _(dve):
            ln = Link(dve, link)
            tt, ts = nc.vector.tensor_tensor, nc.vector.tensor_scalar
            for v, (src, dst, a, b, g) in enumerate(turns):
                dve.wait_ge(turned, v + 1)
                m = 32 if g is None else P
                ps = cr.bank[v % 2][0:m, 0:(b - a) * P]
                if g is None:
                    nc.vector.tensor_copy(dst[0:m, a * P:b * P], ps).then_inc(placed, 1)
                else:
                    ts(dst[:, a * P:b * P], ps, cr.cols[:, g:g + 1], None, ALU.mult).then_inc(placed, 1)
            dve.wait_ge(t_in, 16)
            for i in range(NT):
                dve.wait_ge(un.empty, 2 * i + 2)
                q = qrow[:, i].rearrange("p (h w) -> p h w", w=QKC)
                x1, x2 = q[:, :, 64:80], q[:, :, 80:96]
                c, s_ = (tab[:, i, n].unsqueeze(1).broadcast_to([P, HC, 16]) for n in range(2))
                tt(tmp[0], x1, c, ALU.mult)
                tt(tmp[1], x2, s_, ALU.mult)
                tt(tmp[2], x2, c, ALU.mult)
                ln(tt(tmp[3], x1, s_, ALU.mult))
                ln(tt(x1, tmp[0], tmp[1], ALU.subtract))
                tt(x2, tmp[2], tmp[3], ALU.add).then_inc(q_ok, 1)
                dve.wait_ge(q_ok, i + 1)
            for v in range(16):
                dve.wait_ge(tq, v + 1)
                if v >= 2:
                    dve.wait_ge(qst_[v % 2], 16 * (v // 2))
                nc.vector.tensor_copy(qst[0:QKC, v % 2], cr.bank[6 + v % 2][0:QKC, :]).then_inc(pq, 1)


def block_mla(cr):
    qT, kN, kr_d, v_d = (cr.dram(n, s_) for n, s_ in (
        ("oq_T", [HC * QKC, SEQ]), ("ok_T", [512, NTOK]), ("okr_T", [32, NTOK]), ("ov_rows", [NTOK, 512])))
    O = cr.dram("o_rows", [NTOK, D])
    qa, ka = cr.at(10240, 2, SEQ), cr.at(12288, 2, NTOK)
    vb = cr.at(14848, 2, NTC, HD)
    p_buf, t_buf = cr.at(16128, 2, NTOK), cr.at(18688, 2, NTC, P)
    ob = cr.at(21248, 2, NT, HD)

    def loads(k, it):
        h = 2 * it + k
        return [(qa[0:QKC, k], qT[bass.ds(h * QKC, QKC), :]), (ka[0:HD, k], kN[bass.ds(h * HD, HD), :]),
                (vb[:, k], rows_of(v_d, h * HD, HD, NTC))]

    steps = [Step(k, qa[0:QKC, k, i * P:(i + 1) * P],
                  [(a, min(a + 512, NTOK), ka[0:QKC, k, a:min(a + 512, NTOK)]) for a in range(0, NTOK, 512)], [], NTOK,
                  [(n * P, vb[:, k, n]) for n in range(NTC)], None, ob[:, k, i]) for k in range(2) for i in range(NT)]
    attention(cr, "mla", HC // 2, steps, loads, [(ka[HD:QKC, k], kr_d[:, :]) for k in range(2)],
              lambda k, it: (rows_of(O, (2 * it + k) * HD, HD, NT), ob[:, k]), 3, p_buf, t_buf, True)


def block_oout(cr):
    block_out(cr, "oout", W_OOUT, NT, 4, None, "c_T", [(MC_L + 64, V_LAT)])


def block_final(cr):
    nc, io = cr.nc, cr.io
    x_d = cr.dram("x_rows", [NTOK, D])
    x_in, g_in, ss, var, std, rst, sc, done, st = cr.sems("final", "x_loaded g_loaded squares variance std rstd scaled done stored")
    Xr = X(cr)
    fg = cr.at(10240, D)
    junk = cr.at(11264, 2, D)
    s_ = cr.small[:, 300:332].rearrange("p (n i) -> p n i", n=4)
    out = cr.out.rearrange("b (i p) d -> (b p) i d", p=P)

    with nc.Block() as block:
        @block.sync
        def _(sp):
            sp.dma_start(fg, io["final_g"].broadcast_to([P, D])).then_inc(g_in, 16)
            sp.dma_start(Xr[:, 0:NT], x_d.rearrange("(i p) d -> p i d", p=P)[:, 0:NT]).then_inc(x_in, 16)
            for i in range(NT):
                sp.wait_ge(done, i + 1)
                sp.dma_start(out[:, i], Xr[:, i]).then_inc(st, 16)
            sp.wait_ge(st, 16 * NT)

        @block.scalar
        def _(act):
            act.wait_ge(x_in, 16)
            for i in range(NT):
                if i >= 2:
                    act.wait_ge(ss, i - 1)
                nc.scalar.activation(junk[:, i % 2], Xr[:, i], ACT.Square, accum_out=s_[:, 0, i:i + 1]).then_inc(ss, 1)
            act.wait_ge(var, 1)
            nc.scalar.activation(s_[:, 2], s_[:, 1], ACT.Sqrt).then_inc(std, 1)

        @block.vector
        def _(dve):
            dve.wait_ge(ss, NT)
            nc.vector.tensor_scalar(s_[:, 1], s_[:, 0], 1.0 / D, EPS, ALU.mult, ALU.add).then_inc(var, 1)
            dve.wait_ge(std, 1)
            nc.vector.reciprocal(s_[:, 3], s_[:, 2]).then_inc(rst, 1)
            dve.wait_ge(rst, 1)
            dve.wait_ge(g_in, 16)
            for i in range(NT):
                nc.vector.scalar_tensor_tensor(Xr[:, i], Xr[:, i], s_[:, 3, i:i + 1], fg, ALU.mult, ALU.mult).then_inc(done, 1)


BLOCKS = [block_mods_and_tables, block_a_in, block_ssm, block_a_out, block_kv, block_bq, block_fox, block_bout,
          block_ein, block_window, block_eout, lambda cr: block_router(cr, 0), lambda cr: block_moe(cr, 0),
          block_oin, block_oup, block_mla, block_oout, lambda cr: block_router(cr, 1), lambda cr: block_moe(cr, 1), block_final]


def program(nc, io, out, debug=None):
    with ExitStack() as ctx:
        cr = Core(nc, ctx, io)
        cr.out = out
        for b in BLOCKS:
            b(cr)
            cr.end_block()
        if debug:
            debug(cr)


def _tiles(w, cols=512):
    K, N = w.shape
    out = []
    for c in range(0, N, cols):
        part = w[:, c:c + cols]
        if part.shape[1] < cols:
            part = np.concatenate([part, np.zeros((K, cols - part.shape[1]), np.float32)], 1)
        out.append(part.reshape(K // P, P, cols).transpose(1, 0, 2).reshape(P, -1))
    return out


def _cols(v):
    return np.ascontiguousarray(v.reshape(-1, P).T)


def lay_out(i):
    i = {k: np.asarray(v) for k, v in i.items()}
    t = []
    for m in (i["a_mod_w"][0], i["kv_mod_w"], i["b_mod_w"][0], i["mod_w_2"][0], i["mod_w_2"][1]):
        t += _tiles(m)
    t += _tiles(i["a_w_in"][0]) + _tiles(i["a_w_glu"][0]) + _tiles(i["a_w_out"][0])
    t += _tiles(i["kv_w"][:, :2 * D]) + _tiles(i["b_w_in"][0]) + _tiles(i["b_w_out"][0])
    e = i["ev_w_in_2"][0]
    t += _tiles(e[:, 0:256]) + _tiles(e[:, 256:1792]) + _tiles(i["ev_w_out_2"][0])

    def moe(l):
        for n in range(NE):
            w1, w3, w2 = (_tiles(i[f"exp_{w}_2"][l, n]) for w in ("w1", "w3", "w2"))
            t.extend([w1[0], w3[0], w1[1], w3[1], w2[0], w2[1]])
    moe(0)
    o = i["od_w_in_2"][0]
    t += _tiles(o[:, 0:288]) + _tiles(o[:, 288:672])
    g = [o[:, 672 + 512 * s:672 + 512 * (s + 1)] for s in range(3)]
    t += _tiles(np.concatenate([g[s][:, m * P:(m + 1) * P] for m in range(4) for s in range(3)], 1))
    pad = lambda v: np.concatenate([v, np.zeros((P, TILE - v.shape[1]), np.float32)], 1)
    uq = i["od_w_uq_2"][0]
    t.append(pad(uq.reshape(3, P, 768).transpose(1, 0, 2).reshape(P, -1)))
    kv = i["od_w_ukv_2"][0].reshape(256, HC, 2, HD).transpose(0, 2, 1, 3).reshape(2, P, 1024)
    t.append(pad(kv.transpose(1, 0, 2).reshape(P, -1)))
    t += _tiles(i["od_w_out_2"][0])
    moe(1)
    assert len(t) == N_TILES
    a = {"wstream": np.stack(t)}
    a["x"] = i["x"]
    a["ctx"] = i["ctx_2"]
    a["ccols"] = np.ascontiguousarray(np.stack([_cols(i["c"][0]), _cols(i["c_2"][0]), _cols(i["c_ctx_2"])], 2))
    a["modb"] = np.ascontiguousarray(np.concatenate(
        [_cols(v) for v in (i["a_mod_b"][0], i["kv_mod_b"], i["b_mod_b"][0], i["mod_b_2"][0], i["mod_b_2"][1])], 1))
    a["gains"] = np.ascontiguousarray(np.stack([_cols(v) for v in (
        i["a_norm_g"][0], i["kv_norm_g"], i["b_norm_g"][0], i["norm1_g_2"][0], i["norm1_g_2"][1],
        i["norm2_g_2"][0], i["norm2_g_2"][1])], 1))
    two = lambda v: np.concatenate([v, v]).reshape(P, 1)
    a["cols"] = np.ascontiguousarray(np.concatenate(
        [_cols(i["a_b_glu"][0]), two(i["k_norm_g"]), two(i["q_norm_g"][0]), _cols(i["od_kv_norm_g_2"][0]),
         _cols(i["od_q_norm_g_2"][0])] + [_cols(i["od_conv_w_2"][0, s]) for s in range(3)]
        + [np.zeros((P, 40 - 27), np.float32)], 1))
    pair = lambda v: np.ascontiguousarray(v.reshape(NPAIR, 2, STATE, -1).transpose(1, 2, 0, 3).reshape(P, NPAIR, -1))
    a["a_re"], a["a_im"] = (pair(i[k][0])[:, :, 0] for k in ("a_A_re", "a_A_im"))
    a["a_ldt"] = pair(np.repeat(i["a_log_dt"][0], STATE))[:, :, 0]
    a["b_re"], a["b_im"] = (pair(i[k][0]) for k in ("a_B_re", "a_B_im"))
    a["c_re"], a["c_im"] = (pair(i[k][0].transpose(0, 2, 1)) for k in ("a_C_re", "a_C_im"))
    a["d_cols"] = np.ascontiguousarray(i["a_D"][0].reshape(GROUPS, GRP).T)
    a["f_w"] = np.ascontiguousarray(i["kv_w"][:, 2 * D:].reshape(KT, P, HB).transpose(1, 0, 2))
    a["f_b"] = i["kv_f_bias"].reshape(1, HB)
    a["router"] = np.ascontiguousarray(i["router_w_2"].reshape(2, KT, P, NE).transpose(2, 0, 1, 3))
    a["sink"] = i["ev_sink_2"].reshape(1, HW_)
    a["sgu_w"] = np.ascontiguousarray(i["ev_sgu_w_2"][0].transpose(2, 0, 1))
    a["sgu_b"] = i["ev_sgu_b_2"].reshape(1, 4 * P)
    a["sgu_g"] = i["ev_sgu_norm_g_2"].reshape(1, 512)
    a["final_g"] = i["final_g_2"].reshape(1, D)
    a.update(shape_constants())
    return {k: np.ascontiguousarray(v) for k, v in a.items()}


def shape_constants():
    q, k = np.meshgrid(np.arange(P), np.arange(P), indexing="ij")
    consts = np.stack([np.eye(P), np.ones((P, P)), q <= k, np.where(k <= q, 0.0, NEG), np.where(k >= q, 0.0, NEG)], 1)
    a = {"consts": consts.astype(np.float32), "zeros": np.zeros((GRP, GROUPS, P), np.float32),
         "ones": np.ones((1, NTOK), np.float32)}
    for name, rot in (("rope_a", 64), ("rope_c", 32)):
        n = rot // 4
        inv = (np.float32(10000.0) ** (-np.arange(n, dtype=np.float32) / n)).astype(np.float32)
        pos = np.arange(SEQ)
        row, col = (pos // 64).astype(np.float32), (pos % 64).astype(np.float32)
        ang = np.concatenate([row[:, None] * inv, col[:, None] * inv], 1).astype(np.float32)
        t = np.stack([np.cos(ang), np.sin(ang)], 1).astype(np.float32)
        a[name] = np.ascontiguousarray(t.reshape(NT, P, 2, rot // 2).transpose(1, 0, 2, 3))
    return a


def kernel(**inputs):
    import concourse.bacc as bacc
    from concourse.bass_utils import run_bass_kernel_spmd

    nc = bacc.Bacc("TRN2", target_bir_lowering=False, num_devices=1)
    arrays = lay_out(inputs)
    io = {k: nc.dram_tensor(f"in_{k}", v.shape, F32, kind="ExternalInput").ap() for k, v in arrays.items()}
    out = nc.dram_tensor("out", (1, SEQ, D), F32, kind="ExternalOutput").ap()
    program(nc, io, out)
    r = run_bass_kernel_spmd(nc, [{f"in_{k}": v for k, v in arrays.items()}], core_ids=[0])
    return r.results[0]["out"]
```

```python
import math
import numpy as np
import concourse.bass as bass
from concourse import mybir
from contextlib import ExitStack

F32 = mybir.dt.float32
U32 = mybir.dt.uint32
I32 = mybir.dt.int32
ACT = mybir.ActivationFunctionType
ALU = mybir.AluOpType
AXX = mybir.AxisListType.X

P = 128
D = 1024
SEQ = 1024
KT = D // P
NT = SEQ // P
CTX = 256
NTC = NT + CTX // P
NTOK = SEQ + CTX
EPS = 1e-6
NEG = -1e30
GROUPS, STATE, GRP = 64, 64, 16
T_CH = 8
NCH = SEQ // T_CH
NPAIR = GROUPS // 2
SEG_L = 8
N_SEG = NCH // SEG_L
HD = 64
HB = 16
HW_ = 8
HC = 8
QKC = 96
NE = 16
CAP = 2 * SEQ // NE
CAPC = 2 * CTX // NE
RING = 3
TILE = KT * 512
N_MOD = 40
W_MOD = 0
W_AIN = W_MOD + N_MOD
W_GLU = W_AIN + 4
W_AOUT = W_GLU + 2
W_KV = W_AOUT + 2
W_BIN = W_KV + 4
W_BOUT = W_BIN + 4
W_EIN = W_BOUT + 2
W_EOUT = W_EIN + 4
W_MOE0 = W_EOUT + 2
W_OIN = W_MOE0 + 6 * NE
W_UQ = W_OIN + 5
W_UKV = W_UQ + 1
W_OOUT = W_UKV + 1
W_MOE1 = W_OOUT + 2
N_TILES = W_MOE1 + 6 * NE
MC_A, MC_KV, MC_B, MC_L = 0, 24, 40, 64
V_C, V_LAT, V_CTX = 0, 1, 2
C_ID, C_ONE, C_TRI, C_CAUSAL, C_PREV = range(5)
GS_A, GS_KV, GS_B, GS_1L0, GS_1C0, GS_2L0, GS_2C0, GS_1L1, GS_1C1, GS_2L1 = range(10)


class Link:

    def __init__(self, eng, sem):
        self.eng, self.sem, self.n = eng, sem, 0

    def __call__(self, ins):
        self.n = self.n + 1
        ins.then_inc(self.sem, 1)
        self.eng.wait_ge(self.sem, self.n)


class Core:

    def __init__(self, nc, ctx, io):
        self.nc, self.io = nc, io

        def sb(name, shape, dt=F32):
            return ctx.enter_context(nc.sbuf_tensor(name, shape, dt))

        self.ring = sb("w_ring", [P, RING, TILE])
        self.arena = sb("arena", [P, 38400])
        self.consts = sb("consts", [P, 5, P])
        self.modcol = sb("modcol", [P, 160, 3])
        self.gs = sb("gs", [P, 10, KT])
        self.gains = sb("gains", [P, 7, KT])
        self.cols = sb("cols", [P, 40])
        self.small = sb("small", [P, 900])
        self.psum = ctx.enter_context(nc.psum_tensor("psum", [P, 8, 512], F32))
        self.bank = [self.psum[:, i, :] for i in range(8)]
        self.loaded = [ctx.enter_context(nc.semaphore(f"w_loaded{i}")) for i in range(RING)]
        self.ctx = ctx
        self.scratch = {}
        self.of_block = []

    def score_view(self, n, nb):
        return self.psum[:, n * nb:(n + 1) * nb, :].rearrange("p b c -> p (b c)")

    def dram(self, name, shape):
        if name not in self.scratch:
            self.scratch[name] = self.nc.dram_tensor(name, shape, F32).ap()
        return self.scratch[name]

    def at(self, off, *shape):
        n = int(np.prod(shape))
        assert off + n <= 38400, (off, shape)
        v = self.arena[:, off:off + n]
        if len(shape) == 1:
            return v
        names = [f"a{i}" for i in range(len(shape))]
        return v.rearrange(f"p ({' '.join(names)}) -> p {' '.join(names)}",
                           **{a: s for a, s in zip(names[1:], shape[1:])})

    def const(self, i):
        return self.consts[:, i, :]

    def sems(self, prefix, names):
        new = [self.nc.alloc_semaphore(f"{prefix}_{n}") for n in names.split()]
        self.of_block += new
        return new

    def end_block(self):
        self.nc.clear_and_free_semaphores(self.of_block)
        self.nc.all_engine_barrier(sem_only=True)
        self.of_block = []

    def load_w(self, sp, n):
        if n < N_TILES:
            sp.dma_start(self.ring[:, n % RING, :], self.io["wstream"][n]).then_inc(self.loaded[n % RING], 16)

    def wait_w(self, pe, n):
        pe.wait_ge(self.loaded[n % RING], 16 * (n // RING + 1))

    def w(self, n, kt=KT):
        v = self.ring[:, n % RING, :]
        return v.rearrange("p (k n) -> p k n", k=kt)

    def shift(self, col, variant):
        return lambda k: self.modcol[:, col + k, variant:variant + 1]

    def gain(self, g):
        return lambda k: self.gs[:, g, k:k + 1]


A_V, A_S, A_U, A_Y, A_M = 0, 9216, 17472, 26624, 34816
SCOL = NCH + 1
S_A8R, S_A8I = 0, 32


def block_mods_and_tables(cr):
    nc, io = cr.nc, cr.io
    s_c, s_cs, s_row, s_tr, s_used, s_dve, s_in, s_e, s_ed, s_v, s_g, s_kmm, s_kst, s_kd0, s_kd1, s_gt, s_gte, s_zd = cr.sems(
        "mod", "c_loaded silu_done row_copied transposed tile_used dve in_loaded act dve_for_act v_done g_done k_mm k_staged k_stored0 k_stored1 g_transposed g_copied zeros_stored")
    craw = cr.small[:, 300:324].rearrange("p (k v) -> p k v", v=3)
    cs = cr.small[:, 324:348].rearrange("p (k v) -> p k v", v=3)
    mrow = cr.at(A_M, 3, 512)
    modb = cr.small[:, 348:508]
    V = [cr.at(A_V + r * 4608, NPAIR, 9, GRP) for r in range(2)]
    G = cr.at(A_S, NPAIR, 2, T_CH, GRP)
    WT = cr.at(A_Y, NPAIR, 2, P)
    tmp9 = cr.at(A_U, NPAIR, 9, GRP)
    o = A_U + 4608
    tabs = cr.at(o, 6, NPAIR, GRP)
    c_r, c_i, b_r, b_i, bb_r, bb_i = [tabs[:, i] for i in range(6)]
    Dd = cr.at(o + 3072, NPAIR, GRP)
    vec = cr.at(A_M + 1536, 16, NPAIR)
    kst = cr.at(A_M + 1536 + 512, 2, 4, P)
    bd = cr.at(A_U + 2560, 2, NPAIR, 2, GRP)
    pw = cr.small[:, 508:508 + 288].rearrange("p (j t) -> p j t", t=9)
    pwi_ = cr.at(o + 4096, NPAIR, 9)
    dcol = cr.small[:, 796:796 + NPAIR]
    are, aim, ldt, dt, th, mag, kk, r_, sn, cn, den, nr, cfr, cfi, q1, q2 = [vec[:, i] for i in range(16)]
    psM = cr.bank[3]
    s_kd = (s_kd0, s_kd1)
    N_IN = 12

    with nc.Block() as block:
        @block.sync
        def _(sp):
            for n in range(RING):
                cr.load_w(sp, n)
            with sp.Fori(1, N_MOD // RING) as i:
                for s in range(RING):
                    sp.wait_ge(s_used, RING * i + s - 2)
                    sp.dma_start(cr.ring[:, s, :], io["wstream"][bass.ds(RING * i + s, 1)].rearrange(
                        "a p n -> (a p) n")).then_inc(cr.loaded[s], 16)
            for n in range(N_MOD // RING * RING, N_MOD + RING):
                sp.wait_ge(s_used, n - 2)
                cr.load_w(sp, n)
            Kd = cr.dram("k_lags", [GRP, GROUPS, 2 * P])
            for b in range(8):
                sp.wait_ge(s_kst, b + 1)
                for h in range(2):
                    sp.dma_start(Kd[:, 8 * b + h:8 * b + h + 7:2, P:2 * P], kst[GRP * h:GRP * (h + 1), b % 2]).then_inc(s_kd[b % 2], 16)
            for k in range(2):
                sp.wait_ge(s_kd[k], 32 * 4)

        @block.gpsimd
        def _(pool):
            Kd = cr.dram("k_lags", [GRP, GROUPS, 2 * P])
            pool.dma_start(Kd[:, :, 0:P], io["zeros"][:, :, :]).then_inc(s_zd, 16)
            pool.wait_ge(s_zd, 16)

        @block.tensor
        def _(pe):
            pe.wait_ge(s_e, 1)

            def matvec(n, s, first):
                pe.wait_ge(cr.loaded[s], 16 * first + 16)
                if not (isinstance(n, int) and n < 3):
                    pe.wait_ge(s_row, n - 2)
                for k in range(KT):
                    last = nc.tensor.matmul(cr.bank[s][0:3, :], cs[:, k, :], cr.w(s)[:, k, :],
                                            start=(k == 0), stop=(k == KT - 1))
                last.then_inc(s_used, 1)

            def to_columns(n, s):
                pe.wait_ge(s_row, n + 1)
                for j in range(4):
                    last = nc.tensor.matmul(psM[:, bass.ds(12 * n + 3 * j, 3)], mrow[0:3, s, j * P:(j + 1) * P],
                                            cr.const(C_ID)[0:3, 0:3], start=True, stop=True)
                last.then_inc(s_tr, 1)

            for n in range(RING):
                matvec(n, n, 0)
                if n == 1:
                    pe.wait_ge(s_cs, 1)
                if n:
                    to_columns(n - 1, n - 1)
            with pe.Fori(1, N_MOD // RING) as i:
                for s in range(RING):
                    matvec(RING * i + s, s, i)
                    to_columns(RING * i + s - 1, (s - 1) % RING)
            n = N_MOD - 1
            matvec(n, n % RING, n // RING)
            to_columns(n - 1, (n - 1) % RING)
            to_columns(n, n % RING)
            pe.wait_ge(s_v, 1)
            pe.wait_ge(s_g, 1)
            for j in range(NPAIR):
                b, q = j // 4, j % 4
                if q == 0 and b >= 2:
                    pe.wait_ge(s_kst, b - 1)
                for r in range(2):
                    last = nc.tensor.matmul(cr.bank[4 + b % 2][0:2 * GRP, q * P:(q + 1) * P],
                                            bd[:, r, j].rearrange("p h c -> p (h c)"),
                                            V[r][:, j, 0:8, :].rearrange("p t c -> p (t c)"), start=(r == 0), stop=(r == 1))
                if q == 3:
                    last.then_inc(s_kmm, 1)
            for j in range(NPAIR):
                if j == 0:
                    pe.wait_ge(s_row, N_MOD)
                if j >= 2:
                    pe.wait_ge(s_gte, j - 1)
                for r in range(2):
                    last = nc.tensor.transpose(cr.bank[j % 2][:, r * P:(r + 1) * P],
                                               G[:, j, r].rearrange("p t c -> p (t c)"), cr.const(C_ID))
                last.then_inc(s_gt, 1)

        @block.scalar
        def _(act):
            act.dma_start(craw, io["ccols"]).then_inc(s_c, 16)
            for dst, src in ((cr.consts[:, :, :], "consts"), (cr.gains[:, :, :], "gains"), (cr.cols[:, :], "cols"), (modb, "modb"),
                             (are, "a_re"), (aim, "a_im"), (ldt, "a_ldt"), (c_r, "c_re"), (c_i, "c_im"),
                             (b_r, "b_re"), (b_i, "b_im")):
                act.dma_start(dst, io[src]).then_inc(s_in, 16)
            act.dma_start(dcol[0:2 * GRP, :], io["d_cols"]).then_inc(s_in, 16)
            act.wait_ge(s_c, 16)
            nc.scalar.activation(cs, craw, ACT.Silu).then_inc(s_e, 1)
            act.wait_ge(s_in, 16 * N_IN)
            act.wait_ge(s_e, 1)
            nc.scalar.activation(craw, cs, ACT.Copy).then_inc(s_cs, 1)
            nc.scalar.activation(dt, ldt, ACT.Exp).then_inc(s_e, 1)
            act.wait_ge(s_ed, 1)
            nc.scalar.activation(mag, q1, ACT.Exp).then_inc(s_e, 1)
            act.wait_ge(s_ed, 2)
            nc.scalar.activation(sn, r_, ACT.Sin).then_inc(s_e, 1)
            nc.scalar.activation(cn, q2, ACT.Sin).then_inc(s_e, 1)

            def row(n, s):
                act.wait_ge(s_used, n + 1)
                if not (isinstance(n, int) and n < 3):
                    act.wait_ge(s_tr, n - 2)
                nc.scalar.activation(mrow[0:3, s, :], cr.bank[s][0:3, :], ACT.Copy).then_inc(s_row, 1)

            for n in range(RING):
                row(n, n)
            with act.Fori(1, N_MOD // RING) as i:
                for s in range(RING):
                    row(RING * i + s, s)
            row(N_MOD - 1, (N_MOD - 1) % RING)
            for j in range(NPAIR):
                act.wait_ge(s_gt, j + 1)
                nc.scalar.activation(WT[:, j], cr.bank[j % 2][:, 0:2 * P].rearrange("p (r n) -> p r n", r=2),
                                     ACT.Copy).then_inc(s_gte, 1)

        @block.vector
        def _(dve):
            ln = Link(dve, s_dve)
            tt, ts = nc.vector.tensor_tensor, nc.vector.tensor_scalar
            stt = nc.vector.scalar_tensor_tensor
            dve.wait_ge(s_in, 16 * N_IN)
            dve.wait_ge(s_e, 2)
            tt(q1, are, dt, ALU.mult).then_inc(s_ed, 1)
            ln(tt(th, aim, dt, ALU.mult))
            ln(ts(kk, th, 1.0 / (2 * math.pi), None, ALU.mult))
            ln(ts(kk, kk, 12582912.0, -12582912.0, ALU.add, ALU.add))
            c1 = 6.28125
            c2 = 0.00193500518798828125
            c3 = 2 * math.pi - c1 - c2
            ln(stt(r_, kk, -c1, th, ALU.mult, ALU.add))
            ln(stt(r_, kk, -c2, r_, ALU.mult, ALU.add))
            ln(stt(r_, kk, -c3, r_, ALU.mult, ALU.add))
            pi = 3.1415925
            ln(ts(r_, r_, pi, -pi, ALU.min, ALU.max))
            ln(ts(q2, r_, -1.0, None, ALU.mult))
            ln(tt(q2, q2, r_, ALU.max))
            ts(q2, q2, -1.0, math.pi / 2, ALU.mult, ALU.add).then_inc(s_ed, 1)
            ln(tt(den, are, are, ALU.mult))
            ln(tt(nr, aim, aim, ALU.mult))
            ln(tt(den, den, nr, ALU.add))
            ln(nc.vector.reciprocal(den, den))
            dve.wait_ge(s_e, 5)
            ar, ai = pw[:, :, 1], pwi_[:, :, 1]
            ln(nc.vector.memset(pw[:, :, 0], 1.0))
            ln(nc.vector.memset(pwi_[:, :, 0], 0.0))
            ln(tt(ar, mag, cn, ALU.mult))
            ln(tt(ai, mag, sn, ALU.mult))
            ln(ts(nr, ar, -1.0, None, ALU.add))
            ln(tt(cfr, nr, are, ALU.mult))
            ln(tt(q1, ai, aim, ALU.mult))
            ln(tt(cfr, cfr, q1, ALU.add))
            ln(tt(cfr, cfr, den, ALU.mult))
            ln(tt(cfi, ai, are, ALU.mult))
            ln(tt(q1, nr, aim, ALU.mult))
            ln(tt(cfi, cfi, q1, ALU.subtract))
            ln(tt(cfi, cfi, den, ALU.mult))
            bc = lambda v: v.unsqueeze(2).broadcast_to([P, NPAIR, GRP])
            t16 = tmp9[:, :, 0, :]
            ln(tt(bb_r, b_r, bc(cfr), ALU.mult))
            ln(tt(t16, b_i, bc(cfi), ALU.mult))
            ln(tt(bb_r, bb_r, t16, ALU.subtract))
            ln(tt(bb_i, b_i, bc(cfr), ALU.mult))
            ln(tt(t16, b_r, bc(cfi), ALU.mult))
            ln(tt(bb_i, bb_i, t16, ALU.add))
            for t in range(2, 9):
                pr, pi_ = pw[:, :, t - 1], pwi_[:, :, t - 1]
                ln(tt(q1, pr, ar, ALU.mult))
                ln(tt(q2, pi_, ai, ALU.mult))
                ln(tt(pw[:, :, t], q1, q2, ALU.subtract))
                ln(tt(q1, pr, ai, ALU.mult))
                ln(tt(q2, pi_, ar, ALU.mult))
                ln(tt(pwi_[:, :, t], q1, q2, ALU.add))
            ln(nc.vector.tensor_copy(cr.small[:, S_A8R:S_A8R + 32], pw[:, :, 8]))
            ln(nc.vector.tensor_copy(cr.small[:, S_A8I:S_A8I + 32], pwi_[:, :, 8]))
            S9 = [P, NPAIR, 9, GRP]
            cb = lambda v: v.unsqueeze(2).broadcast_to(S9)
            pb = lambda v: v.unsqueeze(3).broadcast_to(S9)
            flat = lambda v: v.rearrange("p j t c -> p (j t c)")
            ln(tt(V[0], cb(c_r), pb(pw), ALU.mult))
            ln(tt(tmp9, cb(c_i), pb(pwi_), ALU.mult))
            ln(tt(flat(V[0]), flat(V[0]), flat(tmp9), ALU.subtract))
            ln(tt(V[1], cb(c_r), pb(pwi_), ALU.mult))
            ln(tt(tmp9, cb(c_i), pb(pw), ALU.mult))
            stt(flat(V[1]), flat(V[1]), -1.0, flat(tmp9), ALU.mult, ALU.subtract).then_inc(s_v, 1)
            dve.wait_ge(s_v, 1)
            t16 = tmp9[:, :, 0, :]
            for t in range(T_CH):
                pr, pi_ = bc(pw[:, :, 7 - t]), bc(pwi_[:, :, 7 - t])
                ln(tt(G[:, :, 0, t, :], bb_r, pr, ALU.mult))
                ln(tt(t16, bb_i, pi_, ALU.mult))
                ln(tt(G[:, :, 0, t, :], G[:, :, 0, t, :], t16, ALU.subtract))
                ln(tt(G[:, :, 1, t, :], bb_i, pr, ALU.mult))
                ln(tt(t16, bb_r, pi_, ALU.mult))
                ln(tt(G[:, :, 1, t, :], G[:, :, 1, t, :], t16, ALU.add))
            ln(nc.vector.memset(bd, 0.0))
            for r, bb in enumerate((bb_r, bb_i)):
                for h in range(2):
                    ln(nc.vector.tensor_copy(bd[64 * h:64 * h + 64, r, :, h, :], bb[64 * h:64 * h + 64]))
            two = 2 * GRP
            ln(tt(t16[0:two, 0], cr.const(C_ID)[0:two, 0:GRP], cr.const(C_ID)[0:two, GRP:two], ALU.add))
            i16 = t16[0:two, 0].unsqueeze(1).broadcast_to([two, NPAIR, GRP])
            d16 = dcol[0:two, :].unsqueeze(2).broadcast_to([two, NPAIR, GRP])
            tt(Dd[0:two], i16, d16, ALU.mult).then_inc(s_g, 1)
            dve.wait_ge(s_tr, N_MOD)
            ln(tt(cr.modcol[:, :, :], psM[:, 0:480].rearrange("p (m v) -> p m v", v=3),
                  modb.unsqueeze(2).broadcast_to([P, 160, 3]), ALU.add))
            for g, (gain, col, var) in enumerate((
                    (0, MC_A + 8, V_C), (1, MC_KV + 8, V_C), (2, MC_B + 8, V_C),
                    (3, MC_L + 8, V_LAT), (3, MC_L + 8, V_CTX), (5, MC_L + 32, V_LAT), (5, MC_L + 32, V_CTX),
                    (4, MC_L + 56, V_LAT), (4, MC_L + 56, V_CTX), (6, MC_L + 80, V_LAT))):
                ln(stt(cr.gs[:, g, :], cr.modcol[:, col:col + 8, var], 1.0, cr.gains[:, gain, :], ALU.add, ALU.mult))
            dve.wait_ge(s_g, 1)
            for b in range(8):
                dve.wait_ge(s_kmm, b + 1)
                if b >= 2:
                    dve.wait_ge(s_kd[b % 2], 32 * (b // 2))
                ps = cr.bank[4 + b % 2][0:two, :].rearrange("p (g n) -> p g n", g=4)
                st = kst[0:two, b % 2]
                nc.vector.tensor_copy(st[:, :, GRP:P], ps[:, :, GRP:P])
                last = tt(st[:, :, 0:GRP], ps[:, :, 0:GRP], Dd[0:two, 4 * b:4 * b + 4, :], ALU.add)
                last.then_inc(s_kst, 1)


class Norm:
    LEAD = 2

    def __init__(self, cr, prefix, nt, src, xn, outs, stat, store=None):
        (self.ss, self.var, self.std, self.rstd, self.xnr, self.tr, self.ev, self.st0, self.st1) = cr.sems(
            prefix + "_norm", "squares variance std rstd normed turned placed kept0 kept1")
        self.cr, self.nt, self.src, self.xn, self.outs = cr, nt, src, xn, outs
        self.stat, self.store = stat, store
        self.st = (self.st0, self.st1)
        self.parts = [(0, self.LEAD), (self.LEAD, nt)]

    def _stat(self, j, part):
        a, b = part
        return self.stat[:, j * self.nt + a:j * self.nt + b]

    def act_lead(self, act):
        nc = self.cr.nc
        squares = self.cr.score_view(3, 2)
        for n, (a, b) in enumerate(self.parts):
            for i in range(a, b):
                if i:
                    act.wait_ge(self.ss, i)
                nc.scalar.activation(squares, self.src(i), ACT.Square,
                                     accum_out=self.stat[:, i:i + 1]).then_inc(self.ss, 1)
            act.wait_ge(self.var, n + 1)
            nc.scalar.activation(self._stat(2, (a, b)), self._stat(1, (a, b)), ACT.Sqrt).then_inc(self.std, 1)
            act.wait_ge(self.rstd, n + 1)
            for i in range(a, min(b, self.LEAD)):
                self.act_tile(act, i)

    def act_tile(self, act, i):
        if i >= 2:
            act.wait_ge(self.tr, 2 * (i - 1))
            if self.store:
                act.wait_ge(self.st[i % 2], 16 * (i // 2))
        self.cr.nc.scalar.activation(self.xn[i % 2], self.src(i), ACT.Copy,
                                     scale=self._stat(3, (i, i + 1))).then_inc(self.xnr, 1)

    def act(self, act):
        self.act_lead(act)
        for i in range(self.LEAD, self.nt):
            self.act_tile(act, i)

    def act_ahead(self, act, i):
        for j in ([self.LEAD] if i == 0 else []) + [i + self.LEAD + 1]:
            if j < self.nt:
                self.act_tile(act, j)

    def dve_stats(self, dve, n):
        nc, part = self.cr.nc, self.parts[n]
        dve.wait_ge(self.ss, part[1])
        nc.vector.tensor_scalar(self._stat(1, part), self._stat(0, part), 1.0 / D, EPS, ALU.mult, ALU.add).then_inc(self.var, 1)
        dve.wait_ge(self.std, n + 1)
        nc.vector.reciprocal(self._stat(3, part), self._stat(2, part)).then_inc(self.rstd, 1)

    def dve_tile(self, dve, i):
        nc = self.cr.nc
        for h in range(2):
            dve.wait_ge(self.tr, 2 * i + h + 1)
            for q in range(4):
                k = 4 * h + q
                for dst, gain, shift in self.outs:
                    last = nc.vector.tensor_scalar(dst(k, i), self.cr.bank[h][:, q * P:(q + 1) * P],
                                                   gain(i)(k), shift(i)(k), ALU.mult, ALU.add)
            last.then_inc(self.ev, 1)

    def dve_lead(self, dve):
        self.dve_stats(dve, 0)
        for i in range(self.LEAD):
            self.dve_tile(dve, i)
        self.dve_stats(dve, 1)

    def dve(self, dve):
        self.dve_lead(dve)
        for i in range(self.LEAD, self.nt):
            self.dve_tile(dve, i)

    def pe_tile(self, pe, i):
        pe.wait_ge(self.xnr, i + 1)
        for h in range(2):
            if i:
                pe.wait_ge(self.ev, 2 * i + h - 1)
            for q in range(4):
                k = 4 * h + q
                last = self.cr.nc.tensor.transpose(self.cr.bank[h][:, q * P:(q + 1) * P],
                                                   self.xn[i % 2][:, k * P:(k + 1) * P], self.cr.const(C_ID))
            last.then_inc(self.tr, 1)

    def pe(self, pe, count=None):
        for i in range(count or self.nt):
            self.pe_tile(pe, i)

    def tile_ready(self, pe, i):
        pe.wait_ge(self.ev, 2 * i + 2)

    def pe_ahead(self, pe, i):
        if i + self.LEAD < self.nt:
            self.pe_tile(pe, i + self.LEAD)

    def dve_ahead(self, dve, i):
        if i + self.LEAD < self.nt:
            self.dve_tile(dve, i + self.LEAD)

    def keep(self, eng):
        for i in range(self.nt):
            eng.wait_ge(self.xnr, i + 1)
            eng.dma_start(self.store(i), self.xn[i % 2]).then_inc(self.st[i % 2], 16)

    def kept(self, eng):
        for s in range(2):
            eng.wait_ge(self.st[s], 16 * ((self.nt + 1 - s) // 2))


LBANK = (2, 3, 4, 5)


class Units:

    def __init__(self, cr, prefix):
        self.full, self.empty = cr.sems(prefix, "product_ready product_taken")
        self.cr, self.n = cr, 0

    def bank(self, u):
        return self.cr.bank[LBANK[u % 4]][:, :]

    def before(self, pe, u):
        if u >= 4:
            pe.wait_ge(self.empty, u - 3)


def stream(cr, sp, first, count, units, per_tile):
    u = 0
    for t in range(count):
        u += per_tile[t]
        sp.wait_ge(units.full, u)
        cr.load_w(sp, first + t + RING)


def product(cr, pe, un, bank_ap, pairs):
    un.before(pe, un.n)
    for k, (l, r) in enumerate(pairs):
        last = cr.nc.tensor.matmul(bank_ap, l, r, start=(k == 0), stop=(k == len(pairs) - 1))
    last.then_inc(un.full, 1)
    un.n += 1


def block_a_in(cr):
    nc, io = cr.nc, cr.io
    uT, zT = cr.dram("u_T", [D, SEQ]), cr.dram("z_T", [D, SEQ])
    x_in, st0, st1 = cr.sems("ain", "x_loaded stored0 stored1")
    st = (st0, st1)
    hT = cr.at(A_U, KT, SEQ)
    xa = cr.at(A_S, NT, D)
    stage = cr.at(A_M + 2048, 2, 512)
    un = Units(cr, "ain")
    nrm = Norm(cr, "ain", NT, lambda i: xa[:, i], [cr.at(A_M, D), cr.at(A_M + D, D)],
               [(lambda k, i: hT[:, k, i * P:(i + 1) * P], lambda i: cr.gain(GS_A), lambda i: cr.shift(MC_A, V_C))],
               cr.small[:, 300:332])
    NU = 32

    with nc.Block() as block:
        @block.sync
        def _(sp):
            sp.dma_start(xa, io["x"].rearrange("b (c t) d -> (b c) t d", t=T_CH)).then_inc(x_in, 16)
            stream(cr, sp, W_AIN, 4, un, [8] * 4)

        @block.scalar
        def _(act):
            act.wait_ge(x_in, 16)
            nrm.act(act)
            for u in range(NU):
                act.wait_ge(un.full, u + 1)
                if u >= 2:
                    act.wait_ge(st[u % 2], 16 * (u // 2))
                nc.scalar.activation(stage[:, u % 2], un.bank(u), ACT.Copy if u < NU // 2 else ACT.Silu).then_inc(un.empty, 1)

        @block.gpsimd
        def _(pool):
            for u in range(NU):
                m, h = 4 * (u // 8) + u % 4, u // 4 % 2
                dst = (uT if m < KT else zT)[(m % KT) * P:(m % KT + 1) * P, h * 512:(h + 1) * 512]
                pool.wait_ge(un.empty, u + 1)
                pool.dma_start(dst, stage[:, u % 2]).then_inc(st[u % 2], 16)
            for s in range(2):
                pool.wait_ge(st[s], 16 * NU // 2)

        @block.vector
        def _(dve):
            nrm.dve(dve)

        @block.tensor
        def _(pe):
            nrm.pe(pe, 4)
            for t in range(4):
                cr.wait_w(pe, W_AIN + t)
                w = cr.w(W_AIN + t)
                for h in range(2):
                    if t == 0:
                        nrm.tile_ready(pe, 4 * h + 3)
                    for m in range(4):
                        product(cr, pe, un, un.bank(un.n), [(w[:, k, m * P:(m + 1) * P], hT[:, k, h * 512:(h + 1) * 512])
                                                            for k in range(KT)])
                        if t == 0 and h == 0:
                            nrm.pe_tile(pe, 4 + m)


def block_ssm(cr):
    nc = cr.nc
    uT, Kd = cr.dram("u_T", [D, SEQ]), cr.dram("k_lags", [GRP, GROUPS, 2 * P])
    u_in, m0, m1, b_full, b_empty, s_link, s_scan, y_full, y_empty = cr.sems(
        "ssm", "u_loaded m_loaded0 m_loaded1 inputs_ready inputs_taken dve scanned y_ready y_taken")
    m_in = (m0, m1)
    V = [cr.at(A_V + r * 4608, NPAIR, 9, GRP) for r in range(2)]
    S = cr.at(A_S, 2, NPAIR, SCOL)
    U = cr.at(A_U, GROUPS, NCH)
    WT = cr.at(A_Y, NPAIR, 2, P)
    Y = cr.at(A_Y, T_CH, D)
    M = cr.at(A_M, 2, 8, P)
    sm = cr.small
    a8r, a8i = sm[:, S_A8R:S_A8R + 32], sm[:, S_A8I:S_A8I + 32]
    pw = sm[:, 300:300 + 2 * NPAIR * SEG_L].rearrange("p (r j q) -> p r j q", r=2, q=SEG_L)
    ta, tb = cr.at(A_U + GROUPS * NCH, 2, 480), cr.at(A_M + 2048, 2, 512)
    Sg = [S[:, r, :, 1:SCOL].rearrange("p j (n q) -> p j n q", q=SEG_L) for r in range(2)]

    with nc.Block() as block:
        def load_m(eng, c):
            for t in range(T_CH):
                eng.dma_start(M[GRP * t:GRP * (t + 1), c % 2], Kd[:, 8 * c:8 * c + 8, P - GRP * t:2 * P - GRP * t]).then_inc(m_in[c % 2], 16)

        @block.sync
        def _(sp):
            for t in range(T_CH):
                sp.dma_start(U[GRP * t:GRP * (t + 1)], uT.rearrange("(g c) t -> c g t", c=GRP)[:, :, t * NCH:(t + 1) * NCH]).then_inc(u_in, 16)
            for c in range(8):
                if c >= 2:
                    sp.wait_ge(y_full, 2 * (c - 1))
                load_m(sp, c)

        @block.tensor
        def _(pe):
            pe.wait_ge(u_in, 16 * T_CH)
            for j in range(NPAIR):
                if j >= 4:
                    pe.wait_ge(b_empty, j - 3)
                for r in range(2):
                    for h in range(2):
                        last = nc.tensor.matmul(cr.bank[j % 4][64 * h:64 * h + 64, r * P:(r + 1) * P],
                                                WT[:, j, r, 64 * h:64 * h + 64], U[:, 2 * j + h, :], start=True, stop=True)
                last.then_inc(b_full, 1)
            for g in range(GROUPS):
                j, h, b = g // 2, 64 * (g % 2), g // 8
                if g % 8 == 0:
                    pe.wait_ge(s_scan, b + 1)
                    pe.wait_ge(m_in[b % 2], P * (b // 2 + 1))
                    if b >= 2:
                        pe.wait_ge(y_empty, 2 * (b - 1))
                dst = cr.bank[4 + b % 2 * 2 + g % 2][:, (j % 4) * P:(j % 4 + 1) * P]
                nc.tensor.matmul(dst, U[:, g, :], M[:, (g // 8) % 2, g % 8, :], start=True, stop=False)
                for r in range(2):
                    last = nc.tensor.matmul(dst, S[h:h + 64, r, j, 0:NCH],
                                            V[r][h:h + 64, j, 1:9, :].rearrange("p t c -> p (t c)"),
                                            start=False, stop=(r == 1))
                if j % 4 == 3:
                    last.then_inc(y_full, 1)

        @block.scalar
        def _(act):
            for j in range(NPAIR):
                act.wait_ge(b_full, j + 1)
                nc.scalar.activation(S[:, :, j, 1:SCOL], cr.bank[j % 4][:, 0:2 * P].rearrange("p (r n) -> p r n", r=2),
                                     ACT.Copy).then_inc(b_empty, 1)
            for b in range(16):
                act.wait_ge(y_full, b + 1)
                g0 = b // 2 * 8 + b % 2
                nc.scalar.activation(Y.rearrange("p t (g c) -> p g t c", c=GRP)[:, g0:g0 + 7:2],
                                     cr.bank[4 + b % 4][:, :].rearrange("p (g t c) -> p g t c", g=4, t=T_CH),
                                     ACT.Gelu_apprx_tanh).then_inc(y_empty, 1)

        @block.vector
        def _(dve):
            ln = Link(dve, s_link)
            tt = nc.vector.tensor_tensor
            nc.vector.memset(S[:, :, :, 0:1], 0.0)

            def add_times(dst, s_, a, t1, t2):
                tt(t1[0], s_[0], a[0], ALU.mult)
                tt(t2[0], s_[1], a[1], ALU.mult)
                tt(t1[1], s_[1], a[0], ALU.mult)
                ln(tt(t2[1], s_[0], a[1], ALU.mult))
                tt(t1[0], t1[0], t2[0], ALU.subtract)
                ln(tt(t1[1], t1[1], t2[1], ALU.add))
                tt(dst[0], dst[0], t1[0], ALU.add)
                return tt(dst[1], dst[1], t1[1], ALU.add)

            def temps(*shape):
                n = int(np.prod(shape))
                names = [f"a{i}" for i in range(len(shape))]
                form = lambda v: v.rearrange(f"p ({' '.join(names)}) -> p {' '.join(names)}", **dict(zip(names[1:], shape[1:])))
                return [[form(t[:, r, 0:n]) for r in range(2)] for t in (ta, tb)]

            ln(nc.vector.memset(pw, 0.0))
            tt(pw[:, 0, :, 0], pw[:, 0, :, 0], a8r, ALU.add)
            ln(tt(pw[:, 1, :, 0], pw[:, 1, :, 0], a8i, ALU.add))
            for q in range(1, SEG_L):
                t1, t2 = temps(NPAIR)
                ln(add_times([pw[:, r, :, q] for r in range(2)], [pw[:, r, :, q - 1] for r in range(2)], (a8r, a8i), t1, t2))
            half = NPAIR // 2
            for m in range(2):
                dve.wait_ge(b_empty, half * (m + 1))
                t1, t2 = temps(half, N_SEG)
                js = slice(half * m, half * (m + 1))
                a = [pw[:, r, js, 0].unsqueeze(2).broadcast_to([P, half, N_SEG]) for r in range(2)]
                for q in range(1, SEG_L):
                    ln(add_times([Sg[r][:, js, :, q] for r in range(2)], [Sg[r][:, js, :, q - 1] for r in range(2)], a, t1, t2))
            t1, t2 = temps(NPAIR)
            for n in range(1, N_SEG):
                ln(add_times([Sg[r][:, :, n, SEG_L - 1] for r in range(2)], [Sg[r][:, :, n - 1, SEG_L - 1] for r in range(2)],
                             [pw[:, r, :, SEG_L - 1] for r in range(2)], t1, t2))
            shape = (4, N_SEG - 1, SEG_L - 1)
            t1, t2 = temps(*shape)
            for m in range(NPAIR // 4):
                js = slice(4 * m, 4 * m + 4)
                add_times([Sg[r][:, js, 1:N_SEG, 0:SEG_L - 1] for r in range(2)],
                          [Sg[r][:, js, 0:N_SEG - 1, SEG_L - 1].unsqueeze(3).broadcast_to([P, *shape]) for r in range(2)],
                          [pw[:, r, js, 0:SEG_L - 1].unsqueeze(2).broadcast_to([P, *shape]) for r in range(2)], t1, t2).then_inc(s_scan, 1)
                dve.wait_ge(s_scan, m + 1)


def gate_diag(cr, diag, col, variant, sem):
    for k in range(KT):
        last = cr.nc.vector.tensor_scalar(diag[:, k * P:(k + 1) * P], cr.const(C_ID), cr.shift(col, variant)(k), None, ALU.mult)
    last.then_inc(sem, 1)


def gate_rows(cr, diag, banks, sem):
    for k in range(KT):
        last = cr.nc.tensor.matmul(cr.bank[banks[k // 4]][:, (k % 4) * P:(k % 4 + 1) * P], cr.const(C_ONE),
                                   diag[:, k * P:(k + 1) * P], start=True, stop=True)
    last.then_inc(sem, 1)


def X(cr):
    return cr.at(0, NTC, D)


def block_a_out(cr):
    nc, io = cr.nc, cr.io
    zT = cr.dram("z_T", [D, SEQ])
    x_in, z0, z1, t_full, t_empty, sg, s_l, s_g, d_ok, g_mm, g_ok = cr.sems(
        "aout", "x_loaded z_loaded0 z_loaded1 turned placed sigmoid dve gated diag gate_mm gate_copied")
    z_in = (z0, z1)
    Xr = X(cr)
    yT = cr.at(10240, KT, SEQ)
    y3 = cr.at(18432, KT, SEQ)
    Y = cr.at(A_Y, T_CH, D)
    zs = cr.at(34816, 2, SEQ)
    gate = cr.at(36864, D)
    diag = cr.at(8192, D)
    tmp = cr.at(A_Y, 2, 512)
    un = Units(cr, "aout")
    bglu = cr.cols[:, 0:8]

    with nc.Block() as block:
        @block.sync
        def _(sp):
            sp.dma_start(Xr[:, 0:NT], io["x"].rearrange("b (i p) d -> (b p) i d", p=P)).then_inc(x_in, 16)
            stream(cr, sp, W_GLU, 4, un, [8] * 4)

        @block.gpsimd
        def _(pool):
            for m in range(KT):
                if m >= 2:
                    pool.wait_ge(s_g, 2 * (m - 1))
                pool.dma_start(zs[:, m % 2], zT[m * P:(m + 1) * P, :]).then_inc(z_in[m % 2], 16)

        @block.tensor
        def _(pe):
            pe.wait_ge(d_ok, 1)
            gate_rows(cr, diag, (6, 7), g_mm)
            for v in range(16):
                dch, h = v // 2, v % 2
                if v >= 2:
                    pe.wait_ge(t_empty, v - 1)
                for q in range(4):
                    last = nc.tensor.transpose(cr.bank[v % 2][:, q * P:(q + 1) * P], Y[:, 4 * h + q, dch * P:(dch + 1) * P], cr.const(C_ID))
                last.then_inc(t_full, 1)
            pe.wait_ge(t_empty, 16)
            for t in range(2):
                cr.wait_w(pe, W_GLU + t)
                w = cr.w(W_GLU + t)
                for m in range(4):
                    for h in range(2):
                        product(cr, pe, un, un.bank(un.n), [(w[:, k, m * P:(m + 1) * P], yT[:, k, h * 512:(h + 1) * 512]) for k in range(KT)])
            pe.wait_ge(s_g, 16)
            for t in range(2):
                cr.wait_w(pe, W_AOUT + t)
                w = cr.w(W_AOUT + t)
                for i in range(NT):
                    product(cr, pe, un, un.bank(un.n), [(y3[:, k, i * P:(i + 1) * P], w[:, k, :]) for k in range(KT)])

        @block.scalar
        def _(act):
            act.wait_ge(g_mm, 1)
            for b in range(2):
                nc.scalar.activation(gate[:, b * 512:(b + 1) * 512], cr.bank[6 + b][:, :], ACT.Copy).then_inc(g_ok, 1)
            for u in range(16):
                m, h = u // 2, u % 2
                act.wait_ge(un.full, u + 1)
                nc.scalar.activation(y3[:, m, h * 512:(h + 1) * 512], un.bank(u), ACT.Sigmoid, bias=bglu[:, m:m + 1]).then_inc(sg, 1)

        @block.vector
        def _(dve):
            ln = Link(dve, s_l)
            gate_diag(cr, diag, MC_A + 16, V_C, d_ok)
            for v in range(16):
                dch, h = v // 2, v % 2
                dve.wait_ge(t_full, v + 1)
                nc.vector.tensor_copy(yT[:, dch].rearrange("p (c t) -> p t c", t=T_CH)[:, 4 * h:4 * h + 4],
                                      cr.bank[v % 2][:, :].rearrange("p (t c) -> p t c", t=4)).then_inc(t_empty, 1)
            dve.wait_ge(t_empty, 16)
            for u in range(16):
                m, h = u // 2, u % 2
                dve.wait_ge(sg, u + 1)
                y_ = y3[:, m, h * 512:(h + 1) * 512]
                nc.vector.tensor_tensor(y_, y_, yT[:, m, h * 512:(h + 1) * 512], ALU.mult).then_inc(un.empty, 1)
                dve.wait_ge(un.empty, u + 1)
                dve.wait_ge(z_in[m % 2], 16 * (m // 2 + 1))
                y4 = y_.rearrange("p (c t) -> p c t", t=T_CH)
                nc.vector.tensor_tensor(y4, y4, zs[:, m % 2].rearrange("p (t c) -> p c t", t=T_CH)[:, 64 * h:64 * h + 64], ALU.mult).then_inc(s_g, 1)
            dve.wait_ge(x_in, 16)
            dve.wait_ge(g_ok, 2)
            for u in range(16, 32):
                t, i = (u - 16) // NT, (u - 16) % NT
                dve.wait_ge(un.full, u + 1)
                residual_add(cr, dve, ln, un, u, tmp[:, u % 2], gate[:, t * 512:(t + 1) * 512], Xr[:, i, t * 512:(t + 1) * 512])


def residual_add(cr, dve, ln, un, u, tmp, gate, x):
    cr.nc.vector.tensor_tensor(tmp, un.bank(u), gate, ALU.mult).then_inc(un.empty, 1)
    dve.wait_ge(un.empty, u + 1)
    ln(cr.nc.vector.tensor_tensor(x, x, tmp, ALU.add))


def block_heads(cr, name, w0, gain, shift, head_col, scale, dst_T, dst_rows, rows_func, forget):
    nc, io = cr.nc, cr.io
    hT_d, rows_d = cr.dram(dst_T, [D, SEQ]), cr.dram(dst_rows, [SEQ, D])
    sq, red, var, std, rst, scaled, turned, placed, link = cr.sems(
        name, "squared reduced variance std rstd scaled turned placed dve")
    st, kst_ = cr.sems(name, "stored0 stored1"), cr.sems(name, "t_stored0 t_stored1")
    raw = cr.at(18432, NT, D)
    hT = cr.at(10240, KT, SEQ)
    stage = cr.at(28672, 2, 512)
    sqb = cr.at(29696, 2, 512)
    kst = cr.at(30720, 2, 512)
    hs = cr.at(31744, 4, NT * HB)
    un = Units(cr, name)
    Xr = X(cr)
    nrm = Norm(cr, name, NT, lambda i: Xr[:, i], [cr.at(26624, D), cr.at(27648, D)],
               [(lambda k, i: hT[:, k, i * P:(i + 1) * P], lambda i: cr.gain(gain), lambda i: cr.shift(shift, V_C))],
               cr.small[:, 300:332])
    if forget:
        f_in, f_mm, f_x, f_e, f_l, f_ls, f_cum, f_row, f_st = cr.sems(
            name, "f_loaded f_logits f_biased f_exp f_log f_logsig f_sums f_rows f_stored")
        fw = cr.at(32256, KT, HB)
        fb = cr.at(32384, HB)
        fx, fa, fe, fl = [cr.at(32400 + 128 * n, NT, HB) for n in range(4)]
        FT = cr.at(33000, 2, SEQ)
        F_d = cr.dram("f_rows", [2, HB, SEQ])

    with nc.Block() as block:
        @block.sync
        def _(sp):
            if forget:
                sp.dma_start(fw, io["f_w"]).then_inc(f_in, 16)
                sp.dma_start(fb, io["f_b"].broadcast_to([P, HB])).then_inc(f_in, 16)

            def store_t(first, end):
                for v in range(first, end):
                    c, h = v // 2, v % 2
                    sp.wait_ge(placed, v + 1)
                    sp.dma_start(hT_d[c * P:(c + 1) * P, h * 512:(h + 1) * 512], kst[:, v % 2]).then_inc(kst_[v % 2], 16)

            for t in range(4):
                if t == 2 and forget:
                    sp.wait_ge(f_row, 1)
                    for n in range(2):
                        sp.dma_start(F_d[n], FT[0:HB, n]).then_inc(f_st, 16)
                if t >= 2:
                    store_t(*((0, 5), (5, 13))[t - 2])
                sp.wait_ge(un.full, 8 * (t + 1))
                cr.load_w(sp, w0 + t + RING)
            store_t(13, 16)
            for s in range(2):
                sp.wait_ge(kst_[s], 16 * 8)
            if forget:
                sp.wait_ge(f_st, 32)

        @block.gpsimd
        def _(pool):
            for u in range(16, 32):
                t, i = (u - 16) // NT, u % NT
                pool.wait_ge(un.empty, u + 1)
                pool.dma_start(rows_d[i * P:(i + 1) * P, t * 512:(t + 1) * 512], stage[:, u % 2]).then_inc(st[u % 2], 16)
            for s in range(2):
                pool.wait_ge(st[s], 16 * 8)

        @block.tensor
        def _(pe):
            LAG = 2

            def turn(v):
                c, h = v // 2, v % 2
                pe.wait_ge(scaled, NT)
                if v >= 2:
                    pe.wait_ge(placed, v - 1)
                for q in range(4):
                    i = 4 * h + q
                    last = nc.tensor.transpose(cr.bank[6 + v % 2][:, q * P:(q + 1) * P], raw[:, i, c * P:(c + 1) * P], cr.const(C_ID))
                last.then_inc(turned, 1)

            nrm.pe(pe, nrm.LEAD)
            for t in range(4):
                cr.wait_w(pe, w0 + t)
                w = cr.w(w0 + t)
                for i in range(NT):
                    if t == 0:
                        nrm.tile_ready(pe, i)
                    product(cr, pe, un, un.bank(un.n), [(hT[:, k, i * P:(i + 1) * P], w[:, k, :]) for k in range(KT)])
                    if t == 0:
                        nrm.pe_ahead(pe, i)
                    if un.n > 16 + LAG:
                        turn(un.n - 17 - LAG)
                if forget and t == 0:
                    pe.wait_ge(f_in, 32)
                    for i in range(NT):
                        for k in range(KT):
                            last = nc.tensor.matmul(cr.bank[7][:, i * HB:(i + 1) * HB], hT[:, k, i * P:(i + 1) * P], fw[:, k],
                                                    start=(k == 0), stop=(k == KT - 1))
                    last.then_inc(f_mm, 1)
                if forget and t == 1:
                    pe.wait_ge(f_ls, 1)
                    for i in range(NT):
                        for j in range(i + 1):
                            last = nc.tensor.matmul(cr.bank[i // 4][0:HB, (i % 4) * P:(i % 4 + 1) * P], fe[:, j],
                                                    cr.const(C_TRI if j == i else C_ONE), start=(j == 0), stop=(j == i))
                    last.then_inc(f_cum, 1)
            for v in range(16 - LAG, 16):
                turn(v)

        @block.scalar
        def _(act):
            nrm.act_lead(act)
            for u in range(16):
                if u < NT:
                    nrm.act_ahead(act, u)
                if forget and u == NT:
                    act.wait_ge(f_x, 1)
                    nc.scalar.activation(fe, fa, ACT.Exp, scale=-1.0).then_inc(f_e, 1)
                    act.wait_ge(f_e, 1)
                    nc.scalar.activation(fl, fe, ACT.Ln, bias=1.0).then_inc(f_l, 1)
                t, i = u // NT, u % NT
                act.wait_ge(un.full, u + 1)
                r = raw[:, i, t * 512:(t + 1) * 512]
                if u >= 2:
                    act.wait_ge(red, u - 1)
                nc.scalar.activation(sqb[:, u % 2], un.bank(u), ACT.Square).then_inc(sq, 1)
                nc.scalar.activation(r, un.bank(u), ACT.Copy).then_inc(un.empty, 1)
            act.wait_ge(var, 1)
            nc.scalar.activation(hs[:, 2], hs[:, 1], ACT.Sqrt).then_inc(std, 1)
            for u in range(16, 32):
                act.wait_ge(un.full, u + 1)
                if u >= 18:
                    act.wait_ge(st[u % 2], 16 * ((u - 16) // 2))
                nc.scalar.activation(stage[:, u % 2], un.bank(u), rows_func).then_inc(un.empty, 1)

        @block.vector
        def _(dve):
            ln = Link(dve, link)
            nrm.dve_lead(dve)
            tt, ts = nc.vector.tensor_tensor, nc.vector.tensor_scalar
            for u in range(16):
                t, i = u // NT, u % NT
                if t == 0:
                    nrm.dve_ahead(dve, i)
                if forget and u == NT:
                    dve.wait_ge(f_mm, 1)
                    ln(tt(fx, cr.bank[7][:, 0:NT * HB].rearrange("p (i h) -> p i h", h=HB), fb.unsqueeze(1).broadcast_to([P, NT, HB]), ALU.add))
                    ln(ts(fa, fx, -1.0, None, ALU.mult))
                    tt(fa, fa, fx, ALU.max).then_inc(f_x, 1)
                    dve.wait_ge(f_l, 1)
                    flat = lambda v: v.rearrange("p i h -> p (i h)")
                    nc.vector.scalar_tensor_tensor(flat(fe), flat(fx), 0.0, flat(fl), ALU.min, ALU.subtract).then_inc(f_ls, 1)
                dve.wait_ge(sq, u + 1)
                nc.vector.tensor_reduce(hs[:, 0, i * HB + 8 * t:i * HB + 8 * t + 8], sqb[:, u % 2].rearrange("p (h d) -> p h d", d=HD),
                                        AXX, ALU.add).then_inc(red, 1)
            dve.wait_ge(red, 16)
            ts(hs[:, 1], hs[:, 0], 1.0 / HD, EPS, ALU.mult, ALU.add).then_inc(var, 1)
            dve.wait_ge(std, 1)
            nc.vector.reciprocal(hs[:, 3], hs[:, 2]).then_inc(rst, 1)
            dve.wait_ge(rst, 1)
            dve.wait_ge(un.empty, 16)
            for i in range(NT):
                r = raw[:, i].rearrange("p (h d) -> p h d", d=HD)
                tt(r, r, hs[:, 3, i * HB:(i + 1) * HB].unsqueeze(2).broadcast_to([P, HB, HD]), ALU.mult).then_inc(scaled, 1)
            if forget:
                dve.wait_ge(f_cum, 1)
                for b in range(2):
                    ln(nc.vector.tensor_copy(FT[0:HB, 0, b * 512:(b + 1) * 512], cr.bank[b][0:HB, :]))
                ts(FT[0:HB, 1], FT[0:HB, 0], -1.0, None, ALU.mult).then_inc(f_row, 1)
            for v in range(16):
                dve.wait_ge(turned, v + 1)
                if v >= 2:
                    dve.wait_ge(kst_[v % 2], 16 * (v // 2))
                ts(kst[:, v % 2], cr.bank[6 + v % 2][:, :], cr.cols[:, head_col:head_col + 1], scale, ALU.mult, ALU.mult).then_inc(placed, 1)


def block_kv(cr):
    block_heads(cr, "kv", W_KV, GS_KV, MC_KV, 8, 1.0, "k_T", "v_rows", ACT.Copy, True)


def block_bq(cr):
    block_heads(cr, "bq", W_BIN, GS_B, MC_B, 9, HD ** -0.5, "q_T", "zb_rows", ACT.Silu, False)


class Step:

    def __init__(self, slot, q, pieces, masks, width, pv, sink, o):
        self.slot, self.q, self.pieces, self.masks = slot, q, pieces, masks
        self.width, self.pv, self.sink, self.o = width, pv, sink, o
        self.groups = (len(pv) + 3) // 4
        self.o_col = slot * HD


def wait_from_one(eng, sem, value):
    if not (isinstance(value, int) and value < 1):
        eng.wait_ge(sem, value)


def attention(cr, name, n_iter, steps, loads, static_loads, store, score_banks, p_buf, t_buf, padded):
    nc = cr.nc
    qk, mx, pr, tr, te, inv, pv, oe, li, s_in, *zero = cr.sems(
        name, "scores maxima probs turned placed inverses products outputs masked fixed_loaded padded0 padded1")
    ld, st = cr.sems(name, "loaded0 loaded1"), cr.sems(name, "stored0 stored1")
    NS = len(steps)
    goff = [0]
    for s_ in steps:
        goff.append(goff[-1] + s_.groups)
    NG = goff[-1]
    last_of = [max(n for n, s_ in enumerate(steps) if s_.slot == k) for k in range(2)]
    first_of = [min(n for n, s_ in enumerate(steps) if s_.slot == k) for k in range(2)]
    NL = [len(loads(k, 0)) for k in range(2)]
    nb = score_banks
    rest = 8 - 2 * nb
    n_pt = n_o = rest // 2
    nmax, rsum, rinv = [cr.small[:, 300 + 2 * n:302 + 2 * n] for n in range(3)]
    pt_bank = lambda G: cr.bank[2 * nb + G % n_pt]
    o_bank = lambda u: cr.bank[2 * nb + n_pt + u % n_o]

    def sc(u, a, b):
        n = a // 512
        assert (b - 1) // 512 == n
        return cr.bank[u % 2 * nb + n][:, a - 512 * n:b - 512 * n]

    def sc_wide(u, w):
        return cr.score_view(u % 2, nb)[:, 0:w]

    def pipeline(eng, body, lag):
        for u in range(NS):
            body(0, u, True)
        with eng.Fori(1, n_iter) as it:
            for u in range(NS):
                body(it, u, True)
        for u in range(lag):
            body(n_iter, u, False)

    def behind(it, u, lag):
        if u >= lag:
            return it, u - lag
        return None if isinstance(it, int) and it == 0 else (it - 1, u - lag + NS)

    with nc.Block() as block:
        @block.sync
        def _(sp):
            for z in zero:
                sp.wait_ge(z, 1)
            for to, of in static_loads:
                sp.dma_start(to, of).then_inc(s_in, 16)
            for k in range(2):
                for to, of in loads(k, 0):
                    sp.dma_start(to, of).then_inc(ld[k], 16)

            def finish(k, it):
                sp.wait_ge(oe, it * NS + (last_of[k] + 1))
                to, of = store(k, it)
                sp.dma_start(to, of).then_inc(st[k], 16)

            with sp.Fori(0, n_iter - 1) as it:
                for k in range(2):
                    finish(k, it)
                    for to, of in loads(k, it + 1):
                        sp.dma_start(to, of).then_inc(ld[k], 16)
            for k in range(2):
                finish(k, n_iter - 1)
            for k in range(2):
                sp.wait_ge(st[k], 16 * n_iter)

        @block.gpsimd
        def _(pool):
            nc.gpsimd.memset(padded[0], 0.0).then_inc(zero[0], 1)

        @block.tensor
        def _(pe):
            pe.wait_ge(s_in, 16 * len(static_loads))
            for z in zero:
                pe.wait_ge(z, 1)

            def turn(b, g):
                it, u = b
                s_, G = steps[u], goff[u] + g
                if g == 0:
                    pe.wait_ge(pr, it * NS + (u + 1))
                wait_from_one(pe, te, it * NG + (G + 1 - n_pt))
                for n in range(4 * g, min(4 * g + 4, len(s_.pv))):
                    last = nc.tensor.transpose(pt_bank(G)[:, (n % 4) * P:(n % 4 + 1) * P],
                                               p_buf[:, u % 2, s_.pv[n][0]:s_.pv[n][0] + P], cr.const(C_ID))
                last.then_inc(tr, 1)

            def step(it, u, new):
                b = behind(it, u, 2)
                groups = steps[b[1]].groups if b else 0
                pieces = steps[u].pieces if new else []
                for n in range(max(groups, len(pieces))):
                    if n < groups:
                        turn(b, n)
                    if n < len(pieces):
                        s_ = steps[u]
                        if n == 0:
                            if u in first_of:
                                pe.wait_ge(ld[s_.slot], (it + 1) * (16 * NL[s_.slot]))
                            wait_from_one(pe, pr, it * NS + (u - 1))
                        x, y, rhs = pieces[n]
                        last = nc.tensor.matmul(sc(u, x, y), s_.q, rhs, start=True, stop=True)
                        if n == len(pieces) - 1:
                            last.then_inc(qk, 1)
                if b:
                    ib, ub = b
                    s_ = steps[ub]
                    wait_from_one(pe, oe, ib * NS + (ub + 1 - n_o))
                    for n, (_, v) in enumerate(s_.pv):
                        if n % 4 == 0:
                            pe.wait_ge(te, ib * NG + (goff[ub] + n // 4 + 1))
                        last = nc.tensor.matmul(o_bank(ub)[:, 0:P], t_buf[:, ub % 2, n, :], v, start=(n == 0), stop=(n == len(s_.pv) - 1))
                    last.then_inc(pv, 1)

            pipeline(pe, step, 2)

        @block.scalar
        def _(act):
            def step(it, u, new):
                b = behind(it, u, 3)
                if b:
                    ib, ub = b
                    s_ = steps[ub]
                    act.wait_ge(pv, ib * NS + (ub + 1))
                    act.wait_ge(inv, ib * NS + (ub + 1))
                    if ub in first_of:
                        wait_from_one(act, st[s_.slot], ib * 16)
                    nc.scalar.activation(s_.o, o_bank(ub)[:, s_.o_col:s_.o_col + HD], ACT.Copy,
                                         scale=rinv[:, ub % 2:ub % 2 + 1]).then_inc(oe, 1)
                if new:
                    s_ = steps[u]
                    act.wait_ge(mx, it * NS + (u + 1))
                    w = s_.width + (s_.sink is not None)
                    nc.scalar.activation(p_buf[:, u % 2, 0:w], sc_wide(u, w), ACT.Exp, bias=nmax[:, u % 2:u % 2 + 1],
                                         accum_out=rsum[:, u % 2:u % 2 + 1]).then_inc(pr, 1)

            pipeline(act, step, 3)

        @block.vector
        def _(dve):
            nc.vector.memset(padded[1], 0.0).then_inc(zero[1], 1)
            dve.wait_ge(s_in, 16 * len(static_loads))
            loff = [0]
            for s_ in steps:
                loff.append(loff[-1] + (len(s_.masks) + (s_.sink is not None) > 0))

            def step(it, u, new):
                b = behind(it, u, 2)
                if b:
                    ib, ub = b
                    s_ = steps[ub]
                    for g in range(s_.groups):
                        G = goff[ub] + g
                        m = min(4, len(s_.pv) - 4 * g)
                        dve.wait_ge(tr, ib * NG + (G + 1))
                        nc.vector.tensor_copy(t_buf[:, ub % 2, 4 * g:4 * g + m, :].rearrange("p n q -> p (n q)"),
                                              pt_bank(G)[:, 0:m * P]).then_inc(te, 1)
                    wait_from_one(dve, oe, ib * NS + (ub - 1))
                    nc.vector.reciprocal(rinv[:, ub % 2:ub % 2 + 1], rsum[:, ub % 2:ub % 2 + 1]).then_inc(inv, 1)
                if not new:
                    return
                s_ = steps[u]
                dve.wait_ge(qk, it * NS + (u + 1))
                last = None
                for col, c in s_.masks:
                    last = nc.vector.tensor_tensor(sc(u, col, col + P), sc(u, col, col + P), cr.const(c), ALU.add)
                w = s_.width
                if s_.sink is not None:
                    last = nc.vector.tensor_scalar(sc(u, w, w + 1), s_.sink(it), 1.0, None, ALU.mult)
                    w += 1
                if last is not None:
                    last.then_inc(li, 1)
                    dve.wait_ge(li, it * loff[-1] + loff[u + 1])
                nc.vector.tensor_reduce(nmax[:, u % 2:u % 2 + 1], sc_wide(u, w), AXX, ALU.max, negate=True).then_inc(mx, 1)

            pipeline(dve, step, 2)


def rows_of(ap, it_col, width, tiles):
    return ap.rearrange("(i p) c -> p i c", p=P)[:, 0:tiles, bass.ds(it_col, width)]


def block_fox(cr):
    qT, kT, v_d, F_d = (cr.dram(n, s_) for n, s_ in (("q_T", [D, SEQ]), ("k_T", [D, SEQ]), ("v_rows", [SEQ, D]), ("f_rows", [2, HB, SEQ])))
    O = cr.dram("o_rows", [NTOK, D])
    qa, ka = cr.at(10240, 2, SEQ), cr.at(12288, 2, SEQ)
    vb = cr.at(14336, 2, NT, 2 * HD)
    p_buf, t_buf = cr.at(16384, 2, 1024), cr.at(18432, 2, NT, P)
    ob = cr.at(20480, 2, NT, HD)
    ones = cr.io["ones"][0:1, 0:SEQ]

    def loads(k, it):
        h = 2 * it + k
        return [(qa[0:HD, k], qT[bass.ds(h * HD, HD), :]), (ka[0:HD, k], kT[bass.ds(h * HD, HD), :]),
                (qa[HD:HD + 1, k], F_d[0, bass.ds(h, 1), :]), (ka[HD + 1:HD + 2, k], F_d[1, bass.ds(h, 1), :]),
                (vb[:, k], rows_of(v_d, it * (2 * HD), 2 * HD, NT))]

    steps = []
    for k in range(2):
        for i in range(NT):
            w = (i + 1) * P
            pieces = [(a, min(a + 512, w), ka[:, k, a:min(a + 512, w)]) for a in range(0, w, 512)]
            steps.append(Step(k, qa[:, k, i * P:(i + 1) * P], pieces, [(i * P, C_CAUSAL)], w,
                              [(n * P, vb[:, k, n]) for n in range(i + 1)], None, ob[:, k, i]))
    static = [(qa[HD + 1:HD + 2, k], ones) for k in range(2)] + [(ka[HD:HD + 1, k], ones) for k in range(2)]
    attention(cr, "fox", HB // 2, steps, loads, static,
              lambda k, it: (rows_of(O, (2 * it + k) * HD, HD, NT), ob[:, k]), 2, p_buf, t_buf, [qa[HD:P], ka[HD:P]])


def block_out(cr, name, w0, nt, oc, z_name, t_name, gates):
    nc = cr.nc
    O = cr.dram("o_rows", [NTOK, D])
    z_d = cr.dram(z_name, [SEQ, D]) if z_name else None
    t_d = cr.dram(t_name, [512, NTOK]) if t_name else None
    mult, tr, te, t_in, d_ok, g_mm, g_ok, link = cr.sems(name, "gated turned placed t_loaded diag gate_mm gate_copied dve")
    ld = cr.sems(name, "loaded0 loaded1")
    OT = cr.at(10240, KT, NTOK)
    orow, zrow = cr.at(20480, 2, D), cr.at(22528, 2, D)
    gate = cr.at(24576, 2, D)
    diag = cr.at(26624, 2, D)
    tmp = cr.at(28672, 2, 512)
    un = Units(cr, name)
    Xr = X(cr)
    nh = (oc + 3) // 4
    nl = 2 if z_d is not None else 1

    with nc.Block() as block:
        @block.sync
        def _(sp):
            if t_d is not None:
                sp.dma_start(OT[:, oc:KT, 0:nt * P], t_d.rearrange("(k p) n -> p k n", p=P)[:, :, 0:nt * P]).then_inc(t_in, 16)
            for i in range(nt):
                if i >= 2:
                    sp.wait_ge(tr, nh * (i - 1))
                sp.dma_start(orow[:, i % 2, 0:oc * P], O[i * P:(i + 1) * P, 0:oc * P]).then_inc(ld[i % 2], 16)
                if z_d is not None:
                    sp.dma_start(zrow[:, i % 2], z_d[i * P:(i + 1) * P, :]).then_inc(ld[i % 2], 16)
            stream(cr, sp, w0, 2, un, [nt] * 2)

        @block.tensor
        def _(pe):
            for n, g in enumerate(gates):
                pe.wait_ge(d_ok, n + 1)
                if n:
                    pe.wait_ge(g_ok, 2 * n)
                gate_rows(cr, diag[:, n], (6, 7), g_mm)
            for i in range(nt):
                pe.wait_ge(mult if z_d is not None else ld[i % 2], i + 1 if z_d is not None else 16 * (i // 2 + 1))
                for h in range(nh):
                    if i:
                        pe.wait_ge(te, nh * (i - 1) + h + 1)
                    for q in range(4):
                        k = 4 * h + q
                        last = nc.tensor.transpose(cr.bank[h][:, q * P:(q + 1) * P], orow[:, i % 2, k * P:(k + 1) * P], cr.const(C_ID))
                    last.then_inc(tr, 1)
            pe.wait_ge(te, nh * nt)
            if t_d is not None:
                pe.wait_ge(t_in, 16)
            for t in range(2):
                cr.wait_w(pe, w0 + t)
                w = cr.w(w0 + t)
                for i in range(nt):
                    product(cr, pe, un, un.bank(un.n), [(OT[:, k, i * P:(i + 1) * P], w[:, k, :]) for k in range(KT)])

        @block.scalar
        def _(act):
            for n in range(len(gates)):
                act.wait_ge(g_mm, n + 1)
                for b in range(2):
                    nc.scalar.activation(gate[:, n, b * 512:(b + 1) * 512], cr.bank[6 + b][:, :], ACT.Copy).then_inc(g_ok, 1)
            for i in range(nt):
                for h in range(nh):
                    act.wait_ge(tr, nh * i + h + 1)
                    nc.scalar.activation(OT[:, 4 * h:4 * h + 4, i * P:(i + 1) * P], cr.bank[h][:, :].rearrange("p (k n) -> p k n", k=4),
                                         ACT.Copy).then_inc(te, 1)

        @block.vector
        def _(dve):
            ln = Link(dve, link)
            for n, (col, var) in enumerate(gates):
                gate_diag(cr, diag[:, n], col, var, d_ok)
            if z_d is not None:
                for i in range(nt):
                    dve.wait_ge(ld[i % 2], 16 * nl * (i // 2 + 1))
                    nc.vector.tensor_tensor(orow[:, i % 2], orow[:, i % 2], zrow[:, i % 2], ALU.mult).then_inc(mult, 1)
            dve.wait_ge(g_ok, 2 * len(gates))
            for u in range(2 * nt):
                t, i = u // nt, u % nt
                dve.wait_ge(un.full, u + 1)
                g = gate[:, 1 if i >= NT else 0, t * 512:(t + 1) * 512]
                residual_add(cr, dve, ln, un, u, tmp[:, u % 2], g, Xr[:, i, t * 512:(t + 1) * 512])


def block_bout(cr):
    block_out(cr, "bout", W_BOUT, NT, KT, "zb_rows", None, [(MC_B + 16, V_C)])


def variant(lat, ctx):
    return lambda i: lat if i < NT else ctx


def rope(nc, ln, x1, x2, cos, sin, o1, o2, ta, tb):
    tt = nc.vector.tensor_tensor
    tt(o1, x1, cos, ALU.mult)
    tt(ta, x2, sin, ALU.mult)
    tt(o2, x2, cos, ALU.mult)
    ln(tt(tb, x1, sin, ALU.mult))
    tt(o1, o1, ta, ALU.subtract)
    return tt(o2, o2, tb, ALU.add)


def block_ein(cr):
    nc, io = cr.nc, cr.io
    kT, qT, v_d, s_T = (cr.dram(n, s_) for n, s_ in (("ek_T", [P, NTOK]), ("eq_T", [512, NTOK]), ("ev_rows", [NTOK, P]), ("s_T", [512, NTOK])))
    x_in, c_in, link, turned, placed, v_st, s_bn, s_std, s_vn, s_mm, s_s = cr.sems(
        "ein", "ctx_loaded tables_loaded dve turned placed v_stored moments std v_normed mixed gated")
    kst_, sst_ = cr.sems("ein", "t_stored0 t_stored1"), cr.sems("ein", "s_stored0 s_stored1")
    Xr = X(cr)
    hT = cr.at(10240, KT, NTOK)
    raw = cr.at(22528, NTC, 768)
    uT = cr.at(30208, 4, NTOK)
    vrow = cr.at(35328, 2, 512)
    kst = vrow
    wsT = cr.at(36352, 4, P)
    bs = cr.at(36864, 4, P)
    gln = cr.at(37376, 512)
    tab = cr.at(37888, NT, 2, 32)
    vn = cr.at(20480, 2, 512)
    sst = cr.at(21504, 2, 4, P)
    ta, tb = cr.small[:, 340:596], cr.small[:, 596:852]
    mom = cr.small[:, 852:892]
    un = Units(cr, "ein")
    nrm = Norm(cr, "ein", NTC, lambda i: Xr[:, i], [cr.at(20480, D), cr.at(20480 + D, D)],
               [(lambda k, i: hT[:, k, i * P:(i + 1) * P], variant(cr.gain(GS_1L0), cr.gain(GS_1C0)),
                 variant(cr.shift(MC_L, V_LAT), cr.shift(MC_L, V_CTX)))], cr.small[:, 300:340])
    TOK = [(0, 512), (512, 1024), (1024, NTOK)]
    GROUPS_T = [(0, 4), (4, 8), (8, 10)]
    NR = 2 * NTC
    NU = 4 * 3

    with nc.Block() as block:
        @block.sync
        def _(sp):
            sp.dma_start(Xr[:, NT:NTC], io["ctx"].rearrange("b (i p) d -> (b p) i d", p=P)).then_inc(x_in, 16)
            for to, of in ((wsT, io["sgu_w"]), (bs.rearrange("p g q -> p (g q)"), io["sgu_b"].broadcast_to([P, 512])),
                           (gln, io["sgu_g"].broadcast_to([P, 512])), (tab, io["rope_a"])):
                sp.dma_start(to, of).then_inc(c_in, 16)
            stream(cr, sp, W_EIN, 4, un, [NTC, NTC, NU, NTC])

        @block.gpsimd
        def _(pool):
            pool.wait_ge(un.empty, NTC)
            pool.dma_start(v_d.rearrange("(i p) c -> p i c", p=P), raw[:, :, 640:768]).then_inc(v_st, 16)
            for v in range(15):
                c, (a, b) = v // 3, GROUPS_T[v % 3]
                dst = kT if c == 0 else qT[(c - 1) * P:c * P, :]
                pool.wait_ge(placed, v + 1)
                pool.dma_start(dst[:, a * P:b * P], kst[:, v % 2, 0:(b - a) * P]).then_inc(kst_[v % 2], 16)
            for i in range(NTC):
                pool.wait_ge(s_s, i + 1)
                pool.dma_start(s_T.rearrange("(g d) n -> d g n", d=P)[:, :, i * P:(i + 1) * P], sst[:, i % 2]).then_inc(sst_[i % 2], 16)
            pool.wait_ge(v_st, 16)
            for k in range(2):
                pool.wait_ge(kst_[k], 16 * (8 - k))
                pool.wait_ge(sst_[k], 16 * 5)

        @block.tensor
        def _(pe):
            nrm.pe(pe, nrm.LEAD)
            for t in range(2):
                cr.wait_w(pe, W_EIN + t)
                w = cr.w(W_EIN + t)
                n = 512 if t else 256
                for i in range(NTC):
                    if t == 0:
                        nrm.tile_ready(pe, i)
                    product(cr, pe, un, un.bank(un.n)[:, 0:n], [(hT[:, k, i * P:(i + 1) * P], w[:, k, 0:n]) for k in range(KT)])
                    if t == 0:
                        nrm.pe_ahead(pe, i)
            cr.wait_w(pe, W_EIN + 2)
            w = cr.w(W_EIN + 2)

            def turn(v):
                c, (a, b) = v // 3, GROUPS_T[v % 3]
                if v == 0:
                    pe.wait_ge(un.empty, NR)
                if v >= 2:
                    pe.wait_ge(placed, v - 1)
                for i in range(a, b):
                    last = nc.tensor.transpose(cr.bank[6 + v % 2][:, (i - a) * P:(i - a + 1) * P], raw[:, i, c * P:(c + 1) * P], cr.const(C_ID))
                last.then_inc(turned, 1)

            for m in range(4):
                for a, b in TOK:
                    product(cr, pe, un, un.bank(un.n)[:, 0:b - a], [(w[:, k, m * P:(m + 1) * P], hT[:, k, a:b]) for k in range(KT)])
                    if un.n > NR + 1:
                        turn(un.n - NR - 2)
            for v in range(NU - 1, 15):
                turn(v)
            cr.wait_w(pe, W_EIN + 3)
            w = cr.w(W_EIN + 3)
            pe.wait_ge(placed, 15)

            def mix(i):
                pe.wait_ge(s_vn, i + 1)
                if i >= 2:
                    pe.wait_ge(s_s, i - 1)
                for g in range(4):
                    last = nc.tensor.matmul(cr.bank[6 + i % 2][:, g * P:(g + 1) * P], vn[:, i % 2, g * P:(g + 1) * P], wsT[:, g],
                                            start=True, stop=True)
                last.then_inc(s_mm, 1)

            for i in range(NTC):
                product(cr, pe, un, un.bank(un.n), [(hT[:, k, i * P:(i + 1) * P], w[:, k, :]) for k in range(KT)])
                if i:
                    mix(i - 1)
            mix(NTC - 1)

        @block.scalar
        def _(act):
            act.wait_ge(x_in, 16)
            nrm.act(act)
            u0 = NR
            act.wait_ge(un.empty, NR)
            for n in range(NU):
                m, (a, b) = n // 3, TOK[n % 3]
                act.wait_ge(un.full, u0 + n + 1)
                nc.scalar.activation(uT[:, m, a:b], un.bank(u0 + n)[:, 0:b - a], ACT.Gelu_apprx_tanh).then_inc(un.empty, 1)
            act.wait_ge(kst_[0], 16 * 8)
            act.wait_ge(kst_[1], 16 * 7)
            u0 += NU
            for i in range(NTC):
                act.wait_ge(un.full, u0 + i + 1)
                if i >= 2:
                    act.wait_ge(s_vn, i - 1)
                nc.scalar.activation(vrow[:, i % 2], un.bank(u0 + i), ACT.Gelu_apprx_tanh).then_inc(un.empty, 1)
                act.wait_ge(s_bn, i + 1)
                nc.scalar.activation(mom[:, 12 + i % 2:13 + i % 2], mom[:, 10 + i % 2:11 + i % 2], ACT.Sqrt).then_inc(s_std, 1)

        @block.vector
        def _(dve):
            ln = Link(dve, link)
            tt, ts = nc.vector.tensor_tensor, nc.vector.tensor_scalar
            nrm.dve_lead(dve)
            dve.wait_ge(c_in, 64)

            def turn(i, ps, lo, heads):
                x = ps.rearrange("p (h e d) -> p h e d", h=heads, e=2)
                o = raw[:, i, lo:lo + heads * HD].rearrange("p (h e d) -> p h e d", h=heads, e=2)
                c, s_ = (tab[:, i, n].unsqueeze(1).broadcast_to([P, heads, 32]) for n in range(2))
                n = heads * 32
                t1, t2 = (v[:, 0:n].rearrange("p (h d) -> p h d", h=heads) for v in (ta, tb))
                return rope(nc, ln, x[:, :, 0], x[:, :, 1], c, s_, o[:, :, 0], o[:, :, 1], t1, t2)

            for u in range(NR):
                t, i = u // NTC, u % NTC
                if t == 0:
                    nrm.dve_ahead(dve, i)
                dve.wait_ge(un.full, u + 1)
                ps = un.bank(u)
                if t == 0:
                    if i < NT:
                        ln(turn(i, ps[:, 0:P], 0, 2))
                    else:
                        ln(nc.vector.tensor_copy(raw[:, i, 0:P], ps[:, 0:P]))
                    nc.vector.tensor_copy(raw[:, i, 640:768], ps[:, P:2 * P]).then_inc(un.empty, 1)
                else:
                    if i < NT:
                        ln(turn(i, ps, P, 8))
                    else:
                        ln(nc.vector.tensor_copy(raw[:, i, P:640], ps))
                    ts(raw[:, i, P:640], raw[:, i, P:640], HD ** -0.5, None, ALU.mult).then_inc(un.empty, 1)
            for v in range(15):
                a, b = GROUPS_T[v % 3]
                dve.wait_ge(turned, v + 1)
                if v >= 2:
                    dve.wait_ge(kst_[v % 2], 16 * (v // 2))
                nc.vector.tensor_copy(kst[:, v % 2, 0:(b - a) * P], cr.bank[6 + v % 2][:, 0:(b - a) * P]).then_inc(placed, 1)
            u0 = NR + NU
            for i in range(NTC):
                dve.wait_ge(un.empty, u0 + i + 1)
                vr = vrow[:, i % 2]
                ln(nc.vector.bn_stats(mom[:, 0:6], vr))
                ln(nc.vector.bn_aggr(mom[:, 6:8], mom[:, 0:6]))
                ts(mom[:, 10 + i % 2:11 + i % 2], mom[:, 7:8], EPS, None, ALU.add).then_inc(s_bn, 1)
                dve.wait_ge(s_std, i + 1)
                ln(nc.vector.reciprocal(mom[:, 14:15], mom[:, 12 + i % 2:13 + i % 2]))
                if i >= 2:
                    dve.wait_ge(s_mm, i - 1)
                ln(ts(vn[:, i % 2], vr, mom[:, 6:7], mom[:, 14:15], ALU.subtract, ALU.mult))
                tt(vn[:, i % 2], vn[:, i % 2], gln, ALU.mult).then_inc(s_vn, 1)
                dve.wait_ge(s_mm, i + 1)
                if i >= 2:
                    dve.wait_ge(sst_[i % 2], 16 * (i // 2))
                ln(tt(sst[:, i % 2], cr.bank[6 + i % 2].rearrange("p (g q) -> p g q", g=4), bs, ALU.add))
                tt(sst[:, i % 2], sst[:, i % 2], uT[:, :, i * P:(i + 1) * P], ALU.mult).then_inc(s_s, 1)


def block_window(cr):
    kT, qT, v_d = cr.dram("ek_T", [P, NTOK]), cr.dram("eq_T", [512, NTOK]), cr.dram("ev_rows", [NTOK, P])
    O = cr.dram("o_rows", [NTOK, D])
    qa, ka = cr.at(10240, 2, NTOK), cr.at(12800, 2, NTOK)
    vb = cr.at(15360, NTC, 2 * HD)
    p_buf, t_buf = cr.at(16640, 2, 1024), cr.at(18688, 2, NT, P)
    ob = cr.at(20736, 2, NTC, HD)
    sink = cr.at(22016, HW_)
    g = HW_ // 2

    def loads(k, it):
        return [(qa[0:HD, k], qT[bass.ds((g * k + it) * HD, HD), :])]

    static = [(sink, cr.io["sink"].broadcast_to([P, HW_])), (vb, rows_of(v_d, 0, 2 * HD, NTC))]
    static += [(ka[0:HD, k], kT[k * HD:(k + 1) * HD, :]) for k in range(2)]
    steps = []
    for k in range(2):
        keys = ka[:, k]
        snk = lambda it, k=k: sink[:, bass.ds(it + g * k, 1)]
        for i in range(NTC):
            pieces, masks, w = [(0, CTX, keys[:, SEQ:NTOK])], [], CTX
            pv = [(0, vb[:, NT]), (P, vb[:, NT + 1])]
            if i < NT:
                for b in range(max(i - 1, 0), min(i + 1, NT - 1) + 1):
                    if b != i:
                        masks.append((w, C_PREV if b < i else C_CAUSAL))
                    pieces.append((w, w + P, keys[:, b * P:(b + 1) * P]))
                    pv.append((w, vb[:, b]))
                    w += P
            steps.append(Step(k, qa[:, k, i * P:(i + 1) * P], pieces, masks, w, pv, snk, ob[:, k, i]))
    attention(cr, "win", g, steps, loads, static,
              lambda k, it: (rows_of(O, (g * k + it) * HD, HD, NTC), ob[:, k]), 2, p_buf, t_buf, [qa[HD:P], ka[HD:P]])


def block_eout(cr):
    block_out(cr, "eout", W_EOUT, NTC, 4, None, "s_T", [(MC_L + 16, V_LAT), (MC_L + 16, V_CTX)])


S_IX, S_IXC, S_GT, S_GTC = 500, 516, 532, 548


def block_router(cr, l):
    nc, io = cr.nc, cr.io
    nt = NTC if l == 0 else NT
    name = f"router{l}"
    x_d, xn_d = cr.dram("x_rows", [NTOK, D]), cr.dram("xn_rows", [NTOK, D])
    x_st, r_in, lg, s_m, s_e, tr, link, tk, ix = cr.sems(name, "x_stored w_loaded logits shifted exp turned dve chosen columns")
    Xr = X(cr)
    hT = cr.at(10240, KT, NTOK)
    o = 22528
    rw = cr.at(o, KT, NE)
    af = cr.at(o + 128, nt, NE)
    mx, sm = cr.at(o + 300, nt), cr.at(o + 320, nt)
    w0, w1 = cr.at(o + 512, NTOK), cr.at(o + 512 + NTOK, NTOK)
    nv = CAP + CAPC
    vals = cr.at(o + 3200, nv)
    idx = cr.at(o + 3400, nv).bitcast(U32)
    idf = cr.at(o + 3600, nv)
    gs, gc = (GS_2L0, GS_2C0) if l == 0 else (GS_2L1, GS_2L1)
    sh = MC_L + 48 * l + 24
    nrm = Norm(cr, name, nt, lambda i: Xr[:, i], [cr.at(20480, D), cr.at(20480 + D, D)],
               [(lambda k, i: hT[:, k, i * P:(i + 1) * P], variant(cr.gain(gs), cr.gain(gc)),
                 variant(cr.shift(sh, V_LAT), cr.shift(sh, V_CTX)))], cr.small[:, 300:340],
               store=lambda i: xn_d[i * P:(i + 1) * P, :])

    with nc.Block() as block:
        @block.sync
        def _(sp):
            sp.dma_start(rw, io["router"][:, l]).then_inc(r_in, 16)
            sp.dma_start(x_d.rearrange("(i p) d -> p i d", p=P)[:, 0:nt], Xr[:, 0:nt]).then_inc(x_st, 16)
            sp.wait_ge(x_st, 16)

        @block.gpsimd
        def _(pool):
            nrm.keep(pool)
            nrm.kept(pool)

        @block.tensor
        def _(pe):
            nrm.pe(pe, nrm.LEAD)
            pe.wait_ge(r_in, 16)
            for i in range(nt):
                nrm.tile_ready(pe, i)
                for k in range(KT):
                    last = nc.tensor.matmul(cr.bank[2][:, i * NE:(i + 1) * NE], hT[:, k, i * P:(i + 1) * P], rw[:, k],
                                            start=(k == 0), stop=(k == KT - 1))
                if i == nt - 1:
                    last.then_inc(lg, 1)
                nrm.pe_ahead(pe, i)
            pe.wait_ge(s_m, 2)
            for i in range(nt):
                last = nc.tensor.transpose(cr.bank[3 + i // 4][0:NE, (i % 4) * P:(i % 4 + 1) * P], af[:, i], cr.const(C_ID))
            last.then_inc(tr, 1)
            pe.wait_ge(tk, 1)
            i16 = cr.const(C_ID)[0:NE, 0:NE]
            last = nc.tensor.transpose(cr.bank[6][:, 0:NE], idf[0:NE, 0:CAP], i16)
            last = nc.tensor.transpose(cr.bank[6][:, NE:2 * NE], vals[0:NE, 0:CAP], i16)
            if l == 0:
                last = nc.tensor.transpose(cr.bank[6][0:CAPC, 2 * NE:3 * NE], idf[0:NE, CAP:nv], i16)
                last = nc.tensor.transpose(cr.bank[6][0:CAPC, 3 * NE:4 * NE], vals[0:NE, CAP:nv], i16)
            last.then_inc(ix, 1)

        @block.scalar
        def _(act):
            nrm.act(act)
            act.wait_ge(s_m, 1)
            nc.scalar.activation(af, af, ACT.Exp).then_inc(s_e, 1)

        @block.vector
        def _(dve):
            ln = Link(dve, link)
            tt, ts = nc.vector.tensor_tensor, nc.vector.tensor_scalar
            nrm.dve(dve)
            dve.wait_ge(lg, 1)
            ps = cr.bank[2][:, 0:nt * NE].rearrange("p (i e) -> p i e", e=NE)
            bc = lambda v: v.unsqueeze(2).broadcast_to([P, nt, NE])
            ln(nc.vector.tensor_reduce(mx, ps, AXX, ALU.max))
            tt(af, ps, bc(mx), ALU.subtract).then_inc(s_m, 1)
            dve.wait_ge(s_e, 1)
            ln(nc.vector.tensor_reduce(sm, af, AXX, ALU.add))
            ln(nc.vector.reciprocal(sm, sm))
            tt(af, af, bc(sm), ALU.mult).then_inc(s_m, 1)
            dve.wait_ge(tr, 1)
            for b in range((nt + 3) // 4):
                n = min(4, nt - 4 * b) * P
                ln(nc.vector.tensor_copy(w0[0:NE, b * 512:b * 512 + n], cr.bank[3 + b][0:NE, 0:n]))
            for lo, n, at, cap in ((0, SEQ, 0, CAP), (SEQ, CTX, CAP, CAPC))[:2 - l]:
                a, b = w0[0:NE, lo:lo + n], w1[0:NE, lo:lo + n]
                for r in range(cap // 8):
                    v8, i8 = vals[0:NE, at + 8 * r:at + 8 * r + 8], idx[0:NE, at + 8 * r:at + 8 * r + 8]
                    ln(nc.vector.max(v8, a))
                    ln(nc.vector.max_index(i8, v8, a))
                    ln(nc.vector.match_replace(b, v8, a, -1.0))
                    a, b = b, a
            nn = nv if l == 0 else CAP
            ln(nc.vector.tensor_copy(idf[0:NE, 0:nn], idx[0:NE, 0:nn]))
            if l == 0:
                ln(ts(idf[0:NE, CAP:nv], idf[0:NE, CAP:nv], float(SEQ), None, ALU.add))
            nc.vector.tensor_copy(mx[0:NE, 0:1], idf[0:NE, 0:1]).then_inc(tk, 1)
            dve.wait_ge(ix, 1)
            sm_ = cr.small
            ln(nc.vector.tensor_copy(sm_[:, S_IX:S_IX + NE].bitcast(U32), cr.bank[6][:, 0:NE]))
            ln(nc.vector.tensor_copy(sm_[:, S_GT:S_GT + NE], cr.bank[6][:, NE:2 * NE]))
            if l == 0:
                ln(nc.vector.tensor_copy(sm_[0:CAPC, S_IXC:S_IXC + NE].bitcast(U32), cr.bank[6][0:CAPC, 2 * NE:3 * NE]))
                ln(nc.vector.tensor_copy(sm_[0:CAPC, S_GTC:S_GTC + NE], cr.bank[6][0:CAPC, 3 * NE:4 * NE]))


def block_moe(cr, l):
    nc = cr.nc
    w0 = W_MOE0 if l == 0 else W_MOE1
    name = f"moe{l}"
    n = CAP + CAPC if l == 0 else CAP
    parts = [(0, CAP, V_LAT)] + ([(CAP, n, V_CTX)] if l == 0 else [])
    TY = 2 * len(parts)
    TX = 4
    TB = TY + TX
    GX = 16 * len(parts)
    a_r, a_e, b_r, b_e, t_r, t_e, c_r, c_e, gx, sc = cr.sems(
        name, "a_ready a_taken b_ready b_taken turned placed y_ready y_taken gathered scattered")
    x_d, xn_d = cr.dram("x_rows", [NTOK, D]), cr.dram("xn_rows", [NTOK, D])
    xg, xgc = cr.at(0, D), cr.at(1024, D)
    xT = cr.at(2048, KT, n)
    sa = cr.at(3400, 2, 2, n)
    hid = cr.at(4096, KT, n)
    yT = cr.at(5400, KT, n)
    yr, yrc = cr.at(6700, D), cr.at(7724, D)
    src, dst = (xg, xgc), (yr, yrc)
    rows = (P, CAPC)
    sm = cr.small
    ixs = (sm[:, S_IX:S_IX + NE].bitcast(U32), sm[0:CAPC, S_IXC:S_IXC + NE].bitcast(U32))
    gts = (sm[:, S_GT:S_GT + NE], sm[0:CAPC, S_GTC:S_GTC + NE])
    gcol, scol, mcol = (GS_2L0 if l == 0 else GS_2L1), MC_L + 48 * l + 24, MC_L + 48 * l + 40

    def t_base(e):
        return TX if isinstance(e, int) and e == 0 else TX + TX - TB + TB * e

    TBANK, CBANK = (4, 5), (6, 7)

    def half(bank):
        return cr.bank[bank][:, 0:2 * n].rearrange("p (c n) -> p c n", c=2)

    with nc.Block() as block:
        @block.sync
        def _(sp):
            def refill(e):
                for j, (sem, k) in enumerate(((a_r, 2), (b_r, 2), (a_r, 4), (b_r, 4), (c_r, 2), (c_r, 4))):
                    sp.wait_ge(sem, 4 * e + k)
                    t = w0 + 6 * e + j + RING
                    if isinstance(e, int):
                        cr.load_w(sp, t)
                    else:
                        slot = (w0 + j) % RING
                        sp.dma_start(cr.ring[:, slot, :], cr.io["wstream"][bass.ds(t, 1)].rearrange("a p n -> (a p) n")).then_inc(cr.loaded[slot], 16)
            with sp.Fori(0, NE - 1) as e:
                refill(e)
            refill(NE - 1)

        @block.gpsimd
        def _(pool):
            def gather(e):
                if e:
                    pool.wait_ge(t_r, TX if e == 1 else t_base(e - 1))
                for p in range(len(parts)):
                    pool.indirect_dma_start(out=src[p][0:rows[p], :], out_offset=None, in_=xn_d[:, :],
                                            in_offset=bass.IndirectOffsetOnAxis(ap=ixs[p][0:rows[p], e:e + 1], axis=0)).then_inc(gx, 16)

            def scatter(e):
                pool.wait_ge(t_e, t_base(e + 1) + TY if e + 1 < NE else t_base(NE - 1) + 2 * TY)
                if e:
                    pool.wait_ge(sc, GX * e)
                for p in range(len(parts)):
                    pool.indirect_dma_start(out=x_d[:, :], out_offset=bass.IndirectOffsetOnAxis(ap=ixs[p][0:rows[p], e:e + 1], axis=0),
                                            in_=dst[p][0:rows[p], :], in_offset=None, compute_op=ALU.add).then_inc(sc, 16)

            gather(0)
            gather(1)
            for e in range(NE):
                if e + 2 < NE:
                    gather(e + 2)
                scatter(e)
            pool.wait_ge(sc, GX * NE)

        def turned_units(e, with_y, with_x):
            b = t_base(e)
            ys = [("y", v, b + v) for v in range(TY)] if with_y else []
            xs = [("x", v, b + (TY if with_y else 0) + v) for v in range(TX)] if with_x else []
            return ys, xs

        @block.tensor
        def _(pe):
            def up(e, j, bank0, ready, taken, first):
                slot = (w0 + j) % RING
                pe.wait_ge(cr.loaded[slot], 16 * ((w0 + j) // RING + 1) + 32 * e)
                w = cr.w(slot)
                for v in range(2):
                    k0 = 4 * e + first + v
                    if not (isinstance(e, int) and e == 0 and first + v < 2):
                        pe.wait_ge(taken, k0 - 1)
                    for c in range(2):
                        m = 2 * v + c
                        for k in range(KT):
                            last = nc.tensor.matmul(half(bank0 + v)[:, c], w[:, k, m * P:(m + 1) * P], xT[:, k, :],
                                                    start=(k == 0), stop=(k == KT - 1))
                    last.then_inc(ready, 1)

            def turn(units, e):
                for kind, v, at in units:
                    pe.wait_ge(t_e, at - 1)
                    bank = cr.bank[TBANK[v % 2]]
                    if kind == "y":
                        p, h = v // 2, v % 2
                        if v == 0:
                            pe.wait_ge(c_e, 4 * e)
                        a, b, _ = parts[p]
                        for q in range(4):
                            last = nc.tensor.transpose(bank[0:b - a, q * P:(q + 1) * P], yT[:, 4 * h + q, a:b], cr.const(C_ID))
                    else:
                        if v == 0:
                            pe.wait_ge(gx, GX * (e + 2))
                        for c in range(2):
                            k = 2 * v + c
                            for p, (a, b, _) in enumerate(parts):
                                r = b - a
                                last = nc.tensor.transpose(half(TBANK[v % 2])[:, c, a:b], src[p][0:r, k * P:(k + 1) * P], cr.const(C_ID)[0:r, 0:r])
                    last.then_inc(t_r, 1)

            def down(e):
                pe.wait_ge(b_e, 4 * e + 4)
                for j in (4, 5):
                    slot = (w0 + j) % RING
                    pe.wait_ge(cr.loaded[slot], 16 * ((w0 + j) // RING + 1) + 32 * e)
                    w = cr.w(slot)
                    for v in range(2):
                        at = 4 * e + 2 * (j - 4) + v
                        if not (isinstance(e, int) and e == 0 and j == 4):
                            pe.wait_ge(c_e, at - 1)
                        for c in range(2):
                            m = 2 * v + c
                            for k in range(KT):
                                last = nc.tensor.matmul(half(CBANK[v])[:, c], w[:, k, m * P:(m + 1) * P], hid[:, k, :],
                                                        start=(k == 0), stop=(k == KT - 1))
                        last.then_inc(c_r, 1)

            def body(e, with_y, with_x):
                ys, xs = turned_units(e, with_y, with_x)
                pe.wait_ge(t_e, t_base(e))
                up(e, 0, 0, a_r, a_e, 0)
                turn(ys, e)
                up(e, 1, 2, b_r, b_e, 0)
                up(e, 2, 0, a_r, a_e, 2)
                up(e, 3, 2, b_r, b_e, 2)
                turn(xs, e)
                down(e)

            for v in range(TX):
                if v >= 2:
                    pe.wait_ge(t_e, v - 1)
                if v == 0:
                    pe.wait_ge(gx, GX)
                for c in range(2):
                    for p, (a, b, _) in enumerate(parts):
                        k, r = 2 * v + c, b - a
                        last = nc.tensor.transpose(half(TBANK[v % 2])[:, c, a:b], src[p][0:r, k * P:(k + 1) * P], cr.const(C_ID)[0:r, 0:r])
                last.then_inc(t_r, 1)
            body(0, False, True)
            with pe.Fori(1, NE - 1) as e:
                body(e, True, True)
            body(NE - 1, True, False)
            turn([("y", v, t_base(NE - 1) + TY + v) for v in range(TY)], NE)

        @block.scalar
        def _(act):
            def gates(e, first):
                for v in range(first, first + 2):
                    act.wait_ge(a_r, 4 * e + (v + 1))
                    if not (isinstance(e, int) and e == 0 and v < 2):
                        act.wait_ge(b_e, 4 * e + (v - 1))
                    nc.scalar.activation(sa[:, v % 2], half(v % 2), ACT.Silu).then_inc(a_e, 1)

            def outs(e):
                for v in range(4):
                    act.wait_ge(c_r, 4 * e + (v + 1))
                    if v == 0:
                        act.wait_ge(t_r, t_base(e) + (0 if isinstance(e, int) and e == 0 else TY))
                    for c in range(2):
                        k = 2 * v + c
                        for a, b, var in parts:
                            last = nc.scalar.activation(yT[:, k, a:b], half(CBANK[v % 2])[:, c, a:b], ACT.Copy, scale=cr.shift(mcol, var)(k))
                    last.then_inc(c_e, 1)

            def body(e):
                gates(e, 0)
                gates(e, 2)
                outs(e)

            body(0)
            with act.Fori(1, NE - 1) as e:
                body(e)
            body(NE - 1)

        @block.vector
        def _(dve):
            ts = nc.vector.tensor_scalar

            def place(units, e):
                for kind, v, at in units:
                    dve.wait_ge(t_r, at + 1)
                    bank = cr.bank[TBANK[v % 2]]
                    if kind == "y":
                        p, h = v // 2, v % 2
                        if v == 0 and not (isinstance(e, int) and e == 1):
                            dve.wait_ge(sc, GX * (e - 1))
                        r = rows[p]
                        g = gts[p][0:r, e - 1:e] if isinstance(e, int) else gts[p][0:r, bass.ds(e - 1, 1)]
                        last = ts(dst[p][0:r, h * 512:(h + 1) * 512], bank[0:r, :], g, None, ALU.mult)
                    else:
                        for c in range(2):
                            k = 2 * v + c
                            for a, b, var in parts:
                                gc = gcol + (var == V_CTX)
                                last = ts(xT[:, k, a:b], half(TBANK[v % 2])[:, c, a:b], cr.gain(gc)(k), cr.shift(scol, var)(k), ALU.mult, ALU.add)
                    last.then_inc(t_e, 1)

            def hidden(e, first):
                for v in range(first, first + 2):
                    dve.wait_ge(a_e, 4 * e + (v + 1))
                    dve.wait_ge(b_r, 4 * e + (v + 1))
                    nc.vector.tensor_tensor(hid[:, 2 * v:2 * v + 2], sa[:, v % 2], half(2 + v % 2), ALU.mult).then_inc(b_e, 1)

            def body(e, with_y, with_x):
                ys, xs = turned_units(e, with_y, with_x)
                place(ys, e)
                hidden(e, 0)
                hidden(e, 2)
                place(xs, e)

            place([("x", v, v) for v in range(TX)], 0)
            body(0, False, True)
            body(1, True, True)
            with dve.Fori(2, NE - 1) as e:
                body(e, True, True)
            body(NE - 1, True, False)
            place([("y", v, t_base(NE - 1) + TY + v) for v in range(TY)], NE)


O_RAW, O_RAWQ = 10240, 10240 + NTC * 288


def block_oin(cr):
    nc, io = cr.nc, cr.io
    x_d, c_T = cr.dram("x_rows", [NTOK, D]), cr.dram("c_T", [512, NTOK])
    x_in, t_in, link, s_ss, s_var, s_std, s_hh, s_cv = cr.sems(
        "oin", "x_loaded tables_loaded dve squares variance std products conv")
    c_st = cr.sems("oin", "c_stored0 c_stored1")
    Xr = X(cr)
    raw, rawq = cr.at(O_RAW, NTC, 288), cr.at(O_RAWQ, NT, 384)
    hT = cr.at(16192, KT, NTOK)
    gb, gc = cr.at(28480, 2, SEQ), cr.at(30528, 2, SEQ)
    ub = cr.at(32576, SEQ + 2)
    co = cr.at(33604, 2, SEQ)
    junk = cr.at(35652, 2, 384)
    tab = cr.at(36420, NT, 2, 16)
    hh = cr.at(36676, SEQ)
    st = cr.small[:, 360:440].rearrange("p (n i) -> p n i", n=4)
    tmp = [cr.small[:, 560 + 80 * n:640 + 80 * n] for n in range(4)]
    un = Units(cr, "oin")
    nrm = Norm(cr, "oin", NTC, lambda i: Xr[:, i], [cr.at(26432, D), cr.at(26432 + D, D)],
               [(lambda k, i: hT[:, k, i * P:(i + 1) * P], variant(cr.gain(GS_1L1), cr.gain(GS_1C1)),
                 variant(cr.shift(MC_L + 48, V_LAT), cr.shift(MC_L + 48, V_CTX)))], cr.small[:, 300:340])
    NRW = NTC + NT
    convw = lambda s_, m: cr.cols[:, 15 + 4 * s_ + m:16 + 4 * s_ + m]

    with nc.Block() as block:
        @block.sync
        def _(sp):
            sp.dma_start(Xr, x_d.rearrange("(i p) d -> p i d", p=P)).then_inc(x_in, 16)
            sp.dma_start(tab, io["rope_c"]).then_inc(t_in, 16)
            stream(cr, sp, W_OIN, 5, un, [NTC, NT, 8, 8, 8])

        @block.gpsimd
        def _(pool):
            for m in range(4):
                pool.wait_ge(s_cv, m + 1)
                pool.dma_start(c_T[m * P:(m + 1) * P, 0:SEQ], co[:, m % 2]).then_inc(c_st[m % 2], 16)
            for k in range(2):
                pool.wait_ge(c_st[k], 32)

        @block.tensor
        def _(pe):
            nrm.pe(pe, nrm.LEAD)
            for t, n, cnt in ((0, 288, NTC), (1, 384, NT)):
                cr.wait_w(pe, W_OIN + t)
                w = cr.w(W_OIN + t)
                for i in range(cnt):
                    if t == 0:
                        nrm.tile_ready(pe, i)
                    product(cr, pe, un, un.bank(un.n)[:, 0:n], [(hT[:, k, i * P:(i + 1) * P], w[:, k, 0:n]) for k in range(KT)])
                    if t == 0:
                        nrm.pe_ahead(pe, i)
            for t in range(2, 5):
                cr.wait_w(pe, W_OIN + t)
                w = cr.w(W_OIN + t)
                for m in range(4):
                    for h in range(2):
                        product(cr, pe, un, un.bank(un.n), [(w[:, k, m * P:(m + 1) * P], hT[:, k, h * 512:(h + 1) * 512]) for k in range(KT)])

        @block.scalar
        def _(act):
            act.wait_ge(x_in, 16)
            nrm.act_lead(act)
            for u in range(NRW):
                q, i = u >= NTC, u % NTC
                if not q:
                    nrm.act_ahead(act, i)
                n, full = (384, 384) if q else (256, 288)
                act.wait_ge(un.full, u + 1)
                if u >= 2:
                    act.wait_ge(s_ss, u - 1)
                nc.scalar.activation(junk[:, u % 2, 0:n], un.bank(u)[:, 0:n], ACT.Square, accum_out=st[:, 0, u:u + 1]).then_inc(s_ss, 1)
                nc.scalar.activation((rawq if q else raw)[:, i, 0:full], un.bank(u)[:, 0:full], ACT.Copy).then_inc(un.empty, 1)
            act.wait_ge(s_var, 1)
            nc.scalar.activation(st[:, 2, 0:NRW], st[:, 1, 0:NRW], ACT.Sqrt).then_inc(s_std, 1)
            for v in range(24):
                s_, h = v // 2, v % 2
                m, kind = s_ // 3, s_ % 3
                act.wait_ge(un.full, NRW + v + 1)
                if kind == 2 and m:
                    act.wait_ge(s_hh, m)
                if kind == 0 and m >= 2:
                    act.wait_ge(s_cv, m - 1)
                to = (gb[:, m % 2], gc[:, m % 2], hh)[kind]
                nc.scalar.activation(to[:, h * 512:(h + 1) * 512], un.bank(NRW + v), ACT.Copy).then_inc(un.empty, 1)

        @block.vector
        def _(dve):
            ln = Link(dve, link)
            tt, ts, stt = nc.vector.tensor_tensor, nc.vector.tensor_scalar, nc.vector.scalar_tensor_tensor
            nrm.dve(dve)
            dve.wait_ge(s_ss, NRW)
            ts(st[:, 1, 0:NTC], st[:, 0, 0:NTC], 1.0 / 256, EPS, ALU.mult, ALU.add)
            ts(st[:, 1, NTC:NRW], st[:, 0, NTC:NRW], 1.0 / 384, EPS, ALU.mult, ALU.add).then_inc(s_var, 1)
            dve.wait_ge(s_std, 1)
            ln(nc.vector.reciprocal(st[:, 3, 0:NRW], st[:, 2, 0:NRW]))
            dve.wait_ge(un.empty, NRW)
            for i in range(NTC):
                ts(raw[:, i, 0:256], raw[:, i, 0:256], st[:, 3, i:i + 1], None, ALU.mult)
            for i in range(NT):
                ts(rawq[:, i], rawq[:, i], st[:, 3, NTC + i:NTC + i + 1], None, ALU.mult)
            dve.wait_ge(t_in, 16)
            for i0 in range(0, NT, 4):
                k4 = raw[:, i0:i0 + 4, 256:288]
                c, s_ = tab[:, i0:i0 + 4, 0], tab[:, i0:i0 + 4, 1]
                t = [v[:, 0:64].rearrange("p (i d) -> p i d", d=16) for v in tmp]
                tt(t[0], k4[:, :, 0:16], c, ALU.mult)
                tt(t[1], k4[:, :, 16:32], s_, ALU.mult)
                tt(t[2], k4[:, :, 16:32], c, ALU.mult)
                ln(tt(t[3], k4[:, :, 0:16], s_, ALU.mult))
                tt(k4[:, :, 0:16], t[0], t[1], ALU.subtract)
                ln(tt(k4[:, :, 16:32], t[2], t[3], ALU.add))
            nc.vector.memset(ub[:, 0:1], 0.0)
            ln(nc.vector.memset(ub[:, SEQ + 1:SEQ + 2], 0.0))
            for m in range(4):
                dve.wait_ge(un.empty, NRW + 6 * (m + 1))
                tt(ub[:, 1:SEQ + 1], gc[:, m % 2], hh, ALU.mult).then_inc(s_hh, 1)
                dve.wait_ge(s_hh, m + 1)
                if m >= 2:
                    dve.wait_ge(c_st[m % 2], 16 * (m // 2))
                c = co[:, m % 2]
                ln(ts(c, ub[:, 0:SEQ], convw(0, m), None, ALU.mult))
                ln(stt(c, ub[:, 1:SEQ + 1], convw(1, m), c, ALU.mult, ALU.add))
                ln(stt(c, ub[:, 2:SEQ + 2], convw(2, m), c, ALU.mult, ALU.add))
                tt(c, c, gb[:, m % 2], ALU.mult).then_inc(s_cv, 1)
            dve.wait_ge(s_cv, 4)


def block_oup(cr):
    nc, io = cr.nc, cr.io
    qT, kN, kr_d, v_d = (cr.dram(n, s_) for n, s_ in (
        ("oq_T", [HC * QKC, SEQ]), ("ok_T", [512, NTOK]), ("okr_T", [32, NTOK]), ("ov_rows", [NTOK, 512])))
    t_in, link, turned, placed, q_ok, tq, pq, kr_st = cr.sems("oup", "tables_loaded dve turned placed q_rows q_turned q_placed kr_stored")
    st_, qst_ = cr.sems("oup", "stored0 stored1"), cr.sems("oup", "q_stored0 q_stored1")
    raw, rawq = cr.at(O_RAW, NTC, 288), cr.at(O_RAWQ, NT, 384)
    ckvT, cqT = cr.at(16192, 2, NTOK), cr.at(18752, 3, SEQ)
    krT = cr.at(21824, NTOK)
    qrow = cr.at(23104, NT, 768)
    stage, qst = cr.at(29248, 2, 512), cr.at(30272, 2, 512)
    tab = cr.at(31296, NT, 2, 16)
    tmp = [cr.at(31552 + 128 * n, HC, 16) for n in range(4)]
    un = Units(cr, "oup")
    G3 = [(0, 4), (4, 8), (8, 10)]
    turns = [(lambda i, c=c: raw[:, i, c * P:(c + 1) * P], ckvT[:, c], a, b, 10 + c) for c in range(2) for a, b in G3]
    turns += [(lambda i: raw[:, i, 256:288], krT, a, b, None) for a, b in G3]
    turns += [(lambda i, c=c: rawq[:, i, c * P:(c + 1) * P], cqT[:, c], a, b, 12 + c) for c in range(3) for a, b in G3[:2]]
    TOK = [(0, 512), (512, 1024), (1024, NTOK)]
    NQ, NK = 2 * NT, 12

    with nc.Block() as block:
        @block.sync
        def _(sp):
            sp.dma_start(tab, io["rope_c"]).then_inc(t_in, 16)
            sp.wait_ge(placed, len(turns))
            sp.dma_start(kr_d[:, :], krT[0:32]).then_inc(kr_st, 16)
            sp.wait_ge(un.full, NQ)
            cr.load_w(sp, W_UQ + RING)
            for v in range(16):
                if v == 14:
                    sp.wait_ge(un.full, NQ + NK + NTC)
                    cr.load_w(sp, W_UKV + RING)
                h, g = v // 2, v % 2
                sp.wait_ge(pq, v + 1)
                sp.dma_start(qT[h * QKC:(h + 1) * QKC, g * 512:(g + 1) * 512], qst[0:QKC, v % 2]).then_inc(qst_[v % 2], 16)
            sp.wait_ge(kr_st, 16)
            for k in range(2):
                sp.wait_ge(qst_[k], 16 * 8)

        @block.gpsimd
        def _(pool):
            for n in range(NK + NTC):
                pool.wait_ge(un.empty, NQ + n + 1)
                if n < NK:
                    m, (a, b) = n // 3, TOK[n % 3]
                    pool.dma_start(kN[m * P:(m + 1) * P, a:b], stage[:, n % 2, 0:b - a]).then_inc(st_[n % 2], 16)
                else:
                    i = n - NK
                    pool.dma_start(v_d[i * P:(i + 1) * P, :], stage[:, n % 2]).then_inc(st_[n % 2], 16)
            for k in range(2):
                pool.wait_ge(st_[k], 16 * (NK + NTC) // 2)

        @block.tensor
        def _(pe):
            for v, (src, dst, a, b, g) in enumerate(turns):
                if v >= 2:
                    pe.wait_ge(placed, v - 1)
                m = 32 if g is None else P
                for i in range(a, b):
                    last = nc.tensor.transpose(cr.bank[v % 2][0:m, (i - a) * P:(i - a + 1) * P], src(i), cr.const(C_ID))
                last.then_inc(turned, 1)
            pe.wait_ge(placed, len(turns))
            cr.wait_w(pe, W_UQ)
            w = cr.ring[:, W_UQ % RING, 0:3 * 768].rearrange("p (k n) -> p k n", k=3)
            for i in range(NT):
                for c in range(2):
                    product(cr, pe, un, un.bank(un.n)[:, 0:384], [(cqT[:, k, i * P:(i + 1) * P], w[:, k, c * 384:(c + 1) * 384]) for k in range(3)])
            cr.wait_w(pe, W_UKV)
            w = cr.ring[:, W_UKV % RING, 0:2 * 1024].rearrange("p (k n) -> p k n", k=2)

            def turn_q():
                v = un.n - NQ - LAG - 1
                if v < 0:
                    return
                h, g = v // 2, v % 2
                if v == 0:
                    pe.wait_ge(q_ok, NT)
                if v >= 2:
                    pe.wait_ge(pq, v - 1)
                for q in range(4):
                    last = nc.tensor.transpose(cr.bank[6 + v % 2][0:QKC, q * P:(q + 1) * P], qrow[:, 4 * g + q, h * QKC:(h + 1) * QKC], cr.const(C_ID))
                last.then_inc(tq, 1)

            LAG = NK + NTC - 16
            for m in range(4):
                for a, b in TOK:
                    product(cr, pe, un, un.bank(un.n)[:, 0:b - a], [(w[:, k, m * P:(m + 1) * P], ckvT[:, k, a:b]) for k in range(2)])
                    turn_q()
            for i in range(NTC):
                product(cr, pe, un, un.bank(un.n), [(ckvT[:, k, i * P:(i + 1) * P], w[:, k, 512:1024]) for k in range(2)])
                turn_q()

        @block.scalar
        def _(act):
            for u in range(NQ):
                act.wait_ge(un.full, u + 1)
                nc.scalar.activation(qrow[:, u // 2, (u % 2) * 384:(u % 2 + 1) * 384], un.bank(u)[:, 0:384], ACT.Copy,
                                     scale=QKC ** -0.5).then_inc(un.empty, 1)
            for n in range(NK + NTC):
                act.wait_ge(un.full, NQ + n + 1)
                if n >= 2:
                    act.wait_ge(st_[n % 2], 16 * (n // 2))
                a, b = TOK[n % 3] if n < NK else (0, 512)
                nc.scalar.activation(stage[:, n % 2, 0:b - a], un.bank(NQ + n)[:, 0:b - a], ACT.Copy).then_inc(un.empty, 1)

        @block.vector
        def _(dve):
            ln = Link(dve, link)
            tt, ts = nc.vector.tensor_tensor, nc.vector.tensor_scalar
            for v, (src, dst, a, b, g) in enumerate(turns):
                dve.wait_ge(turned, v + 1)
                m = 32 if g is None else P
                ps = cr.bank[v % 2][0:m, 0:(b - a) * P]
                if g is None:
                    nc.vector.tensor_copy(dst[0:m, a * P:b * P], ps).then_inc(placed, 1)
                else:
                    ts(dst[:, a * P:b * P], ps, cr.cols[:, g:g + 1], None, ALU.mult).then_inc(placed, 1)
            dve.wait_ge(t_in, 16)
            for i in range(NT):
                dve.wait_ge(un.empty, 2 * i + 2)
                q = qrow[:, i].rearrange("p (h w) -> p h w", w=QKC)
                x1, x2 = q[:, :, 64:80], q[:, :, 80:96]
                c, s_ = (tab[:, i, n].unsqueeze(1).broadcast_to([P, HC, 16]) for n in range(2))
                tt(tmp[0], x1, c, ALU.mult)
                tt(tmp[1], x2, s_, ALU.mult)
                tt(tmp[2], x2, c, ALU.mult)
                ln(tt(tmp[3], x1, s_, ALU.mult))
                ln(tt(x1, tmp[0], tmp[1], ALU.subtract))
                tt(x2, tmp[2], tmp[3], ALU.add).then_inc(q_ok, 1)
                dve.wait_ge(q_ok, i + 1)
            for v in range(16):
                dve.wait_ge(tq, v + 1)
                if v >= 2:
                    dve.wait_ge(qst_[v % 2], 16 * (v // 2))
                nc.vector.tensor_copy(qst[0:QKC, v % 2], cr.bank[6 + v % 2][0:QKC, :]).then_inc(pq, 1)


def block_mla(cr):
    qT, kN, kr_d, v_d = (cr.dram(n, s_) for n, s_ in (
        ("oq_T", [HC * QKC, SEQ]), ("ok_T", [512, NTOK]), ("okr_T", [32, NTOK]), ("ov_rows", [NTOK, 512])))
    O = cr.dram("o_rows", [NTOK, D])
    qa, ka = cr.at(10240, 2, SEQ), cr.at(12288, 2, NTOK)
    vb = cr.at(14848, 2, NTC, 2 * HD)
    p_buf, t_buf = cr.at(17408, 2, NTOK), cr.at(19968, 2, NTC, P)
    ob = cr.at(22528, 2, NT, HD)

    def loads(k, it):
        h = 2 * it + k
        return [(qa[0:QKC, k], qT[bass.ds(h * QKC, QKC), :]), (ka[0:HD, k], kN[bass.ds(h * HD, HD), :]),
                (vb[:, k], rows_of(v_d, it * (2 * HD), 2 * HD, NTC))]

    steps = [Step(k, qa[:, k, i * P:(i + 1) * P],
                  [(a, min(a + 512, NTOK), ka[:, k, a:min(a + 512, NTOK)]) for a in range(0, NTOK, 512)], [], NTOK,
                  [(n * P, vb[:, k, n]) for n in range(NTC)], None, ob[:, k, i]) for k in range(2) for i in range(NT)]
    attention(cr, "mla", HC // 2, steps, loads, [(ka[HD:QKC, k], kr_d[:, :]) for k in range(2)],
              lambda k, it: (rows_of(O, (2 * it + k) * HD, HD, NT), ob[:, k]), 3, p_buf, t_buf, [qa[QKC:P], ka[QKC:P]])


def block_oout(cr):
    block_out(cr, "oout", W_OOUT, NT, 4, None, "c_T", [(MC_L + 64, V_LAT)])


def block_final(cr):
    nc, io = cr.nc, cr.io
    x_d = cr.dram("x_rows", [NTOK, D])
    g_in, ss, var, std, rst, done, st = cr.sems("final", "g_loaded squares variance std rstd done stored")
    x_in = cr.sems("final", "x_loaded0 x_loaded1 x_loaded2 x_loaded3")
    part = NT // 4
    quarter = lambda q: slice(part * q, part * (q + 1))
    Xr = X(cr)
    fg = cr.at(10240, D)
    junk = cr.at(11264, 2, D)
    s_ = cr.small[:, 300:332].rearrange("p (n i) -> p n i", n=4)
    out = cr.out.rearrange("b (i p) d -> (b p) i d", p=P)

    with nc.Block() as block:
        @block.sync
        def _(sp):
            for q in range(4):
                sp.dma_start(Xr[:, quarter(q)], x_d.rearrange("(i p) d -> p i d", p=P)[:, quarter(q)]).then_inc(x_in[q], 16)
            sp.dma_start(fg, io["final_g"].broadcast_to([P, D])).then_inc(g_in, 16)
            for i in range(NT):
                sp.wait_ge(done, i + 1)
                sp.dma_start(out[:, i], Xr[:, i]).then_inc(st, 16)
            sp.wait_ge(st, 16 * NT)

        @block.scalar
        def _(act):
            for q in range(4):
                act.wait_ge(x_in[q], 16)
                for i in range(part * q, part * (q + 1)):
                    if i >= 2:
                        act.wait_ge(ss, i - 1)
                    nc.scalar.activation(junk[:, i % 2], Xr[:, i], ACT.Square, accum_out=s_[:, 0, i:i + 1]).then_inc(ss, 1)
                act.wait_ge(var, q + 1)
                nc.scalar.activation(s_[:, 2, quarter(q)], s_[:, 1, quarter(q)], ACT.Sqrt).then_inc(std, 1)

        @block.vector
        def _(dve):
            dve.wait_ge(g_in, 16)
            for q in range(4):
                dve.wait_ge(ss, part * (q + 1))
                nc.vector.tensor_scalar(s_[:, 1, quarter(q)], s_[:, 0, quarter(q)], 1.0 / D, EPS, ALU.mult, ALU.add).then_inc(var, 1)
                dve.wait_ge(std, q + 1)
                nc.vector.reciprocal(s_[:, 3, quarter(q)], s_[:, 2, quarter(q)]).then_inc(rst, 1)
                dve.wait_ge(rst, q + 1)
                for i in range(part * q, part * (q + 1)):
                    nc.vector.scalar_tensor_tensor(Xr[:, i], Xr[:, i], s_[:, 3, i:i + 1], fg, ALU.mult, ALU.mult).then_inc(done, 1)


BLOCKS = [block_mods_and_tables, block_a_in, block_ssm, block_a_out, block_kv, block_bq, block_fox, block_bout,
          block_ein, block_window, block_eout, lambda cr: block_router(cr, 0), lambda cr: block_moe(cr, 0),
          block_oin, block_oup, block_mla, block_oout, lambda cr: block_router(cr, 1), lambda cr: block_moe(cr, 1), block_final]


def program(nc, io, out, debug=None):
    with ExitStack() as ctx:
        cr = Core(nc, ctx, io)
        cr.out = out
        for b in BLOCKS:
            b(cr)
            cr.end_block()
        if debug:
            debug(cr)


def _tiles(w, cols=512):
    K, N = w.shape
    out = []
    for c in range(0, N, cols):
        part = w[:, c:c + cols]
        if part.shape[1] < cols:
            part = np.concatenate([part, np.zeros((K, cols - part.shape[1]), np.float32)], 1)
        out.append(part.reshape(K // P, P, cols).transpose(1, 0, 2).reshape(P, -1))
    return out


def _cols(v):
    return np.ascontiguousarray(v.reshape(-1, P).T)


def lay_out(i):
    i = {k: np.asarray(v) for k, v in i.items()}
    t = []
    for m in (i["a_mod_w"][0], i["kv_mod_w"], i["b_mod_w"][0], i["mod_w_2"][0], i["mod_w_2"][1]):
        t += _tiles(m)
    t += _tiles(i["a_w_in"][0]) + _tiles(i["a_w_glu"][0]) + _tiles(i["a_w_out"][0])
    t += _tiles(i["kv_w"][:, :2 * D]) + _tiles(i["b_w_in"][0]) + _tiles(i["b_w_out"][0])
    e = i["ev_w_in_2"][0]
    t += _tiles(e[:, 0:256]) + _tiles(e[:, 256:1792]) + _tiles(i["ev_w_out_2"][0])

    def moe(l):
        for n in range(NE):
            w1, w3, w2 = (_tiles(i[f"exp_{w}_2"][l, n]) for w in ("w1", "w3", "w2"))
            t.extend([w1[0], w3[0], w1[1], w3[1], w2[0], w2[1]])
    moe(0)
    o = i["od_w_in_2"][0]
    t += _tiles(o[:, 0:288]) + _tiles(o[:, 288:672])
    g = [o[:, 672 + 512 * s:672 + 512 * (s + 1)] for s in range(3)]
    t += _tiles(np.concatenate([g[s][:, m * P:(m + 1) * P] for m in range(4) for s in range(3)], 1))
    pad = lambda v: np.concatenate([v, np.zeros((P, TILE - v.shape[1]), np.float32)], 1)
    uq = i["od_w_uq_2"][0]
    t.append(pad(uq.reshape(3, P, 768).transpose(1, 0, 2).reshape(P, -1)))
    kv = i["od_w_ukv_2"][0].reshape(256, HC, 2, HD).transpose(0, 2, 1, 3).reshape(2, P, 1024)
    t.append(pad(kv.transpose(1, 0, 2).reshape(P, -1)))
    t += _tiles(i["od_w_out_2"][0])
    moe(1)
    assert len(t) == N_TILES
    a = {"wstream": np.stack(t)}
    a["x"] = i["x"]
    a["ctx"] = i["ctx_2"]
    a["ccols"] = np.ascontiguousarray(np.stack([_cols(i["c"][0]), _cols(i["c_2"][0]), _cols(i["c_ctx_2"])], 2))
    a["modb"] = np.ascontiguousarray(np.concatenate(
        [_cols(v) for v in (i["a_mod_b"][0], i["kv_mod_b"], i["b_mod_b"][0], i["mod_b_2"][0], i["mod_b_2"][1])], 1))
    a["gains"] = np.ascontiguousarray(np.stack([_cols(v) for v in (
        i["a_norm_g"][0], i["kv_norm_g"], i["b_norm_g"][0], i["norm1_g_2"][0], i["norm1_g_2"][1],
        i["norm2_g_2"][0], i["norm2_g_2"][1])], 1))
    two = lambda v: np.concatenate([v, v]).reshape(P, 1)
    a["cols"] = np.ascontiguousarray(np.concatenate(
        [_cols(i["a_b_glu"][0]), two(i["k_norm_g"]), two(i["q_norm_g"][0]), _cols(i["od_kv_norm_g_2"][0]),
         _cols(i["od_q_norm_g_2"][0])] + [_cols(i["od_conv_w_2"][0, s]) for s in range(3)]
        + [np.zeros((P, 40 - 27), np.float32)], 1))
    pair = lambda v: np.ascontiguousarray(v.reshape(NPAIR, 2, STATE, -1).transpose(1, 2, 0, 3).reshape(P, NPAIR, -1))
    a["a_re"], a["a_im"] = (pair(i[k][0])[:, :, 0] for k in ("a_A_re", "a_A_im"))
    a["a_ldt"] = pair(np.repeat(i["a_log_dt"][0], STATE))[:, :, 0]
    a["b_re"], a["b_im"] = (pair(i[k][0]) for k in ("a_B_re", "a_B_im"))
    a["c_re"], a["c_im"] = (pair(i[k][0].transpose(0, 2, 1)) for k in ("a_C_re", "a_C_im"))
    a["d_cols"] = np.ascontiguousarray(i["a_D"][0].reshape(NPAIR, 2, GRP).transpose(1, 2, 0).reshape(2 * GRP, NPAIR))
    a["f_w"] = np.ascontiguousarray(i["kv_w"][:, 2 * D:].reshape(KT, P, HB).transpose(1, 0, 2))
    a["f_b"] = i["kv_f_bias"].reshape(1, HB)
    a["router"] = np.ascontiguousarray(i["router_w_2"].reshape(2, KT, P, NE).transpose(2, 0, 1, 3))
    a["sink"] = i["ev_sink_2"].reshape(1, HW_)
    a["sgu_w"] = np.ascontiguousarray(i["ev_sgu_w_2"][0].transpose(2, 0, 1))
    a["sgu_b"] = i["ev_sgu_b_2"].reshape(1, 4 * P)
    a["sgu_g"] = i["ev_sgu_norm_g_2"].reshape(1, 512)
    a["final_g"] = i["final_g_2"].reshape(1, D)
    a.update(shape_constants())
    return {k: np.ascontiguousarray(v) for k, v in a.items()}


def shape_constants():
    q, k = np.meshgrid(np.arange(P), np.arange(P), indexing="ij")
    consts = np.stack([np.eye(P), np.ones((P, P)), q <= k, np.where(k <= q, 0.0, NEG), np.where(k >= q, 0.0, NEG)], 1)
    a = {"consts": consts.astype(np.float32), "zeros": np.zeros((GRP, GROUPS, P), np.float32),
         "ones": np.ones((1, NTOK), np.float32)}
    for name, rot in (("rope_a", 64), ("rope_c", 32)):
        n = rot // 4
        inv = (np.float32(10000.0) ** (-np.arange(n, dtype=np.float32) / n)).astype(np.float32)
        pos = np.arange(SEQ)
        row, col = (pos // 64).astype(np.float32), (pos % 64).astype(np.float32)
        ang = np.concatenate([row[:, None] * inv, col[:, None] * inv], 1).astype(np.float32)
        t = np.stack([np.cos(ang), np.sin(ang)], 1).astype(np.float32)
        a[name] = np.ascontiguousarray(t.reshape(NT, P, 2, rot // 2).transpose(1, 0, 2, 3))
    return a


def kernel(**inputs):
    import concourse.bacc as bacc
    from concourse.bass_utils import run_bass_kernel_spmd

    nc = bacc.Bacc("TRN2", target_bir_lowering=False, num_devices=1)
    arrays = lay_out(inputs)
    io = {k: nc.dram_tensor(f"in_{k}", v.shape, F32, kind="ExternalInput").ap() for k, v in arrays.items()}
    out = nc.dram_tensor("out", (1, SEQ, D), F32, kind="ExternalOutput").ap()
    program(nc, io, out)
    r = run_bass_kernel_spmd(nc, [{f"in_{k}": v for k, v in arrays.items()}], core_ids=[0])
    return r.results[0]["out"]
```
